# Optimizing a Trainium2 kernel written in Bass

```python
import math
import jax, jax.numpy as jnp
from jax import lax
import numpy as np

D_MODEL = 1024
BATCH = 1
SEQ = 256
DEPTH = 1
DEC_BATCH = 1
DEC_SEQ = 512
PAST_LEN = 128

N_ATT_HEADS = 8
QK_NOPE = 64
QK_ROPE = 32
V_HEAD = 64
Q_LORA = 384
KV_LORA = 256
ATT_WIDTH = N_ATT_HEADS * V_HEAD
ROPE_BASE = 10000.0
Q_BLOCK = 128
LRU_WIDTH = 512
LRU_BLOCKS = 8
LRU_BLOCK = LRU_WIDTH // LRU_BLOCKS
CONV_W = 4
LRU_C = 8.0
IN_WIDTH = Q_LORA + KV_LORA + QK_ROPE + 2 * LRU_WIDTH
MIX_WIDTH = ATT_WIDTH + LRU_WIDTH
N_GROUPS = 4
EXPERTS_PER_GROUP = 8
N_EXPERTS = N_GROUPS * EXPERTS_PER_GROUP
TOP_K_IN_GROUP = 2
D_EXPERT = 256
EPS = 1e-6

kernel_name = "hymba_rglru_mla_hier_moe_encoder"

def rmsnorm(x, g):
    xf = x.astype(jnp.float32)
    out = xf * lax.rsqrt(jnp.mean(xf * xf, axis=-1, keepdims=True) + EPS)
    return (out * g.astype(jnp.float32)).astype(x.dtype)

def rope_tables(s):
    pos = jnp.arange(s, dtype=jnp.float32)
    inv_freq = 1.0 / (ROPE_BASE ** (jnp.arange(0, QK_ROPE, 2, dtype=jnp.float32) / QK_ROPE))
    freqs = pos[:, None] * inv_freq[None, :]
    return jnp.cos(freqs), jnp.sin(freqs)

def apply_rope(x, cos, sin):
    x1, x2 = jnp.split(x.astype(jnp.float32), 2, axis=-1)
    out = jnp.concatenate([x1 * cos - x2 * sin, x2 * cos + x1 * sin], axis=-1)
    return out.astype(x.dtype)

def mla(q_lat, kv_lat, k_rope, q_norm, w_q_up, kv_norm, w_kv_up):
    b, s, _ = q_lat.shape
    nb = s // Q_BLOCK
    q = (rmsnorm(q_lat, q_norm) @ w_q_up).reshape(b, s, N_ATT_HEADS, QK_NOPE + QK_ROPE)
    kv = (rmsnorm(kv_lat, kv_norm) @ w_kv_up).reshape(b, s, N_ATT_HEADS, QK_NOPE + V_HEAD)
    q_nope, q_pe = q[..., :QK_NOPE], q[..., QK_NOPE:]
    k_nope, v = kv[..., :QK_NOPE], kv[..., QK_NOPE:]
    cos, sin = rope_tables(s)
    q_pe = apply_rope(q_pe, cos[None, :, None, :], sin[None, :, None, :])
    k_pe = apply_rope(k_rope, cos[None], sin[None])
    scale = (QK_NOPE + QK_ROPE) ** -0.5
    qn_blocks = q_nope.reshape(b, nb, Q_BLOCK, N_ATT_HEADS, QK_NOPE).transpose(1, 0, 2, 3, 4)
    qp_blocks = q_pe.reshape(b, nb, Q_BLOCK, N_ATT_HEADS, QK_ROPE).transpose(1, 0, 2, 3, 4)

    def block(args):
        qn, qp = args
        scores = (jnp.einsum('bqhd,bkhd->bhqk', qn, k_nope).astype(jnp.float32)
                  + jnp.einsum('bqhr,bkr->bhqk', qp, k_pe).astype(jnp.float32)) * scale
        p = jax.nn.softmax(scores, axis=-1).astype(v.dtype)
        return jnp.einsum('bhqk,bkhd->bqhd', p, v)

    out = lax.map(block, (qn_blocks, qp_blocks))
    return out.transpose(1, 0, 2, 3, 4).reshape(b, s, ATT_WIDTH)

def centred_depthwise_conv(x, w, bias):
    pad_l = (CONV_W - 1) // 2
    pad_r = CONV_W - 1 - pad_l
    rhs = w.astype(x.dtype)[:, None, :]
    out = lax.conv_general_dilated(x, rhs, window_strides=(1,), padding=[(pad_l, pad_r)],
                                   dimension_numbers=('NWC', 'WIO', 'NWC'),
                                   feature_group_count=x.shape[-1])
    return out + bias.astype(x.dtype)

def _lin_combine(e1, e2):
    a1, b1 = e1
    a2, b2 = e2
    return a1 * a2, a2 * b1 + b2

def rglru_direction(x, w_r, b_r, w_i, b_i, lam, reverse):
    b, s, _ = x.shape
    xb = x.reshape(b, s, LRU_BLOCKS, LRU_BLOCK)
    r = jax.nn.sigmoid(jnp.einsum('bsnc,ncd->bsnd', xb, w_r.astype(jnp.float32)).reshape(b, s, LRU_WIDTH)
                       + b_r.astype(jnp.float32))
    i = jax.nn.sigmoid(jnp.einsum('bsnc,ncd->bsnd', xb, w_i.astype(jnp.float32)).reshape(b, s, LRU_WIDTH)
                       + b_i.astype(jnp.float32))
    log_a = -LRU_C * r * jax.nn.softplus(-lam.astype(jnp.float32))
    a = jnp.exp(log_a)
    u = jnp.sqrt(-jnp.expm1(2.0 * log_a)) * (i * x)
    _, h = lax.associative_scan(_lin_combine, (a, u), reverse=reverse, axis=1)
    return h

def rglru_mixer(x_br, g_br, conv_w, conv_b, w_rg, b_rg, w_ig, b_ig, lru_lambda):
    xc = centred_depthwise_conv(x_br, conv_w, conv_b).astype(jnp.float32)
    h = (rglru_direction(xc, w_rg[0], b_rg[0], w_ig[0], b_ig[0], lru_lambda[0], False)
         + rglru_direction(xc, w_rg[1], b_rg[1], w_ig[1], b_ig[1], lru_lambda[1], True))
    return (h * jax.nn.gelu(g_br.astype(jnp.float32))).astype(x_br.dtype)

def hier_moe(x, w_group, b_group, w_router, b_router, w_gate, w_up, w_down):
    b, s, d = x.shape
    t = x.reshape(-1, d)
    n_tok = t.shape[0]
    g_logits = (t @ w_group + b_group).astype(jnp.float32)
    g_prob = jax.nn.softmax(g_logits, axis=-1)
    g_sel = jnp.argmax(g_logits, axis=-1)
    g_weight = jnp.take_along_axis(g_prob, g_sel[:, None], axis=-1)
    e_logits = (t @ w_router + b_router).astype(jnp.float32).reshape(n_tok, N_GROUPS, EXPERTS_PER_GROUP)
    e_in = jnp.take_along_axis(e_logits, g_sel[:, None, None], axis=1)[:, 0]
    top_v, top_i = lax.top_k(e_in, TOP_K_IN_GROUP)
    top_w = jax.nn.softmax(top_v, axis=-1) * g_weight
    expert_idx = g_sel[:, None] * EXPERTS_PER_GROUP + top_i
    gates = jnp.sum(jax.nn.one_hot(expert_idx, N_EXPERTS, dtype=jnp.float32) * top_w[..., None], axis=1)
    out = jnp.zeros((n_tok, d), jnp.float32)
    for e in range(N_EXPERTS):
        h = jax.nn.silu(t @ w_gate[e]) * (t @ w_up[e])
        out = out + gates[:, e:e + 1] * (h @ w_down[e]).astype(jnp.float32)
    return out.astype(x.dtype).reshape(b, s, d)

def encoder_layer(x, norm1, w_in, q_norm, w_q_up, kv_norm, w_kv_up, conv_w, conv_b,
                  w_rg, b_rg, w_ig, b_ig, lru_lambda, att_out_norm, lru_out_norm, w_out,
                  norm2, w_group, b_group, w_router, b_router, w_gate, w_up, w_down):
    u = rmsnorm(x, norm1)
    z = u @ w_in
    c1 = Q_LORA
    c2 = c1 + KV_LORA
    c3 = c2 + QK_ROPE
    c4 = c3 + LRU_WIDTH
    q_lat, kv_lat, k_rope, x_br, g_br = jnp.split(z, [c1, c2, c3, c4], axis=-1)
    att = mla(q_lat, kv_lat, k_rope, q_norm, w_q_up, kv_norm, w_kv_up)
    lru = rglru_mixer(x_br, g_br, conv_w, conv_b, w_rg, b_rg, w_ig, b_ig, lru_lambda)
    mixed = jnp.concatenate([rmsnorm(att, att_out_norm), rmsnorm(lru, lru_out_norm)], axis=-1)
    x = x + mixed @ w_out
    x = x + hier_moe(rmsnorm(x, norm2), w_group, b_group, w_router, b_router, w_gate, w_up, w_down)
    return x

def trunk(x, norm1, w_in, q_norm, w_q_up, kv_norm, w_kv_up, conv_w, conv_b,
          w_rg, b_rg, w_ig, b_ig, lru_lambda, att_out_norm, lru_out_norm, w_out,
          norm2, w_group, b_group, w_router, b_router, w_gate, w_up, w_down, final_norm):
    for l in range(DEPTH):
        x = encoder_layer(x, norm1[l], w_in[l], q_norm[l], w_q_up[l], kv_norm[l], w_kv_up[l],
                          conv_w[l], conv_b[l], w_rg[l], b_rg[l], w_ig[l], b_ig[l], lru_lambda[l],
                          att_out_norm[l], lru_out_norm[l], w_out[l], norm2[l], w_group[l], b_group[l],
                          w_router[l], b_router[l], w_gate[l], w_up[l], w_down[l])
    return rmsnorm(x, final_norm)

def setup_inputs(seed: int = 0) -> dict:
    key = jax.random.key(seed)
    ks = jax.random.split(key, 32)
    f32 = jnp.float32

    def nrm(k, shape, scale):
        return jax.random.normal(k, shape, f32) * scale

    def gain(k, shape):
        return 1.0 + 0.01 * jax.random.normal(k, shape, f32)

    ac = jax.random.uniform(ks[14], (DEPTH, 2, LRU_WIDTH), f32, 0.9, 0.999)
    a = ac ** (1.0 / LRU_C)
    lru_lambda = jnp.log(a) - jnp.log1p(-a)
    return {
        "x_prompt": jax.random.normal(ks[0], (BATCH, SEQ, D_MODEL), f32),
        "x_sample": jax.random.normal(ks[1], (DEC_BATCH, DEC_SEQ, D_MODEL), f32),
        "norm1": gain(ks[2], (DEPTH, D_MODEL)),
        "w_in": nrm(ks[3], (DEPTH, D_MODEL, IN_WIDTH), D_MODEL ** -0.5),
        "q_norm": gain(ks[4], (DEPTH, Q_LORA)),
        "w_q_up": nrm(ks[5], (DEPTH, Q_LORA, N_ATT_HEADS * (QK_NOPE + QK_ROPE)), Q_LORA ** -0.5),
        "kv_norm": gain(ks[6], (DEPTH, KV_LORA)),
        "w_kv_up": nrm(ks[7], (DEPTH, KV_LORA, N_ATT_HEADS * (QK_NOPE + V_HEAD)), KV_LORA ** -0.5),
        "conv_w": nrm(ks[8], (DEPTH, CONV_W, LRU_WIDTH), CONV_W ** -0.5),
        "conv_b": nrm(ks[9], (DEPTH, LRU_WIDTH), 0.01),
        "w_rg": nrm(ks[10], (DEPTH, 2, LRU_BLOCKS, LRU_BLOCK, LRU_BLOCK), LRU_BLOCK ** -0.5),
        "b_rg": nrm(ks[11], (DEPTH, 2, LRU_WIDTH), 0.01),
        "w_ig": nrm(ks[12], (DEPTH, 2, LRU_BLOCKS, LRU_BLOCK, LRU_BLOCK), LRU_BLOCK ** -0.5),
        "b_ig": nrm(ks[13], (DEPTH, 2, LRU_WIDTH), 0.01),
        "lru_lambda": lru_lambda,
        "att_out_norm": gain(ks[15], (DEPTH, ATT_WIDTH)),
        "lru_out_norm": gain(ks[16], (DEPTH, LRU_WIDTH)),
        "w_out": nrm(ks[17], (DEPTH, MIX_WIDTH, D_MODEL), MIX_WIDTH ** -0.5),
        "norm2": gain(ks[18], (DEPTH, D_MODEL)),
        "w_group": nrm(ks[19], (DEPTH, D_MODEL, N_GROUPS), D_MODEL ** -0.5),
        "b_group": nrm(ks[20], (DEPTH, N_GROUPS), 0.01),
        "w_router": nrm(ks[21], (DEPTH, D_MODEL, N_EXPERTS), D_MODEL ** -0.5),
        "b_router": nrm(ks[22], (DEPTH, N_EXPERTS), 0.01),
        "w_gate": nrm(ks[23], (DEPTH, N_EXPERTS, D_MODEL, D_EXPERT), D_MODEL ** -0.5),
        "w_up": nrm(ks[24], (DEPTH, N_EXPERTS, D_MODEL, D_EXPERT), D_MODEL ** -0.5),
        "w_down": nrm(ks[25], (DEPTH, N_EXPERTS, D_EXPERT, D_MODEL), D_EXPERT ** -0.5),
        "final_norm": gain(ks[26], (D_MODEL,)),
    }

def reference(x_prompt, x_sample, norm1, w_in, q_norm, w_q_up, kv_norm, w_kv_up, conv_w, conv_b,
              w_rg, b_rg, w_ig, b_ig, lru_lambda, att_out_norm, lru_out_norm, w_out,
              norm2, w_group, b_group, w_router, b_router, w_gate, w_up, w_down, final_norm):
    y_prompt = trunk(x_prompt, norm1, w_in, q_norm, w_q_up, kv_norm, w_kv_up, conv_w, conv_b,
                     w_rg, b_rg, w_ig, b_ig, lru_lambda, att_out_norm, lru_out_norm, w_out,
                     norm2, w_group, b_group, w_router, b_router, w_gate, w_up, w_down, final_norm)
    y_sample = trunk(x_sample, norm1, w_in, q_norm, w_q_up, kv_norm, w_kv_up, conv_w, conv_b,
                     w_rg, b_rg, w_ig, b_ig, lru_lambda, att_out_norm, lru_out_norm, w_out,
                     norm2, w_group, b_group, w_router, b_router, w_gate, w_up, w_down, final_norm)
    return (y_prompt, y_sample)


_drawn_inputs = setup_inputs


def setup_inputs(seed=0):
    import zlib

    import numpy as np

    out = dict(_drawn_inputs(seed))
    spreads = {}
    factors = {'q_norm': 4.332,
     'kv_norm': 3.418,
     'b_rg': 8.0,
     'b_ig': 8.0,
     'att_out_norm': 4.249,
     'lru_out_norm': 4.474,
     'norm2': 2.756,
     'b_group': 6.15,
     'b_router': 3.859,
     'final_norm': 5.582}
    for name, (base, spread) in spreads.items():
        noise = np.random.default_rng([zlib.crc32(name.encode()), seed]).standard_normal(out[name].shape)
        drawn = base * np.exp(spread * noise) if base else spread * noise
        out[name] = __import__('jax').numpy.asarray(drawn.astype(out[name].dtype))
    for name, factor in factors.items():
        out[name] = (out[name] * factor).astype(out[name].dtype)
    return out
```

```python
import concourse.bass as bass
from concourse import mybir
from contextlib import ExitStack

P = 128
TOK, PROMPT = 768, 256
NT = TOK // P
D = 1024
DC = D // P
QL, KVL, RP, LRU = 384, 256, 32, 512
NH, NOPE, VH = 8, 64, 64
LC = LRU // P
QC, KVC = QL // P, KVL // P
CHUNKS = ((0, PROMPT), (PROMPT, TOK - PROMPT))
XPAD = (PROMPT + 3) + (TOK - PROMPT + 3)
XOFF = (0, PROMPT + 3)
NE, NG, EG, F = 32, 4, 8, 256
FC = F // P
WB = 80
RING = 4
MAXQ = (TOK - 1) // WB
MAXB = NE + (2 * TOK) // WB
ITERS_MAX = -(-MAXB // RING)
NBC = RING * ITERS_MAX + 1
EXTRA = NBC - NE
EPS = 1e-6
SCALE = float(NOPE + RP) ** -0.5
BIG = 1e30

COLS = {}
_at = 0
for _n, _w in (("norm1", DC), ("q_norm", QC), ("kv_norm", KVC), ("conv_w", 4 * LC), ("conv_b", LC),
               ("b_rg", 2 * LC), ("b_ig", 2 * LC), ("lam", 2 * LC), ("att_norm", LC), ("lru_norm", LC)):
    COLS[_n] = _at
    _at += _w
NCOLS = _at
CONSTS = {}
_at = 0
for _n, _w in (("ident", P), ("before", P), ("ones", P), ("iota_w", WB), ("iota_b", NBC), ("iota_e", NE),
               ("thr", MAXQ), ("tokid", NT), ("eps", 1), ("iota_x", EXTRA), ("iter_thr", ITERS_MAX)):
    CONSTS[_n] = _at
    _at += _w
NCONSTS = _at


def encoder_layer(nc, A_x, A_cols, A_consts, A_rope, A_rows, A_win, A_wq, A_wkv, A_wrg, A_wig, A_wout,
                  A_wrt, A_wgate, A_wup, A_wdown, y_prompt, y_sample):
    f32, i32 = mybir.dt.float32, mybir.dt.int32
    ALU = mybir.AluOpType
    ACT = mybir.ActivationFunctionType
    AX = mybir.AxisListType
    ctx = ExitStack()
    with ctx:
        def sb(name, shape, dt=f32):
            return ctx.enter_context(nc.sbuf_tensor(name, shape, dt))

        def sem(name):
            return ctx.enter_context(nc.semaphore(name))

        SLOT = 3 * DC * F
        ring = sb("ring", [P, RING * SLOT])
        lowrank = sb("lowrank", [P, (QC + KVC) * TOK])
        upw = sb("upw", [P, QC * TOK + KVC * D])
        xb = sb("xb", [P, LC, XPAD])
        gg = sb("gg", [P, LC, TOK])
        softm = sb("softm", [P, 2048])
        rope = sb("rope", [P, 2, TOK])
        consts = sb("consts", [P, NCONSTS])
        cols = sb("cols", [P, NCOLS])
        n2row = sb("n2row", [P, D])
        tmp = sb("tmp", [P, 6144])
        gatew = sb("gatew", [P, 2, 2, LC, P])
        wrt = sb("wrt", [P, DC, NG + NE])
        brt = sb("brt", [P, NG + NE])
        small = sb("small", [P, 160])
        idx = sb("idx", [WB, NBC], i32)
        idx_now = sb("idx_now", [WB, RING], i32)
        pos_i = sb("pos_i", [P, 2 * NT], i32)
        ctl = sb("ctl", [1, NBC + 3], i32)
        psum = [ctx.enter_context(nc.psum_tensor(f"bank{b}", [P, 512], f32)) for b in range(8)]
        x2_d = nc.dram_tensor("x2_rows", [TOK, D], f32, kind="Internal").ap()
        xn_d = nc.dram_tensor("xn_rows", [TOK, D], f32, kind="Internal").ap()
        ys_d = nc.dram_tensor("expert_rows", [NBC * WB, D], f32, kind="Internal").ap()

        def C(name, n=None, p0=0, p1=P):
            a = CONSTS[name]
            return consts[p0:p1, a:a + (n or 1)]

        ident, before, ones = C("ident", P), C("before", P), C("ones", P)

        def col(name, j, p0=0, p1=P):
            a = COLS[name] + j
            return cols[p0:p1, a:a + 1]

        logits = rope[:, 0, 0:NT * (NG + NE)].rearrange("p (i n) -> p i n", i=NT)
        uT = ring[:, 0:DC * TOK].rearrange("p (c t) -> p c t", c=DC)
        qT = ring[:, 0:NH * TOK].rearrange("p (h t) -> p h t", h=NH)
        win = ring[:, SLOT:SLOT + DC * 1696]
        W_XB, W_GB, W_QK = 0, DC * LRU, 2 * DC * LRU
        NQK = QL + KVL + RP
        win_x = win[:, W_XB:W_XB + DC * LRU].rearrange("p (c n) -> p c n", c=DC)
        win_g = win[:, W_GB:W_GB + DC * LRU].rearrange("p (c n) -> p c n", c=DC)
        win_q = win[:, W_QK:W_QK + DC * NQK].rearrange("p (c n) -> p c n", c=DC)
        kT = ring[:, SLOT:SLOT + NH * TOK].rearrange("p (h t) -> p h t", h=NH)
        wout = ring[:, 2 * SLOT:2 * SLOT + DC * D].rearrange("p (c n) -> p c n", c=DC)
        V = ring[:, 3 * SLOT + 3072:4 * SLOT].rearrange("p (i n) -> p i n", i=NT)
        zl = lowrank[:, :].rearrange("p (c t) -> p c t", c=QC + KVC)
        att = lowrank[:, 0:NT * 512].rearrange("p (i n) -> p i n", i=NT)
        wq = upw[:, 0:QC * TOK].rearrange("p (c n) -> p c n", c=QC)
        wkv = upw[:, QC * TOK:].rearrange("p (c n) -> p c n", c=KVC)
        attT = upw[:, 0:LC * TOK].rearrange("p (c t) -> p c t", c=LC)
        r_bc = softm[:, 0:TOK]
        prob = softm[:, 0:1024].rearrange("p (b n) -> p b n", b=2)
        probT = softm[:, 1024:2048].rearrange("p (b n) -> p b n", b=2)
        xin = tmp[:, 0:2 * D].rearrange("p (b n) -> p b n", b=2)
        un = tmp[:, 2 * D:4 * D].rearrange("p (b n) -> p b n", b=2)
        junk = tmp[:, 4 * D:5 * D]
        kr = tmp[:, 5 * D:5 * D + TOK]
        xc = tmp[:, 0:1544].rearrange("p (b n) -> p b n", b=2)
        thr, thi, dec, th, dec2 = (tmp[:, 1544 + k * TOK:1544 + (k + 1) * TOK] for k in range(5))
        tb = 5384
        rstd1 = small[:, 0:NT]
        ssq = small[:, 8:8 + NT]
        lamc = small[:, 16:24]
        nlamc = small[:, 24:32]
        lam_t = small[:, 32:80].rearrange("p (k n) -> p k n", k=6)
        hb_r = small[:, 80:88]
        hb_i = small[:, 88:96]
        mx = small[:, 96:98]
        nm = small[:, 98:100]
        rs = small[:, 100:102]
        rr = small[:, 102:104]
        ssq2 = small[:, 104:104 + NT]
        rstd2 = small[:, 112:112 + NT]
        gate0 = small[:, 120:120 + NT]
        gate1 = small[:, 128:128 + NT]
        ssq3 = small[:, 136:136 + NT]
        rstd3 = small[:, 144:144 + NT]

        sqz = tmp[:, 0:(QC + KVC) * TOK].rearrange("p (c t) -> p c t", c=QC + KVC)
        xn = tmp[:, 2 * D:4 * D].rearrange("p (b n) -> p b n", b=2)
        x2t = tmp[:, 0:2 * D].rearrange("p (b n) -> p b n", b=2)
        tT = tmp[:, 4 * D:5 * D].rearrange("p (c t) -> p c t", c=DC)
        flat = lowrank
        E0 = flat[:, 0:192].rearrange("p (i e) -> p i e", i=NT)
        E1 = flat[:, 192:384].rearrange("p (i e) -> p i e", i=NT)
        mask = flat[:, 384:576].rearrange("p (i e) -> p i e", i=NT)
        em = flat[:, 576:768].rearrange("p (i e) -> p i e", i=NT)
        t1 = flat[:, 768:960].rearrange("p (i e) -> p i e", i=NT)
        rank = flat[:, 960:1152].rearrange("p (i e) -> p i e", i=NT)
        g4 = flat[:, 1152:1152 + 24].rearrange("p (i n) -> p i n", i=NT)
        g4b = flat[:, 1176:1176 + 24].rearrange("p (i n) -> p i n", i=NT)
        v6 = [flat[:, 1200 + 8 * k:1200 + 8 * k + NT] for k in range(16)]
        v12 = [flat[:, 1328 + 16 * k:1328 + 16 * k + 2 * NT] for k in range(8)]
        cnt = flat[:, 1456:1456 + NE]
        ovf = flat[:, 1488:1488 + NE]
        off = flat[:, 1520:1520 + NE]
        off_end = flat[:, 1552:1552 + NE]
        q9 = upw[:, 0:2 * NT * MAXQ].rearrange("p (k m) -> p k m", m=MAXQ)
        q9e = upw[:, 256:256 + NE * MAXQ].rearrange("p (e m) -> p e m", m=MAXQ)
        xe = upw[:, 640:640 + EXTRA * NE].rearrange("p (x e) -> p x e", e=NE)
        xe2 = upw[:, 1408:1408 + EXTRA * NE].rearrange("p (x e) -> p x e", e=NE)
        itt = upw[:, 2200:2200 + ITERS_MAX]
        ctlf = upw[:, 2220:2220 + NBC + 1]
        oh_w = upw[:, 2304:2304 + 2 * NT * WB].rearrange("p (k w) -> p k w", k=2 * NT)
        oh_b = upw[:, 3300:3300 + 2 * NT * NBC].rearrange("p (k w) -> p k w", k=2 * NT)
        rn = softm[:, 0:2 * TOK].rearrange("p (a t) -> p a t", a=2)
        zeros = softm[:, 0:D]
        rnorm2 = softm[:, 0:TOK]
        sqj = softm[:, 0:D]
        qr = tmp[:, 1544:1544 + 2 * TOK].rearrange("p (r t) -> p r t", r=2)
        qs = tmp[:, 1544 + 2 * TOK:1544 + 4 * TOK].rearrange("p (r t) -> p r t", r=2)
        krs = tmp[0:RP, 3840:3840 + TOK]
        lam2 = small[:, 152:160]
        fin_x = ring[:, 0:NT * D].rearrange("p (i n) -> p i n", i=NT)
        fin_y = ring[:, SLOT:SLOT + 2 * NT * D].rearrange("p (k i n) -> p k i n", k=2, i=NT)
        fin_row = ring[:, 3 * SLOT:3 * SLOT + D]
        fin_junk = ring[:, 3 * SLOT + D:3 * SLOT + 2 * D]
        xg = tmp[:, 0:2 * D].rearrange("p (b n) -> p b n", b=2)
        ysb = tmp[:, 2 * D:4 * D].rearrange("p (b n) -> p b n", b=2)
        xT = tmp[:, 4 * D:4 * D + 2 * DC * WB].rearrange("p (b c n) -> p b c n", b=2, c=DC)
        act_t = xb[:, 0, 0:FC * WB].rearrange("p (f n) -> p f n", f=FC)
        act_s = xb[:, 1, 0:FC * WB].rearrange("p (f n) -> p f n", f=FC)
        hT = xb[:, 2, 0:FC * WB].rearrange("p (f n) -> p f n", f=FC)

        S = {}
        for n in ("consts", "cols", "rope", "rows", "x0", "x1", "winx", "wing", "winq", "wq", "wkv", "gw", "wout", "wrt",
                  "gatew0", "pads", "gather_go", "zero", "ys_init",
                  "sqd", "sd", "rs1", "un", "uTp", "uT", "zp", "ze", "conv", "lamA", "lam",
                  "sqz", "statp", "rqs", "rq", "zn", "up", "upe", "ropeq", "ropek", "kpe", "vp", "vpe",
                  "sc", "mxd", "pr", "pT", "pTe", "pv", "pve",
                  "gp", "ga", "gm", "gs", "gh",
                  "lsq", "lst", "lrs", "ln", "asq", "asd", "an", "atp", "atT",
                  "xr0", "xr1", "op", "x2", "x2s", "x2q", "x2n", "x2st0", "x2st1", "xnst0", "xnst1", "ttp", "tt", "lgp", "lg",
                  "rt_e", "rt_d", "rt_m", "rt_p", "rt_a", "rt_ap", "ctl", "idx",
                  "ic", "xg0", "xg1", "xgp", "xT", "gu", "tnh", "hh", "dn", "ye", "ys0", "ys1", "wd0s",
                  "fx0", "fx1", "fs", "fq", "fo", "fr", "fst0", "fst1", "frow",
                  "dch", "ach", "pch", "gp2", "gx", "acs"):
            S[n] = sem("s_" + n)
        s_wg = [sem(f"s_wgu{s}") for s in range(RING)]
        s_fy = [sem(f"s_fy{k}") for k in range(2 * NT)]
        s_wd = [sem(f"s_wd{s}") for s in range(RING)]

        def g(name):
            return S[name]

        tiles = [("x", c) for c in range(LC)] + [("g", c) for c in range(LC)] + \
                [("z", c) for c in range(QC + KVC)] + [("k", 0)]
        units = [(kind, c, n) for kind, c in tiles for n in range(2)]
        ZB = 4
        steps = [(h, i) for h in range(NH) for i in range(NT)]

        def keys(i):
            return CHUNKS[0] if i * P < PROMPT else CHUNKS[1]

        ups = [("qr", r, n) for r in range(2) for n in range(2)] + \
              [("qn", m, n) for m in range(4) for n in range(2)] + \
              [("kn", m, n) for m in range(4) for n in range(2)] + \
              [("v", i, 0) for i in range(NT)]

        block = ctx.enter_context(nc.Block())

        @block.sync
        def _(sp):
            sp.dma_start(consts[:], A_consts).then_inc(g("consts"), 16)
            sp.dma_start(cols[:], A_cols).then_inc(g("cols"), 16)
            xv = A_x.rearrange("(i p) d -> i p d", p=P)

            def load_x(i):
                if i >= 2:
                    sp.wait_ge(g("un"), i - 1)
                sp.dma_start(xin[:, i % 2, :], xv[i]).then_inc(g(f"x{i % 2}"), 16)
            load_x(0)
            load_x(1)
            wv = A_win.rearrange("(p c) n -> p c n", c=DC)
            o = NQK
            sp.dma_start(win_x, wv[:, :, o:o + LRU]).then_inc(g("winx"), 16)
            for i in range(2, NT):
                load_x(i)
            sp.dma_start(win_g, wv[:, :, o + LRU:o + 2 * LRU]).then_inc(g("wing"), 16)
            sp.dma_start(win_q, wv[:, :, 0:NQK]).then_inc(g("winq"), 16)
            sp.wait_ge(g("zero"), 1)
            zr = EXTRA * WB // 120
            sp.dma_start(ys_d[NE * WB:, :].rearrange("(p r) d -> p r d", r=zr),
                         zeros[0:120, :].unsqueeze(1).to_broadcast([120, zr, D])).then_inc(g("ys_init"), 16)
            sp.wait_ge(g("gatew0"), 1)
            for t, src in enumerate((A_wrg, A_wig)):
                for half in range(2):
                    for d in range(2):
                        sp.dma_start(gatew[64 * half:64 * half + 64, t, d, :, 64 * half:64 * half + 64],
                                     src[d].rearrange("(c two) i o -> two i c o", two=2)[half]).then_inc(g("gw"), 16)
            sp.dma_start(wq, A_wq.rearrange("(c p) n -> p c n", p=P)).then_inc(g("wq"), 16)
            sp.dma_start(wkv, A_wkv.rearrange("(c p) n -> p c n", p=P)).then_inc(g("wkv"), 16)
            sp.dma_start(rope[:], A_rope.rearrange("p (a t) -> p a t", a=2)).then_inc(g("rope"), 16)
            sp.dma_start(n2row[:], A_rows[0:1, 0:D].to_broadcast([P, D])).then_inc(g("rows"), 16)
            sp.dma_start(brt[:], A_rows[2:3, 0:NG + NE].to_broadcast([P, NG + NE])).then_inc(g("rows"), 16)
            sp.dma_start(wrt[:], A_wrt.rearrange("(p c) n -> p c n", c=DC)).then_inc(g("wrt"), 16)
            sp.wait_ge(g("zp"), len(units))
            sp.dma_start(wout, A_wout.rearrange("(c p) n -> p c n", p=P)).then_inc(g("wout"), 16)

            def load_res(i):
                if i >= 2:
                    sp.wait_ge(g(f"x2st{i % 2}"), 16 * (i // 2))
                    sp.wait_ge(g("x2n"), i - 1)
                sp.dma_start(tmp[:, (i % 2) * D:(i % 2 + 1) * D], xv[i]).then_inc(g(f"xr{i % 2}"), 16)
            sp.wait_ge(g("gh"), 8)
            for i in range(NT):
                load_res(i)

            wg_v = A_wgate.rearrange("e (p c) n -> e p (c n)", c=DC)
            wu_v = A_wup.rearrange("e (p c) n -> e p (c n)", c=DC)
            wd_v = A_wdown.rearrange("e (k p) n -> e p k n", p=P)

            def load_expert(s, e, gu=True, dn=True):
                base = s * SLOT
                if gu:
                    sp.dma_start(ring[:, base:base + DC * F], wg_v[e]).then_inc(s_wg[s], 16)
                    sp.dma_start(ring[:, base + DC * F:base + 2 * DC * F], wu_v[e]).then_inc(s_wg[s], 16)
                if dn:
                    sp.dma_start(ring[:, base + 2 * DC * F:base + 3 * DC * F]
                                 .rearrange("p (k n) -> p k n", k=FC), wd_v[e]).then_inc(s_wd[s], 16)
            sp.wait_ge(g("sc"), len(steps))
            load_expert(0, 0)
            load_expert(1, 1)
            sp.wait_ge(g("op"), 2 * NT)
            load_expert(2, 2)
            load_expert(3, 3)
            sp.wait_ge(g("ctl"), 1)
            iters = sp.value_load(ctl[0:1, NBC:NBC + 1], min_val=NE // RING, max_val=ITERS_MAX)
            with sp.Fori(1, iters) as i:
                for s in range(RING):
                    b = i * RING + s
                    e = sp.value_load(ctl[0:1, bass.ds(b, 1)], min_val=0, max_val=NE - 1)
                    sp.wait_ge(g("gu"), b - RING + 1)
                    sp.dma_start(ring[:, s * SLOT:s * SLOT + DC * F], wg_v[bass.ds(e, 1)].rearrange("e p n -> (e p) n")).then_inc(s_wg[s], 16)
                    sp.dma_start(ring[:, s * SLOT + DC * F:s * SLOT + 2 * DC * F], wu_v[bass.ds(e, 1)].rearrange("e p n -> (e p) n")).then_inc(s_wg[s], 16)
                    sp.wait_ge(g("dn"), b - RING + 2)
                    sp.dma_start(ring[:, s * SLOT + 2 * DC * F:(s + 1) * SLOT].rearrange("p (k n) -> p k n", k=FC),
                                 wd_v[bass.ds(e, 1)].rearrange("e p k n -> (e p) k n")).then_inc(s_wd[s], 16)
            sp.wait_ge(g("dn"), iters * RING + 1)
            sp.wait_ge(g("ctl"), 1)
            sp.dma_start(fin_row, A_rows[1:2, 0:D].to_broadcast([P, D])).then_inc(g("frow"), 16)
            x2v = x2_d.rearrange("(i p) d -> i p d", p=P)
            for i in range(NT):
                sp.dma_start(fin_x[:, i, :], x2v[i]).then_inc(g("fx0"), 16)
            outs = [y_prompt.rearrange("b (i p) d -> (b i) p d", p=P)[i] for i in range(PROMPT // P)] + \
                   [y_sample.rearrange("b (i p) d -> (b i) p d", p=P)[i] for i in range((TOK - PROMPT) // P)]
            for i in range(NT):
                sp.wait_ge(g("fo"), i + 1)
                sp.dma_start(outs[i], fin_x[:, i, :]).then_inc(g("fst0"), 16)
            sp.wait_ge(g("fst0"), 16 * NT)

        @block.gpsimd
        def _(po):
            chain = [0]

            def link(ins):
                chain[0] += 1
                ins.then_inc(g("pch"), 1)
                po.wait_ge(g("pch"), chain[0])
            po.memset(gatew[:], 0.0).then_inc(g("gatew0"), 1)
            po.memset(xb[:], 0.0).then_inc(g("pads"), 1)
            po.memset(zeros, 0.0).then_inc(g("zero"), 1)
            po.wait_ge(g("ze"), 2 * (2 * LC + QC + KVC))
            po.wait_ge(g("ropek"), 1)
            for h in range(1, NH):
                last = po.tensor_copy(kT[64:96, h, :], kT[64:96, 0, :])
            last.then_inc(g("kpe"), 1)
            po.wait_ge(g("gh"), 8)
            po.tensor_tensor(xb[:, :, 0:TOK], gg[:], gg[:], ALU.mult).then_inc(g("lsq"), 1)
            po.wait_ge(g("idx"), 1)
            po.wait_ge(g("xnst0"), 8 * NT)
            po.wait_ge(g("xnst1"), 8 * NT)
            po.wait_ge(g("ctl"), 1)
            iters = po.value_load(ctl[0:1, NBC:NBC + 1], min_val=NE // RING, max_val=ITERS_MAX)
            link(po.tensor_copy(idx_now[:, 0:1], idx[:, 0:1]))
            po.wait_ge(g("lgp"), NT)
            po.wait_ge(g("x2st0"), 8 * NT)
            po.wait_ge(g("x2st1"), 8 * NT)
            po.indirect_dma_start(xg[0:WB, 0, :], None, xn_d, bass.IndirectOffsetOnAxis(idx_now[:, 0:1], 0)).then_inc(g("xg0"), 16)
            with po.Fori(0, iters) as i:
                for s in range(RING):
                    b = i * RING + s
                    po.tensor_copy(idx_now[:, (s + 1) % RING:(s + 1) % RING + 1],
                                   idx[:, bass.ds(b + 1, 1)]).then_inc(g("ic"), 1)
                    po.wait_ge(g("xgp"), b + 1)
                    po.wait_ge(g("ic"), b + 1)
                    po.sem_inc(g("gather_go"), 1)
                    po.indirect_dma_start(xg[0:WB, (s + 1) % 2, :], None, xn_d,
                                          bass.IndirectOffsetOnAxis(idx_now[:, (s + 1) % RING:(s + 1) % RING + 1], 0)
                                          ).then_inc(g(f"xg{(s + 1) % 2}"), 16)
            po.wait_ge(g("ys0"), iters * (RING * 8) + 16)
            po.wait_ge(g("ys1"), iters * (RING * 8) + 16)
            po.wait_ge(g("dn"), iters * RING + 1)
            po.sem_inc(g("gather_go"), 1)
            for i in range(NT):
                for k in range(2):
                    po.indirect_dma_start(fin_y[:, k, i, :], None, ys_d,
                                          bass.IndirectOffsetOnAxis(pos_i[:, k * NT + i:k * NT + i + 1], 0)
                                          ).then_inc(s_fy[2 * i + k], 16)

        @block.tensor
        def _(pe):
            pe.wait_ge(g("consts"), 16)
            for i in range(NT):
                pe.wait_ge(g("un"), i + 1)
                for j in range(2):
                    if i >= 1:
                        pe.wait_ge(g("uT"), 2 * (i - 1) + j + 1)
                    for c in range(4):
                        last = pe.transpose(psum[4 + 2 * 0 + j][:, c * P:(c + 1) * P],
                                            un[:, i % 2, (4 * j + c) * P:(4 * j + c + 1) * P], ident)
                    last.then_inc(g("uTp"), 1)
            pe.wait_ge(g("uT"), 2 * NT)
            for u, (kind, c, n) in enumerate(units):
                if c == 0 and n == 0:
                    if kind == "x":
                        pe.wait_ge(g("winx"), 16)
                    if kind == "g":
                        pe.wait_ge(g("wing"), 16)
                    if kind == "z":
                        pe.wait_ge(g("winq"), 16)
                if u >= ZB:
                    pe.wait_ge(g("ze"), u - ZB + 1)
                t0, tn = CHUNKS[n]
                w, o, m = {"x": (win_x, c * P, P), "g": (win_g, c * P, P), "z": (win_q, c * P, P),
                           "k": (win_q, QL + KVL, RP)}[kind]
                for k in range(DC):
                    last = pe.matmul(psum[u % ZB][0:m, 0:tn], w[:, k, o:o + m], uT[:, k, t0:t0 + tn],
                                     start=(k == 0), stop=(k == DC - 1))
                last.then_inc(g("zp"), 1)
            pe.wait_ge(g("sqz"), 1)
            for a, (c0, cn) in enumerate(((0, QC), (QC, KVC))):
                for n, (t0, tn) in enumerate(CHUNKS):
                    for c in range(cn):
                        last = pe.matmul(psum[4 + 2 * a + n][:, 0:tn], ones, sqz[:, c0 + c, t0:t0 + tn],
                                         start=(c == 0), stop=(c == cn - 1))
                    last.then_inc(g("statp"), 1)
            pe.wait_ge(g("wq"), 16)
            pe.wait_ge(g("zn"), QC)
            for u, (kind, j, n) in enumerate(ups):
                if kind == "kn" and j == 0 and n == 0:
                    pe.wait_ge(g("zn"), QC + KVC)
                    pe.wait_ge(g("wkv"), 16)
                if u >= ZB:
                    pe.wait_ge(g("upe"), u - ZB + 1)
                t0, tn = CHUNKS[n]
                bank = psum[u % ZB]
                if kind in ("qr", "qn"):
                    o = 512 + j * P if kind == "qr" else j * P
                    for c in range(QC):
                        last = pe.matmul(bank[:, 0:tn], wq[:, c, o:o + P], zl[:, c, t0:t0 + tn],
                                         start=(c == 0), stop=(c == QC - 1))
                elif kind == "kn":
                    for c in range(KVC):
                        last = pe.matmul(bank[:, 0:tn], wkv[:, c, j * P:(j + 1) * P], zl[:, QC + c, t0:t0 + tn],
                                         start=(c == 0), stop=(c == KVC - 1))
                else:
                    for c in range(KVC):
                        last = pe.matmul(bank[:, :], zl[:, QC + c, j * P:(j + 1) * P], wkv[:, c, 512:1024],
                                         start=(c == 0), stop=(c == KVC - 1))
                last.then_inc(g("up"), 1)
            pe.wait_ge(g("gw"), 16 * 8)

            def gates(u):
                c, d = u // 2, u % 2
                pe.wait_ge(g("conv"), c + 1)
                if u >= 1:
                    pe.wait_ge(g("ga"), 4 * u)
                for t in range(2):
                    pe.matmul(psum[5 + t][:, :], gatew[:, t, d, c, :], xc[:, c % 2, XOFF[1]:XOFF[1] + 512],
                              start=True, stop=True)
                for t in range(2):
                    last = pe.matmul(psum[7][:, t * PROMPT:(t + 1) * PROMPT], gatew[:, t, d, c, :],
                                     xc[:, c % 2, 0:PROMPT], start=(t == 0), stop=(t == 1), skip_group_check=True)
                last.then_inc(g("gp"), 1)

            def scores(n):
                h, i = steps[n]
                k0, kn = keys(i)
                if n >= 2:
                    pe.wait_ge(g("pr"), n - 1)
                pe.matmul(psum[n % 2][:, 0:kn], qT[0:96, h, i * P:(i + 1) * P], kT[0:96, h, k0:k0 + kn],
                          start=True, stop=True).then_inc(g("sc"), 1)

            def turn(n):
                h, i = steps[n]
                kn = keys(i)[1]
                pe.wait_ge(g("pr"), n + 1)
                if n >= 2:
                    pe.wait_ge(g("pTe"), n - 1)
                for b in range(kn // P):
                    last = pe.transpose(psum[2 + n % 2][:, b * P:(b + 1) * P], prob[:, n % 2, b * P:(b + 1) * P], ident)
                last.then_inc(g("pT"), 1)

            def values(n):
                h, i = steps[n]
                k0, kn = keys(i)
                pe.wait_ge(g("pTe"), n + 1)
                if n >= 1:
                    pe.wait_ge(g("pve"), n)
                for b in range(kn // P):
                    last = pe.matmul(psum[4][:, 0:VH], probT[:, n % 2, b * P:(b + 1) * P],
                                     V[:, k0 // P + b, h * VH:(h + 1) * VH], start=(b == 0), stop=(b == kn // P - 1))
                last.then_inc(g("pv"), 1)
            pe.wait_ge(g("upe"), len(ups))
            pe.wait_ge(g("ropeq"), 8)
            pe.wait_ge(g("kpe"), 1)
            scores(0)
            for n in range(len(steps)):
                if n % NT == 0:
                    gates(n // NT)
                if n + 1 < len(steps):
                    scores(n + 1)
                turn(n)
                if n >= 1:
                    values(n - 1)
            values(len(steps) - 1)
            pe.wait_ge(g("lsq"), 1)
            pe.wait_ge(g("ga"), 32)
            for n, (t0, tn) in enumerate(CHUNKS):
                for c in range(LC):
                    last = pe.matmul(psum[5 + n][:, 0:tn], ones, xb[:, c, t0:t0 + tn], start=(c == 0), stop=(c == LC - 1))
                last.then_inc(g("lst"), 1)
            for i in range(NT):
                pe.wait_ge(g("an"), i + 1)
                if i >= 2:
                    pe.wait_ge(g("atT"), i - 1)
                for c in range(LC):
                    last = pe.transpose(psum[i % 2][:, c * P:(c + 1) * P], att[:, i, c * P:(c + 1) * P], ident)
                last.then_inc(g("atp"), 1)
            pe.wait_ge(g("wout"), 16)
            pe.wait_ge(g("ln"), LC)
            pe.wait_ge(g("wrt"), 16)

            def router(i):
                pe.wait_ge(g("x2n"), i + 1)
                for j in range(2):
                    if i >= 1:
                        pe.wait_ge(g("tt"), 2 * (i - 1) + j + 1)
                    for c in range(4):
                        last = pe.transpose(psum[6 + j][:, c * P:(c + 1) * P], xn[:, i % 2, (4 * j + c) * P:(4 * j + c + 1) * P], ident)
                    last.then_inc(g("ttp"), 1)
                pe.wait_ge(g("tt"), 2 * i + 2)
                if i >= 1:
                    pe.wait_ge(g("lg"), i)
                for c in range(DC):
                    last = pe.matmul(psum[0][:, 0:NG + NE], tT[:, c, :], wrt[:, c, :], start=(c == 0), stop=(c == DC - 1))
                last.then_inc(g("lgp"), 1)
            pe.wait_ge(g("atT"), NT)
            for i in range(NT):
                for half in range(2):
                    bank = psum[2 + 2 * (i % 2) + half]
                    if i >= 2:
                        pe.wait_ge(g("x2"), i - 1)
                    for c in range(2 * LC):
                        src = gg if c >= LC else attT
                        last = pe.matmul(bank[:, :], src[:, c % LC, i * P:(i + 1) * P], wout[:, c, half * 512:(half + 1) * 512],
                                         start=(c == 0), stop=(c == 2 * LC - 1))
                    last.then_inc(g("op"), 1)
                if i >= 1:
                    router(i - 1)
            router(NT - 1)
            pe.wait_ge(g("rt_m"), 1)
            for i in range(NT):
                for j in range(i):
                    pe.matmul(psum[1][:, i * NE:(i + 1) * NE], ones, mask[:, j, :], start=(i == 0 and j == 0),
                              stop=False, skip_group_check=True)
                pe.matmul(psum[1][:, i * NE:(i + 1) * NE], before, mask[:, i, :], start=(i == 0),
                          stop=(i == NT - 1), skip_group_check=True)
            for j in range(NT):
                last = pe.matmul(psum[2][:, 0:NE], ones, mask[:, j, :], start=(j == 0), stop=(j == NT - 1))
            last.then_inc(g("rt_p"), 1)
            pe.wait_ge(g("rt_a"), 1)
            for k in range(2 * NT):
                last = pe.matmul(psum[3][0:WB, 0:NBC], oh_w[:, k, :], oh_b[:, k, :], start=(k == 0), stop=(k == 2 * NT - 1))
            last.then_inc(g("rt_ap"), 1)

            pe.wait_ge(g("ctl"), 1)
            iters = pe.value_load(ctl[0:1, NBC:NBC + 1], min_val=NE // RING, max_val=ITERS_MAX)

            def turn_rows(par, b, first=False):
                pe.wait_ge(g(f"xg{par}"), 16 if first else (b - par) * 8 + 16)
                if not first:
                    pe.wait_ge(g("xT"), b * 2)
                for j in range(2):
                    for c in range(4):
                        last = pe.transpose(psum[2 + j][:, c * WB:(c + 1) * WB],
                                            xg[0:WB, par, (4 * j + c) * P:(4 * j + c + 1) * P], ident[0:WB, 0:WB])
                last.then_inc(g("xgp"), 1)
            pe.sem_inc(g("xgp"), 1)
            pe.sem_inc(g("dn"), 1)
            pe.wait_ge(g("idx"), 1)
            turn_rows(0, 0, True)
            with pe.Fori(0, iters) as i:
                for s in range(RING):
                    b = i * RING + s
                    w = ring[:, s * SLOT:(s + 1) * SLOT]
                    wgu = w[:, 0:2 * DC * F].rearrange("p (t c n) -> p t c n", t=2, c=DC)
                    wdn = w[:, 2 * DC * F:].rearrange("p (k n) -> p k n", k=FC)
                    pe.wait_ge(s_wg[s], i * 32 + 32)
                    pe.wait_ge(g("xT"), b * 2 + 2)
                    for f in range(FC):
                        pe.wait_ge(g("hh"), b * FC + f + 1)
                        for t in range(2):
                            for c in range(DC):
                                last = pe.matmul(psum[f][:, t * WB:(t + 1) * WB], wgu[:, t, c, f * P:(f + 1) * P],
                                                 xT[:, s % 2, c, :], start=(t == 0 and c == 0), stop=(t == 1 and c == DC - 1),
                                                 skip_group_check=True)
                        if f == 0:
                            last.then_inc(g("gp2"), 1)
                    last.then_inc(g("gu"), 1)
                    turn_rows((s + 1) % 2, b + 1)
                    pe.wait_ge(s_wd[s], i * 16 + 16)
                    pe.wait_ge(g("ye"), b + 1)
                    for k in range(FC):
                        pe.wait_ge(g("hh"), (b + 1) * FC + k + 1)
                        for half in range(2):
                            last = pe.matmul(psum[4 + 2 * (s % 2) + half][0:WB, :], hT[:, k, :],
                                             wdn[:, k, half * 512:(half + 1) * 512], start=(k == 0), stop=(k == FC - 1),
                                             skip_group_check=True)
                    last.then_inc(g("dn"), 1)

        @block.scalar
        def _(ac):
            chain = [0]

            def link(ins):
                chain[0] += 1
                ins.then_inc(g("ach"), 1)
                ac.wait_ge(g("ach"), chain[0])
            eps = C("eps")
            ac.wait_ge(g("consts"), 16)
            ac.wait_ge(g("cols"), 16)
            for i in range(NT):
                ac.wait_ge(g(f"x{i % 2}"), 16 * (i // 2 + 1))
                link(ac.activation(junk, xin[:, i % 2, :], ACT.Square, accum_out=ssq[:, i:i + 1]))
                ac.activation(rstd1[:, i:i + 1], ssq[:, i:i + 1], ACT.Sqrt, bias=eps, scale=1.0 / D).then_inc(g("sd"), 1)
            ac.wait_ge(g("pads"), 1)
            for u, (kind, c, n) in enumerate(units):
                ac.wait_ge(g("zp"), u + 1)
                t0, tn = CHUNKS[n]
                src = psum[u % ZB]
                if kind == "x":
                    ins = ac.activation(xb[:, c, XOFF[n] + 1:XOFF[n] + 1 + tn], src[:, 0:tn], ACT.Copy)
                elif kind == "g":
                    ins = ac.activation(gg[:, c, t0:t0 + tn], src[:, 0:tn], ACT.Gelu_apprx_tanh)
                elif kind == "z":
                    ins = ac.activation(zl[:, c, t0:t0 + tn], src[:, 0:tn], ACT.Copy)
                else:
                    ins = ac.activation(kr[0:RP, t0:t0 + tn], src[0:RP, 0:tn], ACT.Copy)
                ins.then_inc(g("ze"), 1)
            ac.wait_ge(g("ze"), len(units))
            ac.activation(sqz, zl, ACT.Square).then_inc(g("sqz"), 1)
            ac.wait_ge(g("lam"), 1)
            ac.activation(lam_t[:, 1, :], lam_t[:, 0, :], ACT.Exp, scale=-1.0).then_inc(g("lamA"), 1)
            ac.wait_ge(g("lam"), 2)
            ac.activation(lam_t[:, 3, :], lam_t[:, 2, :], ACT.Ln).then_inc(g("lamA"), 1)
            ac.wait_ge(g("ys_init"), 16)
            for a, (w, dst) in enumerate(((QL, 0), (KVL, 1))):
                for n, (t0, tn) in enumerate(CHUNKS):
                    ac.wait_ge(g("statp"), 2 * a + n + 1)
                    ac.activation(rn[:, dst, t0:t0 + tn], psum[4 + 2 * a + n][:, 0:tn], ACT.Sqrt, bias=eps,
                                  scale=1.0 / w).then_inc(g("rqs"), 1)
            for u, (kind, j, n) in enumerate(ups):
                ac.wait_ge(g("up"), u + 1)
                t0, tn = CHUNKS[n]
                src = psum[u % ZB]
                if kind == "qr":
                    if u == 0:
                        ac.wait_ge(g("statp"), 4)
                    ins = ac.activation(qr[:, j, t0:t0 + tn], src[:, 0:tn], ACT.Copy)
                elif kind == "v":
                    if j == 0:
                        ac.wait_ge(g("zp"), len(units))
                    ins = ac.activation(V[:, j, :], src[:, :], ACT.Copy)
                else:
                    dst = qT if kind == "qn" else kT
                    if n == 0 and j == 0:
                        ac.wait_ge(g("zp"), len(units))
                    ac.activation(dst[0:64, 2 * j, t0:t0 + tn], src[0:64, 0:tn], ACT.Copy)
                    ins = ac.activation(dst[0:64, 2 * j + 1, t0:t0 + tn], src[64:128, 0:tn], ACT.Copy)
                ins.then_inc(g("upe"), 1)

            def exps(n):
                h, i = steps[n]
                kn = keys(i)[1]
                ac.wait_ge(g("mxd"), n + 1)
                if n >= 2:
                    ac.wait_ge(g("pT"), n - 1)
                    ac.wait_ge(g("pve"), n - 1)
                ac.activation(prob[:, n % 2, 0:kn], psum[n % 2][:, 0:kn], ACT.Exp, bias=nm[:, n % 2:n % 2 + 1], scale=SCALE,
                              accum_out=rs[:, n % 2:n % 2 + 1]).then_inc(g("pr"), 1)

            def pt_out(n):
                kn = keys(steps[n][1])[1]
                ac.wait_ge(g("pT"), n + 1)
                if n >= 2:
                    ac.wait_ge(g("pv"), n - 1)
                ac.activation(probT[:, n % 2, 0:kn], psum[2 + n % 2][:, 0:kn], ACT.Copy).then_inc(g("pTe"), 1)

            def unit_a(u):
                c, d = u // 2, u % 2
                j = d * LC + c
                ac.wait_ge(g("gp"), u + 1)
                if u >= 1:
                    ac.wait_ge(g("gh"), u)
                for t, (dst, hb) in enumerate(((thr, hb_r), (thi, hb_i))):
                    ac.activation(dst[:, PROMPT:TOK], psum[5 + t][:, :], ACT.Tanh, bias=hb[:, j:j + 1], scale=0.5).then_inc(g("ga"), 1)
                    ac.activation(dst[:, 0:PROMPT], psum[7][:, t * PROMPT:(t + 1) * PROMPT], ACT.Tanh,
                                  bias=hb[:, j:j + 1], scale=0.5).then_inc(g("ga"), 1)
                ac.wait_ge(g("ga"), 4 * u + 4)
                ac.activation(dec, thr, ACT.Exp, bias=lamc[:, j:j + 1], scale=lamc[:, j:j + 1])
                ac.activation(th, thr, ACT.Tanh, bias=nlamc[:, j:j + 1], scale=nlamc[:, j:j + 1])
                ac.activation(dec2, thr, ACT.Exp, bias=lam2[:, j:j + 1], scale=lam2[:, j:j + 1]).then_inc(g("gx"), 1)

            def unit_b(u):
                ac.wait_ge(g("gm"), 2 * u + 1)
                ac.activation(th, dec2, ACT.Sqrt, scale=0.25).then_inc(g("gs"), 1)
            ac.wait_ge(g("lam"), 4)
            exps(0)
            for n in range(len(steps)):
                u = n // NT
                if n + 1 < len(steps):
                    exps(n + 1)
                if n % NT == 0:
                    unit_a(u)
                if n % NT == 3:
                    unit_b(u)
                pt_out(n)
            for n, (t0, tn) in enumerate(CHUNKS):
                ac.wait_ge(g("lst"), n + 1)
                ac.activation(rnorm2[:, t0:t0 + tn], psum[5 + n][:, 0:tn], ACT.Sqrt, bias=eps, scale=1.0 / LRU).then_inc(g("lrs"), 1)
            for i in range(NT):
                if i == 0:
                    ac.wait_ge(g("pve"), len(steps))
                    ac.wait_ge(g("pv"), len(steps))
                ac.activation(probT[:, 0, :] if i % 2 == 0 else probT[:, 1, :], att[:, i, :], ACT.Square,
                              accum_out=ssq[:, i:i + 1]).then_inc(g("asq"), 1)
                ac.wait_ge(g("asq"), i + 1)
            ac.activation(rstd1, ssq, ACT.Sqrt, bias=eps, scale=1.0 / 512).then_inc(g("asd"), 1)
            for i in range(NT):
                ac.wait_ge(g("x2"), i + 1)
                link(ac.activation(sqj, x2t[:, i % 2, :], ACT.Square, accum_out=ssq2[:, i:i + 1]))
                ac.activation(rstd2[:, i:i + 1], ssq2[:, i:i + 1], ACT.Sqrt, bias=eps, scale=1.0 / D).then_inc(g("x2s"), 1)
                ac.dma_start(x2_d[i * P:(i + 1) * P, :], x2t[:, i % 2, :]).then_inc(g(f"x2st{i % 2}"), 16)
                ac.wait_ge(g("x2n"), i + 1)
                ac.dma_start(xn_d[i * P:(i + 1) * P, :], xn[:, i % 2, :]).then_inc(g(f"xnst{i % 2}"), 16)
            ac.wait_ge(g("rt_d"), 1)
            ac.activation(g4b, g4b, ACT.Exp).then_inc(g("rt_e"), 1)
            ac.wait_ge(g("rt_d"), 2)
            ac.activation(v6[5], v6[4], ACT.Exp).then_inc(g("rt_e"), 1)
            ac.wait_ge(g("ctl"), 1)
            iters = ac.value_load(ctl[0:1, NBC:NBC + 1], min_val=NE // RING, max_val=ITERS_MAX)
            ac.sem_inc(g("ys0"), 16)
            ac.sem_inc(g("ys1"), 16)
            ac.sem_inc(g("ye"), 2)
            with ac.Fori(0, iters) as i:
                for s in range(RING):
                    b = i * RING + s
                    for f in range(FC):
                        ac.wait_ge(g("gp2") if f == 0 else g("gu"), b + 1)
                        ac.activation(act_t[:, f, :], psum[f][:, 0:WB], ACT.Tanh, scale=0.5).then_inc(g("tnh"), 1)
                    ac.wait_ge(g(f"ys{s % 2}"), (b - s % 2) * 8 + 16)
                    ac.wait_ge(g("dn"), b + 2)
                    for half in range(2):
                        ins = ac.activation(ysb[0:WB, s % 2, half * 512:(half + 1) * 512],
                                            psum[4 + 2 * (s % 2) + half][0:WB, :], ACT.Copy)
                    ins.then_inc(g("ye"), 1)
                    ac.wait_ge(g("ye"), b + 3)
                    ac.dma_start(ys_d[bass.ds(b * WB, WB), :], ysb[0:WB, s % 2, :]).then_inc(g(f"ys{s % 2}"), 16)
            for i in range(NT):
                ac.wait_ge(g("fs"), 2 * i + 2)
                link(ac.activation(fin_junk, fin_x[:, i, :], ACT.Square, accum_out=ssq3[:, i:i + 1]))
                ac.activation(rstd3[:, i:i + 1], ssq3[:, i:i + 1], ACT.Sqrt, bias=eps, scale=1.0 / D).then_inc(g("fq"), 1)

        def bc(a, n):
            return a.unsqueeze(2).to_broadcast([P, a.shape[1], n])

        def bm(a, n):
            return a.unsqueeze(1).to_broadcast([P, n, a.shape[1]])

        def routing(v, link):
            v.wait_ge(g("lg"), NT)
            gl, el = logits[:, :, 0:NG], logits[:, :, NG:NG + NE]
            iota_e = C("iota_e", NE)

            def first_max(src, n, work, top, at, hot):
                io = bm(iota_e[:, 0:n], NT)
                link(v.tensor_reduce(top, src, AX.X, ALU.max))
                link(v.tensor_tensor(work, src, bc(top, n), ALU.is_equal))
                link(v.scalar_tensor_tensor(out=work, in0=work, scalar=-64.0, in1=io, op0=ALU.mult, op1=ALU.add))
                link(v.tensor_reduce(at, work, AX.X, ALU.min))
                link(v.tensor_scalar(at, at, 64.0, None, ALU.add))
                link(v.tensor_tensor(hot, io, bc(at, n), ALU.is_equal))
            first_max(gl, NG, g4, v6[0], v6[1], g4)
            v.tensor_tensor(g4b, gl, bc(v6[0], NG), ALU.subtract).then_inc(g("rt_d"), 1)
            link(v.tensor_tensor(em.rearrange("p i (g e) -> p i g e", g=NG), el.rearrange("p i (g e) -> p i g e", g=NG),
                                 g4.unsqueeze(3).to_broadcast([P, NT, NG, EG]), ALU.mult))
            link(v.tensor_scalar(g4, g4, -1.0, BIG, ALU.add, ALU.mult))
            link(v.tensor_tensor(em.rearrange("p i (g e) -> p i g e", g=NG), em.rearrange("p i (g e) -> p i g e", g=NG),
                                 g4.unsqueeze(3).to_broadcast([P, NT, NG, EG]), ALU.add))
            first_max(em, NE, t1, v6[2], v6[3], E0)
            link(v.scalar_tensor_tensor(out=em, in0=E0, scalar=-2 * BIG, in1=em, op0=ALU.mult, op1=ALU.add))
            first_max(em, NE, t1, v6[6], v6[7], E1)
            v.tensor_tensor(mask, E0, E1, ALU.add).then_inc(g("rt_m"), 1)
            v.tensor_tensor(v6[4], v6[6], v6[2], ALU.subtract).then_inc(g("rt_d"), 1)
            v.wait_ge(g("rt_e"), 2)
            link(v.tensor_reduce(v6[8], g4b, AX.X, ALU.add))
            link(v.tensor_scalar(v6[9], v6[5], 1.0, None, ALU.add))
            link(v.tensor_tensor(v6[9], v6[9], v6[8], ALU.mult))
            link(v.reciprocal(v6[9], v6[9]))
            link(v.tensor_scalar(gate0, v6[9], 0.5, None, ALU.mult))
            link(v.tensor_tensor(gate1, gate0, v6[5], ALU.mult))
            r, q, ovs, at, blk, sel, place, pos = v12
            v.wait_ge(g("rt_p"), 1)
            link(v.tensor_copy(rank.rearrange("p i e -> p (i e)"), psum[1][:, 0:NT * NE]))
            link(v.tensor_copy(cnt, psum[2][:, 0:NE]))
            for k, E in enumerate((E0, E1)):
                link(v.tensor_tensor(t1, E, rank, ALU.mult))
                link(v.tensor_reduce(r[:, k * NT:(k + 1) * NT], t1, AX.X, ALU.add))
            thr_m = C("thr", MAXQ)
            link(v.tensor_tensor(q9, bc(r, MAXQ), bm(thr_m, 2 * NT), ALU.is_ge))
            link(v.tensor_reduce(q, q9, AX.X, ALU.add))
            link(v.tensor_tensor(q9e, bc(cnt, MAXQ), bm(thr_m, NE), ALU.is_gt))
            link(v.tensor_reduce(ovf, q9e, AX.X, ALU.add))
            link(v.tensor_tensor_scan(off_end, ones[:, 0:NE], ovf, 0.0, ALU.mult, ALU.add))
            link(v.tensor_tensor(off, off_end, ovf, ALU.subtract))
            for k, (E, a) in enumerate(((E0, v6[3]), (E1, v6[7]))):
                link(v.tensor_tensor(t1, E, bm(off, NT), ALU.mult))
                link(v.tensor_reduce(ovs[:, k * NT:(k + 1) * NT], t1, AX.X, ALU.add))
                link(v.tensor_copy(at[:, k * NT:(k + 1) * NT], a))
            link(v.tensor_tensor(ovs, ovs, q, ALU.add))
            link(v.scalar_tensor_tensor(out=blk, in0=ovs, scalar=float(NE - 1), in1=at, op0=ALU.add, op1=ALU.subtract))
            link(v.tensor_scalar(sel, q, 0.5, None, ALU.is_gt))
            link(v.tensor_tensor(blk, blk, sel, ALU.mult))
            link(v.tensor_tensor(blk, blk, at, ALU.add))
            link(v.scalar_tensor_tensor(out=place, in0=q, scalar=-float(WB), in1=r, op0=ALU.mult, op1=ALU.add))
            link(v.tensor_tensor(oh_w, bc(place, WB), bm(C("iota_w", WB), 2 * NT), ALU.is_equal))
            link(v.tensor_tensor(oh_b, bc(blk, NBC), bm(C("iota_b", NBC), 2 * NT), ALU.is_equal))
            for k in range(2):
                part = oh_b[:, k * NT:(k + 1) * NT, :]
                ins = v.tensor_tensor(part, part, bc(C("tokid", NT), NBC), ALU.mult)
            ins.then_inc(g("rt_a"), 1)
            link(v.tensor_tensor(xe, bc(C("iota_x", EXTRA), NE), bm(off, EXTRA), ALU.is_ge))
            link(v.tensor_tensor(xe2, bc(C("iota_x", EXTRA), NE), bm(off_end, EXTRA), ALU.is_lt))
            link(v.tensor_tensor(xe, xe, xe2, ALU.mult))
            link(v.tensor_tensor(xe, xe, bm(iota_e, EXTRA), ALU.mult))
            link(v.tensor_reduce(ctlf[:, NE:NBC], xe, AX.X, ALU.add))
            link(v.tensor_copy(ctlf[:, 0:NE], iota_e))
            link(v.tensor_scalar(itt, C("iter_thr", ITERS_MAX), off_end[:, NE - 1:NE], None, ALU.is_lt))
            link(v.tensor_reduce(ctlf[:, NBC:NBC + 1], itt, AX.X, ALU.add))
            link(v.tensor_scalar(ctlf[:, NBC:NBC + 1], ctlf[:, NBC:NBC + 1], float(NE // RING), None, ALU.add))
            v.tensor_copy(ctl[0:1, 0:NBC + 1], ctlf[0:1, :]).then_inc(g("ctl"), 1)
            link(v.scalar_tensor_tensor(out=pos, in0=blk, scalar=float(WB), in1=place, op0=ALU.mult, op1=ALU.add))
            link(v.tensor_copy(pos_i[:], pos))
            v.wait_ge(g("rt_ap"), 1)
            v.tensor_copy(idx[:], psum[3][0:WB, 0:NBC]).then_inc(g("idx"), 1)

        @block.vector
        def _(v):
            chain = [0]

            def link(ins):
                chain[0] += 1
                ins.then_inc(g("dch"), 1)
                v.wait_ge(g("dch"), chain[0])
            v.wait_ge(g("cols"), 16)
            for i in range(NT):
                v.wait_ge(g("sd"), i + 1)
                link(v.reciprocal(rstd1[:, i:i + 1], rstd1[:, i:i + 1]))
                if i >= 2:
                    v.wait_ge(g("uTp"), 2 * (i - 1))
                v.tensor_scalar(un[:, i % 2, :].rearrange("t (c p) -> t p c", c=DC),
                                xin[:, i % 2, :].rearrange("t (p c) -> t p c", c=DC),
                                rstd1[:, i:i + 1], None, ALU.mult).then_inc(g("un"), 1)
                for j in range(2):
                    v.wait_ge(g("uTp"), 2 * i + j + 1)
                    n1 = cols[:, COLS["norm1"] + 4 * j:COLS["norm1"] + 4 * j + 4].unsqueeze(2).to_broadcast([P, 4, P])
                    v.tensor_tensor(uT[:, 4 * j:4 * j + 4, i * P:(i + 1) * P],
                                    psum[4 + j][:, :].rearrange("p (c t) -> p c t", c=4), n1, ALU.mult).then_inc(g("uT"), 1)
            lam = cols[:, COLS["lam"]:COLS["lam"] + 8]
            link(v.tensor_scalar(lam_t[:, 4, :], lam, -1.0, None, ALU.mult))
            link(v.tensor_tensor(lam_t[:, 0, :], lam_t[:, 4, :], lam, ALU.max))
            link(v.tensor_scalar(hb_r, cols[:, COLS["b_rg"]:COLS["b_rg"] + 8], 0.5, None, ALU.mult))
            v.tensor_scalar(hb_i, cols[:, COLS["b_ig"]:COLS["b_ig"] + 8], 0.5, None, ALU.mult).then_inc(g("lam"), 1)
            v.wait_ge(g("lamA"), 1)
            v.tensor_scalar(lam_t[:, 2, :], lam_t[:, 1, :], 1.0, None, ALU.add).then_inc(g("lam"), 1)
            v.wait_ge(g("lam"), 2)
            v.wait_ge(g("lamA"), 2)
            link(v.tensor_scalar(lam_t[:, 5, :], lam_t[:, 2, :], 1.0, None, ALU.is_equal))
            link(v.tensor_tensor(lam_t[:, 3, :], lam_t[:, 3, :], lam_t[:, 5, :], ALU.add))
            link(v.tensor_tensor(lam_t[:, 3, :], lam_t[:, 3, :], lam_t[:, 1, :], ALU.mult))
            link(v.scalar_tensor_tensor(out=lam_t[:, 5, :], in0=lam_t[:, 2, :], scalar=-1.0, in1=lam_t[:, 5, :],
                                        op0=ALU.add, op1=ALU.add))
            link(v.reciprocal(lam_t[:, 5, :], lam_t[:, 5, :]))
            link(v.tensor_tensor(lam_t[:, 3, :], lam_t[:, 3, :], lam_t[:, 5, :], ALU.mult))
            link(v.scalar_tensor_tensor(out=lam_t[:, 3, :], in0=lam_t[:, 4, :], scalar=0.0, in1=lam_t[:, 3, :],
                                        op0=ALU.max, op1=ALU.add))
            link(v.tensor_scalar(lamc, lam_t[:, 3, :], -4.0, None, ALU.mult))
            link(v.tensor_scalar(nlamc, lam_t[:, 3, :], 4.0, None, ALU.mult))
            v.tensor_scalar(lam2[:], lam_t[:, 3, :], -8.0, None, ALU.mult).then_inc(g("lam"), 2)

            for a in range(2):
                for n in range(2):
                    t0, tn = CHUNKS[n]
                    v.wait_ge(g("rqs"), 2 * a + n + 1)
                    link(v.reciprocal(rn[:, a, t0:t0 + tn], rn[:, a, t0:t0 + tn]))
                for c in range(QC) if a == 0 else range(QC, QC + KVC):
                    gain = col("q_norm", c) if a == 0 else col("kv_norm", c - QC)
                    v.scalar_tensor_tensor(out=zl[:, c, :], in0=zl[:, c, :], scalar=gain, in1=rn[:, a, :],
                                           op0=ALU.mult, op1=ALU.mult).then_inc(g("zn"), 1)
            swap = list(range(16, 32)) + list(range(0, 16))
            v.wait_ge(g("ze"), len(units))
            v.wait_ge(g("rope"), 16)
            link(v.stream_shuffle(krs, kr[0:RP, :], swap))
            link(v.tensor_tensor(krs, krs, rope[0:RP, 1, :], ALU.mult))
            link(v.tensor_tensor(kr[0:RP, :], kr[0:RP, :], rope[0:RP, 0, :], ALU.mult))
            v.tensor_tensor(kT[64:96, 0, :], kr[0:RP, :], krs, ALU.add).then_inc(g("ropek"), 1)

            def conv(c):
                n = XPAD - 3
                if c >= 2:
                    v.wait_ge(g("gh"), 2 * c - 2)
                wcol = lambda t: col("conv_w", t * LC + c)
                link(v.tensor_scalar(xc[:, c % 2, 0:n], xb[:, c, 0:n], wcol(0), col("conv_b", c), ALU.mult, ALU.add))
                for t in range(1, 4):
                    ins = v.scalar_tensor_tensor(out=xc[:, c % 2, 0:n], in0=xb[:, c, t:t + n], scalar=wcol(t),
                                                 in1=xc[:, c % 2, 0:n], op0=ALU.mult, op1=ALU.add)
                    if t < 3:
                        link(ins)
                ins.then_inc(g("conv"), 1)
            v.wait_ge(g("upe"), 4)
            v.wait_ge(g("ropek"), 1)
            for r in range(2):
                link(v.stream_shuffle(qs[:, r, :], qr[:, r, :], swap))
                link(v.tensor_tensor(qs[:, r, :], qs[:, r, :], rope[:, 1, :], ALU.mult))
                link(v.tensor_tensor(qr[:, r, :], qr[:, r, :], rope[:, 0, :], ALU.mult))
                for j in range(4):
                    v.tensor_tensor(qT[64:96, 4 * r + j, :], qr[32 * j:32 * j + 32, r, :], qs[32 * j:32 * j + 32, r, :],
                                    ALU.add).then_inc(g("ropeq"), 1)
            v.wait_ge(g("statp"), 4)
            conv(0)
            conv(1)

            def maxes(n):
                kn = keys(steps[n][1])[1]
                v.wait_ge(g("sc"), n + 1)
                if n >= 2:
                    v.wait_ge(g("pr"), n - 1)
                link(v.tensor_reduce(mx[:, n % 2:n % 2 + 1], psum[n % 2][:, 0:kn], AX.X, ALU.max))
                v.tensor_scalar(nm[:, n % 2:n % 2 + 1], mx[:, n % 2:n % 2 + 1], -SCALE, None, ALU.mult).then_inc(g("mxd"), 1)

            def att_out(n):
                h, i = steps[n]
                v.wait_ge(g("pr"), n + 1)
                link(v.reciprocal(rr[:, n % 2:n % 2 + 1], rs[:, n % 2:n % 2 + 1]))
                v.wait_ge(g("pv"), n + 1)
                v.tensor_scalar(att[:, i, h * VH:(h + 1) * VH], psum[4][:, 0:VH], rr[:, n % 2:n % 2 + 1], None,
                                ALU.mult).then_inc(g("pve"), 1)

            def unit_m(u):
                c = u // 2
                v.wait_ge(g("gx"), u + 1)
                v.scalar_tensor_tensor(out=dec2, in0=dec2, scalar=1.0, in1=th, op0=ALU.add, op1=ALU.mult).then_inc(g("gm"), 1)
                for n, (t0, tn) in enumerate(CHUNKS):
                    ins = v.scalar_tensor_tensor(out=thi[:, t0:t0 + tn], in0=thi[:, t0:t0 + tn], scalar=1.0,
                                                 in1=xc[:, c % 2, XOFF[n]:XOFF[n] + tn], op0=ALU.add, op1=ALU.mult)
                ins.then_inc(g("gm"), 1)

            def unit_s(u):
                c, d = u // 2, u % 2
                v.wait_ge(g("gs"), u + 1)
                v.wait_ge(g("gm"), 2 * u + 2)
                link(v.tensor_tensor(thi, thi, th, ALU.mult))
                h_fwd = xb[:, c, 0:TOK]
                for n, (t0, tn) in enumerate(CHUNKS):
                    if d == 0:
                        ins = v.tensor_tensor_scan(h_fwd[:, t0:t0 + tn], dec[:, t0:t0 + tn], thi[:, t0:t0 + tn], 0.0,
                                                   ALU.mult, ALU.add)
                    else:
                        ins = v.tensor_tensor_scan(thr[:, t0:t0 + tn][:, ::-1], dec[:, t0:t0 + tn][:, ::-1],
                                                   thi[:, t0:t0 + tn][:, ::-1], 0.0, ALU.mult, ALU.add)
                    if d == 1 or n == 0:
                        link(ins)
                if d == 0:
                    ins.then_inc(g("gh"), 1)
                else:
                    link(v.tensor_tensor(h_fwd, h_fwd, thr, ALU.add))
                    v.tensor_tensor(gg[:, c, :], gg[:, c, :], h_fwd, ALU.mult).then_inc(g("gh"), 1)
            maxes(0)
            for n in range(len(steps)):
                u = n // NT
                if n + 1 < len(steps):
                    maxes(n + 1)
                if n % NT == 1:
                    unit_m(u)
                if n % NT == 5:
                    unit_s(u)
                    if u % 2 == 1 and u // 2 + 2 < LC:
                        conv(u // 2 + 2)
                if n >= 1:
                    att_out(n - 1)
            att_out(len(steps) - 1)
            v.wait_ge(g("lrs"), 2)
            link(v.reciprocal(rnorm2, rnorm2))
            for c in range(LC):
                v.scalar_tensor_tensor(out=gg[:, c, :], in0=gg[:, c, :], scalar=col("lru_norm", c), in1=rnorm2,
                                       op0=ALU.mult, op1=ALU.mult).then_inc(g("ln"), 1)
            v.wait_ge(g("asd"), 1)
            link(v.reciprocal(rstd1, rstd1))
            for i in range(NT):
                v.tensor_scalar(att[:, i, :], att[:, i, :], rstd1[:, i:i + 1], None, ALU.mult).then_inc(g("an"), 1)
            ga = cols[:, COLS["att_norm"]:COLS["att_norm"] + LC].unsqueeze(2).to_broadcast([P, LC, P])
            v.wait_ge(g("up"), len(ups))
            for i in range(NT):
                v.wait_ge(g("atp"), i + 1)
                v.tensor_tensor(attT[:, :, i * P:(i + 1) * P], psum[i % 2][:, :].rearrange("p (c t) -> p c t", c=LC), ga,
                                ALU.mult).then_inc(g("atT"), 1)
            v.wait_ge(g("rows"), 32)

            def logits_out(i):
                v.wait_ge(g("lgp"), i + 1)
                v.tensor_tensor(logits[:, i, :], psum[0][:, 0:NG + NE], brt[:], ALU.add).then_inc(g("lg"), 1)

            def tt_out(i):
                for j in range(2):
                    v.wait_ge(g("ttp"), 2 * i + j + 1)
                    if i >= 1:
                        v.wait_ge(g("lgp"), i)
                    v.tensor_copy(tT[:, 4 * j:4 * j + 4, :], psum[6 + j][:, :].rearrange("p (c t) -> p c t", c=4)).then_inc(g("tt"), 1)
            for i in range(NT):
                v.wait_ge(g(f"xr{i % 2}"), 16 * (i // 2 + 1))
                v.wait_ge(g("op"), 2 * i + 2)
                for half in range(2):
                    ins = v.tensor_tensor(x2t[:, i % 2, half * 512:(half + 1) * 512], psum[2 + 2 * (i % 2) + half][:, :],
                                          x2t[:, i % 2, half * 512:(half + 1) * 512], ALU.add)
                ins.then_inc(g("x2"), 1)
                v.wait_ge(g("x2s"), i + 1)
                link(v.reciprocal(rstd2[:, i:i + 1], rstd2[:, i:i + 1]))
                if i >= 2:
                    v.wait_ge(g(f"xnst{i % 2}"), 16 * (i // 2))
                    v.wait_ge(g("ttp"), 2 * (i - 1))
                v.scalar_tensor_tensor(out=xn[:, i % 2, :].rearrange("t (c p) -> t p c", c=DC),
                                       in0=x2t[:, i % 2, :].rearrange("t (p c) -> t p c", c=DC), scalar=rstd2[:, i:i + 1],
                                       in1=n2row[:].rearrange("t (p c) -> t p c", c=DC),
                                       op0=ALU.mult, op1=ALU.mult).then_inc(g("x2n"), 1)
                tt_out(i)
                logits_out(i)
            routing(v, link)
            v.wait_ge(g("idx"), 1)
            v.wait_ge(g("ctl"), 1)
            iters = v.value_load(ctl[0:1, NBC:NBC + 1], min_val=NE // RING, max_val=ITERS_MAX)

            def rows_out(par, b, first=False):
                v.wait_ge(g("xgp"), 2 if first else b + 2)
                for j in range(2):
                    v.tensor_copy(xT[:, par, 4 * j:4 * j + 4, :],
                                  psum[2 + j][:, 0:4 * WB].rearrange("p (c n) -> p c n", c=4)).then_inc(g("xT"), 1)
            v.sem_inc(g("hh"), FC)
            rows_out(0, 0, True)
            with v.Fori(0, iters) as i:
                for s in range(RING):
                    b = i * RING + s
                    for f in range(FC):
                        v.wait_ge(g("tnh"), b * FC + f + 1)
                        v.scalar_tensor_tensor(out=act_s[:, f, :], in0=act_t[:, f, :], scalar=1.0, in1=psum[f][:, 0:WB],
                                               op0=ALU.add, op1=ALU.mult).then_inc(g("acs"), 1)
                        v.wait_ge(g("acs"), b * FC + f + 1)
                        v.wait_ge(g("dn"), b + 1)
                        v.tensor_tensor(hT[:, f, :], act_s[:, f, :], psum[f][:, WB:2 * WB], ALU.mult).then_inc(g("hh"), 1)
                    rows_out((s + 1) % 2, b + 1)
            v.wait_ge(g("frow"), 16)
            v.wait_ge(g("fx0"), 16 * NT)
            for i in range(NT):
                for k, gt in enumerate((gate0, gate1)):
                    v.wait_ge(s_fy[2 * i + k], 16)
                    v.scalar_tensor_tensor(out=fin_x[:, i, :], in0=fin_y[:, k, i, :], scalar=gt[:, i:i + 1],
                                           in1=fin_x[:, i, :], op0=ALU.mult, op1=ALU.add).then_inc(g("fs"), 1)
                    v.wait_ge(g("fs"), 2 * i + k + 1)
                v.wait_ge(g("fq"), i + 1)
                link(v.reciprocal(rstd3[:, i:i + 1], rstd3[:, i:i + 1]))
                v.scalar_tensor_tensor(out=fin_x[:, i, :], in0=fin_x[:, i, :], scalar=rstd3[:, i:i + 1], in1=fin_row,
                                       op0=ALU.mult, op1=ALU.mult).then_inc(g("fo"), 1)


def kernel(**inputs):
    import numpy as np
    import concourse.bacc as bacc
    from concourse.bass_utils import run_bass_kernel_spmd as run

    a = {k: np.asarray(v) for k, v in inputs.items()}

    def feat(v, inner):
        return v.reshape(P, -1) if inner else v.reshape(-1, P).T
    cols = np.concatenate([feat(a["norm1"][0], True), feat(a["q_norm"][0], False), feat(a["kv_norm"][0], False)] +
                          [feat(a["conv_w"][0].reshape(-1), False), feat(a["conv_b"][0], False),
                           feat(a["b_rg"][0].reshape(-1), False), feat(a["b_ig"][0].reshape(-1), False),
                           feat(a["lru_lambda"][0].reshape(-1), False), feat(a["att_out_norm"][0], False),
                           feat(a["lru_out_norm"][0], False)], axis=1)
    c = np.zeros((P, NCONSTS), np.float32)

    def put(name, v):
        v = np.asarray(v, np.float32)
        c[:, CONSTS[name]:CONSTS[name] + v.shape[-1]] = v
    put("ident", np.eye(P))
    put("before", np.triu(np.ones((P, P)), 1))
    put("ones", np.ones((P, P)))
    put("iota_w", np.arange(WB)[None])
    put("iota_b", np.arange(NBC)[None])
    put("iota_e", np.arange(NE)[None])
    put("thr", WB * (1 + np.arange(MAXQ))[None])
    put("tokid", np.arange(TOK).reshape(NT, P).T)
    put("eps", np.full((1, 1), EPS))
    put("iota_x", np.arange(EXTRA)[None])
    put("iter_thr", RING * np.arange(ITERS_MAX)[None])
    inv = 1.0 / (np.float32(10000.0) ** (np.arange(0, RP, 2, dtype=np.float32) / np.float32(RP)))
    at = np.concatenate([np.arange(n, dtype=np.float32) for _, n in CHUNKS])
    ang = (at[None, :] * inv[:, None].astype(np.float32)).astype(np.float32)
    cos, sin = np.cos(ang), np.sin(ang)
    rope = np.concatenate([np.tile(np.concatenate([cos, cos]), (4, 1)), np.tile(np.concatenate([-sin, sin]), (4, 1))], axis=1)
    rows = np.zeros((3, D), np.float32)
    rows[0] = a["norm2"][0]
    rows[1] = a["final_norm"]
    rows[2, :NG] = a["b_group"][0]
    rows[2, NG:NG + NE] = a["b_router"][0]
    wq = a["w_q_up"][0].reshape(QL, NH, NOPE + RP)
    wkv = a["w_kv_up"][0].reshape(KVL, NH, NOPE + VH)
    ins = {
        "x": np.concatenate([a["x_prompt"].reshape(-1, D), a["x_sample"].reshape(-1, D)]),
        "cols": cols, "consts": c, "rope_t": rope, "rows": rows, "w_in": a["w_in"][0],
        "w_q": np.concatenate([wq[..., :NOPE].reshape(QL, -1), wq[..., NOPE:].reshape(QL, -1)], axis=1),
        "w_kv": np.concatenate([wkv[..., :NOPE].reshape(KVL, -1), wkv[..., NOPE:].reshape(KVL, -1)], axis=1),
        "w_rg": a["w_rg"][0], "w_ig": a["w_ig"][0], "w_out": a["w_out"][0],
        "w_router": np.concatenate([a["w_group"][0], a["w_router"][0]], axis=1),
        "w_gate": a["w_gate"][0], "w_up": a["w_up"][0], "w_down": a["w_down"][0],
    }
    nc = bacc.Bacc("TRN2", target_bir_lowering=False, num_devices=1)
    arrays, args = {}, []
    for name, v in ins.items():
        v = np.ascontiguousarray(v)
        arrays[f"in_{name}"] = v
        args.append(nc.dram_tensor(f"in_{name}", v.shape, mybir.dt.from_np(v.dtype), kind="ExternalInput").ap())
    for i, n in enumerate((PROMPT, TOK - PROMPT)):
        args.append(nc.dram_tensor(f"out_{i}", (1, n, D), mybir.dt.float32, kind="ExternalOutput").ap())
    encoder_layer(nc, *args)
    r = run(nc, [arrays], core_ids=[0])
    return tuple(r.results[0][f"out_{i}"] for i in range(2))
```

```python
import concourse.bass as bass
from concourse import mybir
from contextlib import ExitStack

P = 128
TOK, PROMPT = 768, 256
NT = TOK // P
D = 1024
DC = D // P
QL, KVL, RP, LRU = 384, 256, 32, 512
NH, NOPE, VH = 8, 64, 64
LC = LRU // P
QC, KVC = QL // P, KVL // P
CHUNKS = ((0, PROMPT), (PROMPT, TOK - PROMPT))
XPAD = (PROMPT + 3) + (TOK - PROMPT + 3)
XOFF = (0, PROMPT + 3)
IN_W = QL + KVL + RP + 2 * LRU
NE, NG, EG, F = 32, 4, 8, 256
FC = F // P
WB = 80
RING = 4
MAXQ = (TOK - 1) // WB
MAXB = NE + (2 * TOK) // WB
ITERS_MAX = -(-MAXB // RING)
NBC = RING * ITERS_MAX + 1
EXTRA = NBC - NE
EPS = 1e-6
SCALE = float(NOPE + RP) ** -0.5
BIG = 1e30

COLS = {}
_at = 0
for _n, _w in (("norm1", DC), ("q_norm", QC), ("kv_norm", KVC), ("conv_w", 4 * LC), ("conv_b", LC),
               ("b_rg", 2 * LC), ("b_ig", 2 * LC), ("lam", 2 * LC), ("att_norm", LC), ("lru_norm", LC)):
    COLS[_n] = _at
    _at += _w
NCOLS = _at
CONSTS = {}
_at = 0
for _n, _w in (("ident", P), ("before", P), ("ones", P), ("iota_w", WB), ("iota_b", NBC), ("iota_e", NE),
               ("thr", MAXQ), ("tokid", NT), ("eps", 1), ("iota_x", EXTRA), ("iter_thr", ITERS_MAX)):
    CONSTS[_n] = _at
    _at += _w
NCONSTS = _at


def encoder_layer(nc, A_x, A_cols, A_consts, A_rope, A_rows, A_win, A_wq, A_wkv, A_wrg, A_wig, A_wout,
                  A_wrt, A_wgate, A_wup, A_wdown, y_prompt, y_sample):
    f32, i32 = mybir.dt.float32, mybir.dt.int32
    ALU = mybir.AluOpType
    ACT = mybir.ActivationFunctionType
    AX = mybir.AxisListType
    ctx = ExitStack()
    with ctx:
        def sb(name, shape, dt=f32):
            return ctx.enter_context(nc.sbuf_tensor(name, shape, dt))

        def sem(name):
            return ctx.enter_context(nc.semaphore(name))

        SLOT = 3 * DC * F
        ring = sb("ring", [P, RING * SLOT])
        lowrank = sb("lowrank", [P, (QC + KVC) * TOK])
        upw = sb("upw", [P, QC * TOK + KVC * D])
        xb = sb("xb", [P, LC, XPAD])
        gg = sb("gg", [P, LC, TOK])
        softm = sb("softm", [P, 2048])
        rope = sb("rope", [P, 2, TOK])
        consts = sb("consts", [P, NCONSTS])
        cols = sb("cols", [P, NCOLS])
        n2row = sb("n2row", [P, D])
        tmp = sb("tmp", [P, 6144])
        gatew = sb("gatew", [P, 2, 2, LC, P])
        wrt = sb("wrt", [P, DC, NG + NE])
        brt = sb("brt", [P, NG + NE])
        small = sb("small", [P, 160])
        idx = sb("idx", [WB, NBC], i32)
        idx_now = sb("idx_now", [WB, RING], i32)
        pos_i = sb("pos_i", [P, 2 * NT], i32)
        ctl = sb("ctl", [1, NBC + 3], i32)
        psum = [ctx.enter_context(nc.psum_tensor(f"bank{b}", [P, 512], f32)) for b in range(8)]
        x2_d = nc.dram_tensor("x2_rows", [TOK, D], f32, kind="Internal").ap()
        xn_d = nc.dram_tensor("xn_rows", [TOK, D], f32, kind="Internal").ap()
        ys_d = nc.dram_tensor("expert_rows", [NBC * WB, D], f32, kind="Internal").ap()

        def C(name, n=None, p0=0, p1=P):
            a = CONSTS[name]
            return consts[p0:p1, a:a + (n or 1)]

        ident, before, ones = C("ident", P), C("before", P), C("ones", P)

        def col(name, j, p0=0, p1=P):
            a = COLS[name] + j
            return cols[p0:p1, a:a + 1]

        logits = rope[:, 0, 0:NT * (NG + NE)].rearrange("p (i n) -> p i n", i=NT)
        uT = ring[:, 0:DC * TOK].rearrange("p (c t) -> p c t", c=DC)
        qT = ring[:, 0:NH * TOK].rearrange("p (h t) -> p h t", h=NH)
        win = ring[:, SLOT:SLOT + DC * IN_W]
        NQK = QL + KVL + RP
        W_XB, W_QK, W_GB = 0, DC * LRU, DC * (LRU + NQK)
        win_x = win[:, W_XB:W_XB + DC * LRU].rearrange("p (c n) -> p c n", c=DC)
        win_g = win[:, W_GB:W_GB + DC * LRU].rearrange("p (c n) -> p c n", c=DC)
        win_q = win[:, W_QK:W_QK + DC * NQK].rearrange("p (c n) -> p c n", c=DC)
        kT = ring[:, SLOT:SLOT + NH * TOK].rearrange("p (h t) -> p h t", h=NH)
        wout = ring[:, 2 * SLOT:2 * SLOT + DC * D].rearrange("p (c n) -> p c n", c=DC)
        V = ring[:, 3 * SLOT + 3072:4 * SLOT].rearrange("p (i n) -> p i n", i=NT)
        zl = lowrank[:, :].rearrange("p (c t) -> p c t", c=QC + KVC)
        att = lowrank[:, 0:NT * 512].rearrange("p (i n) -> p i n", i=NT)
        wq = upw[:, 0:QC * TOK].rearrange("p (c n) -> p c n", c=QC)
        wkv = upw[:, QC * TOK:].rearrange("p (c n) -> p c n", c=KVC)
        attT = upw[:, 0:LC * TOK].rearrange("p (c t) -> p c t", c=LC)
        prob = softm[:, 0:1024].rearrange("p (b n) -> p b n", b=2)
        probT = softm[:, 1024:2048].rearrange("p (b n) -> p b n", b=2)
        xin = tmp[:, 0:2 * D].rearrange("p (b n) -> p b n", b=2)
        un = tmp[:, 2 * D:4 * D].rearrange("p (b n) -> p b n", b=2)
        junk = tmp[:, 4 * D:5 * D]
        spare = SLOT + DC * IN_W
        sqz = ring[:, spare:spare + (QC + KVC) * TOK].rearrange("p (c t) -> p c t", c=QC + KVC)
        kr = ring[:, spare + (QC + KVC) * TOK:spare + (QC + KVC + 1) * TOK]
        rn = ring[:, 2 * SLOT:2 * SLOT + 2 * TOK].rearrange("p (a t) -> p a t", a=2)
        krs = ring[0:RP, 2 * SLOT + 2 * TOK:2 * SLOT + 3 * TOK]
        qr = ring[:, 2 * SLOT:2 * SLOT + 2 * TOK].rearrange("p (r t) -> p r t", r=2)
        qs = ring[:, 2 * SLOT + 2 * TOK:2 * SLOT + 4 * TOK].rearrange("p (r t) -> p r t", r=2)
        xc = softm[:, 0:2 * (XPAD - 3)].rearrange("p (b n) -> p b n", b=2)
        temps = [[tmp[:, (4 * k + m) * TOK:(4 * k + m + 1) * TOK] for m in range(4)] for k in range(2)]
        rnorm2 = tmp[:, 5 * D:5 * D + TOK]
        att_junk = tmp[:, 4 * D:4 * D + 512]
        rstd1 = small[:, 0:NT]
        ssq = small[:, 8:8 + NT]
        lamc = small[:, 16:24]
        nlamc = small[:, 24:32]
        lam_t = small[:, 32:80].rearrange("p (k n) -> p k n", k=6)
        hb_r = small[:, 80:88]
        hb_i = small[:, 88:96]
        mx, nm, rs, rr = (small[:, 32 + 4 * k:36 + 4 * k] for k in range(4))
        ssq2 = small[:, 104:104 + NT]
        rstd2 = small[:, 112:112 + NT]
        gate0 = small[:, 120:120 + NT]
        gate1 = small[:, 128:128 + NT]
        ssq3 = small[:, 136:136 + NT]
        rstd3 = small[:, 144:144 + NT]

        xn = tmp[:, 2 * D:4 * D].rearrange("p (b n) -> p b n", b=2)
        x2t = tmp[:, 0:2 * D].rearrange("p (b n) -> p b n", b=2)
        tT = tmp[:, 4 * D:5 * D].rearrange("p (c t) -> p c t", c=DC)
        flat = lowrank
        E0 = flat[:, 0:192].rearrange("p (i e) -> p i e", i=NT)
        E1 = flat[:, 192:384].rearrange("p (i e) -> p i e", i=NT)
        mask = flat[:, 384:576].rearrange("p (i e) -> p i e", i=NT)
        em = flat[:, 576:768].rearrange("p (i e) -> p i e", i=NT)
        t1 = flat[:, 768:960].rearrange("p (i e) -> p i e", i=NT)
        rank = flat[:, 960:1152].rearrange("p (i e) -> p i e", i=NT)
        g4 = flat[:, 1152:1152 + 24].rearrange("p (i n) -> p i n", i=NT)
        g4b = flat[:, 1176:1176 + 24].rearrange("p (i n) -> p i n", i=NT)
        v6 = [flat[:, 1200 + 8 * k:1200 + 8 * k + NT] for k in range(16)]
        v12 = [flat[:, 1328 + 16 * k:1328 + 16 * k + 2 * NT] for k in range(8)]
        cnt = flat[:, 1456:1456 + NE]
        ovf = flat[:, 1488:1488 + NE]
        off = flat[:, 1520:1520 + NE]
        off_end = flat[:, 1552:1552 + NE]
        q9 = upw[:, 0:2 * NT * MAXQ].rearrange("p (k m) -> p k m", m=MAXQ)
        q9e = upw[:, 256:256 + NE * MAXQ].rearrange("p (e m) -> p e m", m=MAXQ)
        xe = upw[:, 640:640 + EXTRA * NE].rearrange("p (x e) -> p x e", e=NE)
        xe2 = upw[:, 1408:1408 + EXTRA * NE].rearrange("p (x e) -> p x e", e=NE)
        itt = upw[:, 2200:2200 + ITERS_MAX]
        ctlf = upw[:, 2220:2220 + NBC + 1]
        oh_w = upw[:, 2304:2304 + 2 * NT * WB].rearrange("p (k w) -> p k w", k=2 * NT)
        oh_b = upw[:, 3300:3300 + 2 * NT * NBC].rearrange("p (k w) -> p k w", k=2 * NT)
        zeros = n2row[:, 0:D]
        sqj = softm[:, 0:D]
        lam2 = small[:, 152:160]
        fin_x = ring[:, 0:NT * D].rearrange("p (i n) -> p i n", i=NT)
        fin_y = ring[:, SLOT:SLOT + 2 * NT * D].rearrange("p (k i n) -> p k i n", k=2, i=NT)
        fin_row = ring[:, 3 * SLOT:3 * SLOT + D]
        fin_junk = ring[:, 3 * SLOT + D:3 * SLOT + 2 * D]
        xg = tmp[:, 0:2 * D].rearrange("p (b n) -> p b n", b=2)
        ysb = tmp[:, 2 * D:4 * D].rearrange("p (b n) -> p b n", b=2)
        xT = tmp[:, 4 * D:4 * D + 2 * DC * WB].rearrange("p (b c n) -> p b c n", b=2, c=DC)
        act_t = xb[:, 0, 0:FC * WB].rearrange("p (f n) -> p f n", f=FC)
        act_s = xb[:, 1, 0:FC * WB].rearrange("p (f n) -> p f n", f=FC)
        hT = xb[:, 2, 0:FC * WB].rearrange("p (f n) -> p f n", f=FC)

        S = {}
        for n in ("consts", "cols", "rope", "rows", "x0", "x1", "n2", "gel", "stc", "aq", "winx", "wing", "winq", "wq", "wkv", "gw", "wout", "wrt",
                  "gatew0", "pads", "gather_go", "zero", "ys_init",
                  "sqd", "sd", "rs1", "un", "uTp", "uT", "zp", "ze", "conv", "lamA", "lam",
                  "sqz", "statp", "rqs", "rq", "zn", "up", "upe", "ropeq", "ropek", "kpe", "vp", "vpe",
                  "sc", "mxd", "pr", "pT", "pTe", "pv", "pve",
                  "gp", "ga", "gm", "gs", "gh",
                  "lsq", "lst", "lrs", "ln", "asq", "asd", "an", "atp", "atT",
                  "xr0", "xr1", "op", "x2", "x2s", "x2q", "x2n", "x2st0", "x2st1", "xnst0", "xnst1", "ttp", "tt", "lgp", "lg",
                  "rt_e", "rt_d", "rt_m", "rt_p", "rt_a", "rt_ap", "ctl", "idx",
                  "ic", "xg0", "xg1", "xgp", "xT", "gu", "tnh", "hh", "dn", "ye", "ys0", "ys1", "wd0s",
                  "fx0", "fx1", "fs", "fq", "fo", "fr", "fst0", "fst1", "frow",
                  "dch", "ach", "pch", "gp2", "gx", "acs"):
            S[n] = sem("s_" + n)
        s_wg = [sem(f"s_wgu{s}") for s in range(RING)]
        s_fy = [sem(f"s_fy{k}") for k in range(2 * NT)]
        s_wd = [sem(f"s_wd{s}") for s in range(RING)]

        def g(name):
            return S[name]

        units = [("x", c, n) for n in range(2) for c in range(LC)] + \
                [("z", c, n) for c in range(QC + KVC) for n in range(2)] + [("k", 0, n) for n in range(2)] + \
                [("g", c, n) for c in range(LC) for n in range(2)]
        U_Z, U_G = 2 * LC, 2 * (LC + QC + KVC + 1)
        GATES_AT = {U_Z + 1: 0, U_Z + 2: 1, U_Z + 5: 2, U_Z + 6: 3, U_Z + 9: 4, U_Z + 10: 5, U_G + 1: 6, U_G + 2: 7}
        ROOTS_AT = {U_Z + 4: 0, U_Z + 8: 1, U_G: 2}
        STATS_AT = {U_G + 2 + k: k for k in range(4)}
        STATS_END = U_G + 6
        ZB = 4
        steps = [(h, i) for h in range(NH) for i in range(NT)]

        def keys(i):
            return CHUNKS[0] if i * P < PROMPT else CHUNKS[1]

        ups = [("qr", r, n) for r in range(2) for n in range(2)] + \
              [("qn", m, n) for m in range(4) for n in range(2)] + \
              [("kn", m, n) for m in range(4) for n in range(2)] + \
              [("v", i, 0) for i in range(NT)]
        LSUM_AT = len(ups) - 2
        GELU_AT = {2: 0, 4: 1, 6: 2, 8: 3}

        block = ctx.enter_context(nc.Block())

        @block.sync
        def _(sp):
            sp.dma_start(consts[:], A_consts).then_inc(g("consts"), 16)
            sp.dma_start(cols[:], A_cols).then_inc(g("cols"), 16)
            xv = A_x.rearrange("(i p) d -> i p d", p=P)

            def load_x(i):
                if i >= 2:
                    sp.wait_ge(g("un"), i - 1)
                sp.dma_start(xin[:, i % 2, :], xv[i]).then_inc(g(f"x{i % 2}"), 16)
            load_x(0)
            load_x(1)
            wv = A_win.rearrange("(p c) n -> p c n", c=DC)
            o = NQK
            sp.dma_start(win_x, wv[:, :, o:o + LRU]).then_inc(g("winx"), 16)
            for i in range(2, NT):
                load_x(i)
            sp.dma_start(win_q, wv[:, :, 0:NQK]).then_inc(g("winq"), 16)
            sp.wait_ge(g("gatew0"), 1)
            for t, src in enumerate((A_wrg, A_wig)):
                for half in range(2):
                    for d in range(2):
                        sp.dma_start(gatew[64 * half:64 * half + 64, t, d, :, 64 * half:64 * half + 64],
                                     src[d].rearrange("(c two) i o -> two i c o", two=2)[half]).then_inc(g("gw"), 16)
            sp.dma_start(wq, A_wq.rearrange("(c p) n -> p c n", p=P)).then_inc(g("wq"), 16)
            sp.dma_start(wkv, A_wkv.rearrange("(c p) n -> p c n", p=P)).then_inc(g("wkv"), 16)
            sp.dma_start(win_g, wv[:, :, o + LRU:o + 2 * LRU]).then_inc(g("wing"), 16)
            sp.dma_start(rope[:], A_rope.rearrange("p (a t) -> p a t", a=2)).then_inc(g("rope"), 16)
            sp.dma_start(brt[:], A_rows[2:3, 0:NG + NE].to_broadcast([P, NG + NE])).then_inc(g("rows"), 16)
            sp.dma_start(wrt[:], A_wrt.rearrange("(p c) n -> p c n", c=DC)).then_inc(g("wrt"), 16)
            sp.wait_ge(g("zero"), 1)
            zr = EXTRA * WB // 120
            sp.dma_start(ys_d[NE * WB:, :].rearrange("(p r) d -> p r d", r=zr),
                         zeros[0:120, :].unsqueeze(1).to_broadcast([120, zr, D])).then_inc(g("ys_init"), 16)
            sp.wait_ge(g("ys_init"), 16)
            sp.dma_start(n2row[:], A_rows[0:1, 0:D].to_broadcast([P, D])).then_inc(g("rows"), 16)
            sp.wait_ge(g("zp"), len(units))
            sp.wait_ge(g("statp"), 4)
            sp.wait_ge(g("ropeq"), 8)
            sp.dma_start(wout, A_wout.rearrange("(c p) n -> p c n", p=P)).then_inc(g("wout"), 16)

            def load_res(i):
                if i >= 2:
                    sp.wait_ge(g(f"x2st{i % 2}"), 16 * (i // 2))
                    sp.wait_ge(g("x2n"), i - 1)
                sp.dma_start(tmp[:, (i % 2) * D:(i % 2 + 1) * D], xv[i]).then_inc(g(f"xr{i % 2}"), 16)
            sp.wait_ge(g("gh"), 8)
            for i in range(NT):
                load_res(i)

            wg_v = A_wgate.rearrange("e (p c) n -> e p (c n)", c=DC)
            wu_v = A_wup.rearrange("e (p c) n -> e p (c n)", c=DC)
            wd_v = A_wdown.rearrange("e (k p) n -> e p k n", p=P)

            def load_expert(s, e, gu=True, dn=True):
                base = s * SLOT
                if gu:
                    sp.dma_start(ring[:, base:base + DC * F], wg_v[e]).then_inc(s_wg[s], 16)
                    sp.dma_start(ring[:, base + DC * F:base + 2 * DC * F], wu_v[e]).then_inc(s_wg[s], 16)
                if dn:
                    sp.dma_start(ring[:, base + 2 * DC * F:base + 3 * DC * F]
                                 .rearrange("p (k n) -> p k n", k=FC), wd_v[e]).then_inc(s_wd[s], 16)
            sp.wait_ge(g("sc"), len(steps))
            load_expert(0, 0)
            load_expert(1, 1)
            sp.wait_ge(g("op"), 2 * NT)
            load_expert(2, 2)
            load_expert(3, 3)
            sp.wait_ge(g("ctl"), 1)
            iters = sp.value_load(ctl[0:1, NBC:NBC + 1], min_val=NE // RING, max_val=ITERS_MAX)
            with sp.Fori(1, iters) as i:
                for s in range(RING):
                    b = i * RING + s
                    e = sp.value_load(ctl[0:1, bass.ds(b, 1)], min_val=0, max_val=NE - 1)
                    sp.wait_ge(g("gu"), b - RING + 1)
                    sp.dma_start(ring[:, s * SLOT:s * SLOT + DC * F], wg_v[bass.ds(e, 1)].rearrange("e p n -> (e p) n")).then_inc(s_wg[s], 16)
                    sp.dma_start(ring[:, s * SLOT + DC * F:s * SLOT + 2 * DC * F], wu_v[bass.ds(e, 1)].rearrange("e p n -> (e p) n")).then_inc(s_wg[s], 16)
                    sp.wait_ge(g("dn"), b - RING + 2)
                    sp.dma_start(ring[:, s * SLOT + 2 * DC * F:(s + 1) * SLOT].rearrange("p (k n) -> p k n", k=FC),
                                 wd_v[bass.ds(e, 1)].rearrange("e p k n -> (e p) k n")).then_inc(s_wd[s], 16)
            sp.wait_ge(g("dn"), iters * RING + 1)
            sp.wait_ge(g("ctl"), 1)
            sp.dma_start(fin_row, A_rows[1:2, 0:D].to_broadcast([P, D])).then_inc(g("frow"), 16)
            x2v = x2_d.rearrange("(i p) d -> i p d", p=P)
            for i in range(NT):
                sp.dma_start(fin_x[:, i, :], x2v[i]).then_inc(g("fx0"), 16)
            outs = [y_prompt.rearrange("b (i p) d -> (b i) p d", p=P)[i] for i in range(PROMPT // P)] + \
                   [y_sample.rearrange("b (i p) d -> (b i) p d", p=P)[i] for i in range((TOK - PROMPT) // P)]
            for i in range(NT):
                sp.wait_ge(g("fo"), i + 1)
                sp.dma_start(outs[i], fin_x[:, i, :]).then_inc(g("fst0"), 16)
            sp.wait_ge(g("fst0"), 16 * NT)

        @block.gpsimd
        def _(po):
            chain = [0]

            def link(ins):
                chain[0] += 1
                ins.then_inc(g("pch"), 1)
                po.wait_ge(g("pch"), chain[0])
            po.memset(gatew[:], 0.0).then_inc(g("gatew0"), 1)
            po.memset(xb[:], 0.0).then_inc(g("pads"), 1)
            po.memset(zeros, 0.0).then_inc(g("zero"), 1)
            for c in range(LC):
                po.wait_ge(g("gel"), c + 1)
                po.wait_ge(g("gh"), 2 * c + 2)
                link(po.tensor_tensor(gg[:, c, :], gg[:, c, :], xb[:, c, 0:TOK], ALU.mult))
                po.tensor_tensor(xb[:, c, 0:TOK], gg[:, c, :], gg[:, c, :], ALU.mult).then_inc(g("lsq"), 1)
                po.wait_ge(g("lsq"), c + 1)
            po.wait_ge(g("ropek"), 1)
            for h in range(1, NH):
                last = po.tensor_copy(kT[64:96, h, :], kT[64:96, 0, :])
            last.then_inc(g("kpe"), 1)
            po.wait_ge(g("idx"), 1)
            po.wait_ge(g("xnst0"), 8 * NT)
            po.wait_ge(g("xnst1"), 8 * NT)
            po.wait_ge(g("ctl"), 1)
            iters = po.value_load(ctl[0:1, NBC:NBC + 1], min_val=NE // RING, max_val=ITERS_MAX)
            link(po.tensor_copy(idx_now[:, 0:1], idx[:, 0:1]))
            po.wait_ge(g("lgp"), NT)
            po.wait_ge(g("x2st0"), 8 * NT)
            po.wait_ge(g("x2st1"), 8 * NT)
            po.indirect_dma_start(xg[0:WB, 0, :], None, xn_d, bass.IndirectOffsetOnAxis(idx_now[:, 0:1], 0)).then_inc(g("xg0"), 16)
            with po.Fori(0, iters) as i:
                for s in range(RING):
                    b = i * RING + s
                    po.tensor_copy(idx_now[:, (s + 1) % RING:(s + 1) % RING + 1],
                                   idx[:, bass.ds(b + 1, 1)]).then_inc(g("ic"), 1)
                    po.wait_ge(g("xgp"), b + 1)
                    po.wait_ge(g("ic"), b + 1)
                    po.sem_inc(g("gather_go"), 1)
                    po.indirect_dma_start(xg[0:WB, (s + 1) % 2, :], None, xn_d,
                                          bass.IndirectOffsetOnAxis(idx_now[:, (s + 1) % RING:(s + 1) % RING + 1], 0)
                                          ).then_inc(g(f"xg{(s + 1) % 2}"), 16)
            po.wait_ge(g("ys0"), iters * (RING * 8) + 16)
            po.wait_ge(g("ys1"), iters * (RING * 8) + 16)
            po.wait_ge(g("dn"), iters * RING + 1)
            po.sem_inc(g("gather_go"), 1)
            for i in range(NT):
                for k in range(2):
                    po.indirect_dma_start(fin_y[:, k, i, :], None, ys_d,
                                          bass.IndirectOffsetOnAxis(pos_i[:, k * NT + i:k * NT + i + 1], 0)
                                          ).then_inc(s_fy[2 * i + k], 16)

        @block.tensor
        def _(pe):
            pe.wait_ge(g("consts"), 16)
            def turn_input(i):
                pe.wait_ge(g("un"), i + 1)
                for j in range(2):
                    if i >= 1:
                        pe.wait_ge(g("uT"), 2 * (i - 1) + j + 1)
                    for c in range(4):
                        last = pe.transpose(psum[4 + j][:, c * P:(c + 1) * P],
                                            un[:, i % 2, (4 * j + c) * P:(4 * j + c + 1) * P], ident)
                    last.then_inc(g("uTp"), 1)

            def gates(u):
                c, d = u // 2, u % 2
                pe.wait_ge(g("conv"), c + 1)
                if u >= 1:
                    pe.wait_ge(g("ga"), 4 * u)
                for t in range(2):
                    pe.matmul(psum[5 + t][:, :], gatew[:, t, d, c, :], xc[:, c % 2, XOFF[1]:XOFF[1] + 512],
                              start=True, stop=True)
                for t in range(2):
                    last = pe.matmul(psum[7][:, t * PROMPT:(t + 1) * PROMPT], gatew[:, t, d, c, :],
                                     xc[:, c % 2, 0:PROMPT], start=(t == 0), stop=(t == 1), skip_group_check=True)
                last.then_inc(g("gp"), 1)

            def latent_sums(k):
                a, n = k // 2, k % 2
                c0, cn = ((0, QC), (QC, KVC))[a]
                t0, tn = CHUNKS[n]
                pe.wait_ge(g("sqz"), 1)
                if k >= 1:
                    pe.wait_ge(g("stc"), k)
                for c in range(cn):
                    last = pe.matmul(psum[4][:, 0:tn], ones, sqz[:, c0 + c, t0:t0 + tn],
                                     start=(c == 0), stop=(c == cn - 1))
                last.then_inc(g("statp"), 1)

            turn_input(0)
            turn_input(1)
            pe.wait_ge(g("uT"), 4)
            pe.wait_ge(g("winx"), 16)
            for u, (kind, c, n) in enumerate(units):
                if u == LC:
                    pe.wait_ge(g("uT"), 2 * NT)
                if u == U_Z:
                    pe.wait_ge(g("winq"), 16)
                    pe.wait_ge(g("gw"), 16 * 8)
                if u == U_G:
                    pe.wait_ge(g("wing"), 16)
                if u in GATES_AT:
                    gates(GATES_AT[u])
                if u in STATS_AT:
                    latent_sums(STATS_AT[u])
                if u >= ZB:
                    pe.wait_ge(g("ze"), u - ZB + 1)
                t0, tn = CHUNKS[n]
                w, o, m = {"x": (win_x, c * P, P), "g": (win_g, c * P, P), "z": (win_q, c * P, P),
                           "k": (win_q, QL + KVL, RP)}[kind]
                for k in range(DC):
                    last = pe.matmul(psum[u % ZB][0:m, 0:tn], w[:, k, o:o + m], uT[:, k, t0:t0 + tn],
                                     start=(k == 0), stop=(k == DC - 1))
                last.then_inc(g("zp"), 1)
                if u < LC:
                    turn_input(2 + u)
            pe.wait_ge(g("wq"), 16)
            pe.wait_ge(g("zn"), QC)
            pe.wait_ge(g("ze"), len(units))
            for u, (kind, j, n) in enumerate(ups):
                if u == LSUM_AT:
                    pe.wait_ge(g("ga"), 32)
                    for m, (t0, tn) in enumerate(CHUNKS):
                        for c in range(LC):
                            if m == 0:
                                pe.wait_ge(g("lsq"), c + 1)
                            last = pe.matmul(psum[6 + m][:, 0:tn], ones, xb[:, c, t0:t0 + tn], start=(c == 0),
                                             stop=(c == LC - 1))
                        last.then_inc(g("lst"), 1)
                if kind == "kn" and j == 0 and n == 0:
                    pe.wait_ge(g("zn"), QC + KVC)
                    pe.wait_ge(g("wkv"), 16)
                if u >= ZB:
                    pe.wait_ge(g("upe"), u - ZB + 1)
                t0, tn = CHUNKS[n]
                bank = psum[u % ZB]
                if kind in ("qr", "qn"):
                    o = 512 + j * P if kind == "qr" else j * P
                    for c in range(QC):
                        last = pe.matmul(bank[:, 0:tn], wq[:, c, o:o + P], zl[:, c, t0:t0 + tn],
                                         start=(c == 0), stop=(c == QC - 1))
                elif kind == "kn":
                    for c in range(KVC):
                        last = pe.matmul(bank[:, 0:tn], wkv[:, c, j * P:(j + 1) * P], zl[:, QC + c, t0:t0 + tn],
                                         start=(c == 0), stop=(c == KVC - 1))
                else:
                    for c in range(KVC):
                        last = pe.matmul(bank[:, :], zl[:, QC + c, j * P:(j + 1) * P], wkv[:, c, 512:1024],
                                         start=(c == 0), stop=(c == KVC - 1))
                last.then_inc(g("up"), 1)
            def scores(n):
                h, i = steps[n]
                k0, kn = keys(i)
                if n >= 3:
                    pe.wait_ge(g("pr"), n - 2)
                pe.matmul(psum[n % 3][:, 0:kn], qT[0:96, h, i * P:(i + 1) * P], kT[0:96, h, k0:k0 + kn],
                          start=True, stop=True).then_inc(g("sc"), 1)

            def turn(n):
                kn = keys(steps[n][1])[1]
                pe.wait_ge(g("pr"), n + 1)
                if n >= 2:
                    pe.wait_ge(g("pTe"), n - 1)
                for b in range(kn // P):
                    last = pe.transpose(psum[3 + n % 2][:, b * P:(b + 1) * P], prob[:, n % 2, b * P:(b + 1) * P], ident)
                last.then_inc(g("pT"), 1)

            def values(n):
                h, i = steps[n]
                k0, kn = keys(i)
                pe.wait_ge(g("pTe"), n + 1)
                if n >= 1:
                    pe.wait_ge(g("pve"), n)
                for b in range(kn // P):
                    last = pe.matmul(psum[5][:, 0:VH], probT[:, n % 2, b * P:(b + 1) * P],
                                     V[:, k0 // P + b, h * VH:(h + 1) * VH], start=(b == 0), stop=(b == kn // P - 1))
                last.then_inc(g("pv"), 1)

            def turn_att(i):
                pe.wait_ge(g("pve"), len(steps) - NT + i + 1)
                if i < 2:
                    pe.wait_ge(g("lrs"), 2)
                else:
                    pe.wait_ge(g("atT"), i - 1)
                for c in range(LC):
                    last = pe.transpose(psum[6 + i % 2][:, c * P:(c + 1) * P], att[:, i, c * P:(c + 1) * P], ident)
                last.then_inc(g("atp"), 1)
            pe.wait_ge(g("upe"), len(ups))
            pe.wait_ge(g("ropeq"), 8)
            pe.wait_ge(g("kpe"), 1)
            scores(0)
            scores(1)
            for n in range(len(steps)):
                if n + 2 < len(steps):
                    scores(n + 2)
                turn(n)
                if n >= 1:
                    values(n - 1)
                if n - 3 >= len(steps) - NT:
                    turn_att(n - 3 - (len(steps) - NT))
            values(len(steps) - 1)
            for i in range(NT - 3, NT):
                turn_att(i)
            pe.wait_ge(g("wout"), 16)
            pe.wait_ge(g("ln"), LC)
            pe.wait_ge(g("wrt"), 16)

            def router(i):
                pe.wait_ge(g("x2n"), i + 1)
                pe.wait_ge(g("atT"), NT)
                for j in range(2):
                    if i >= 1:
                        pe.wait_ge(g("tt"), 2 * (i - 1) + j + 1)
                    for c in range(4):
                        last = pe.transpose(psum[6 + j][:, c * P:(c + 1) * P], xn[:, i % 2, (4 * j + c) * P:(4 * j + c + 1) * P], ident)
                    last.then_inc(g("ttp"), 1)
                pe.wait_ge(g("tt"), 2 * i + 2)
                if i >= 1:
                    pe.wait_ge(g("lg"), i)
                for c in range(DC):
                    last = pe.matmul(psum[0][:, 0:NG + NE], tT[:, c, :], wrt[:, c, :], start=(c == 0), stop=(c == DC - 1))
                last.then_inc(g("lgp"), 1)
            for i in range(NT):
                for half in range(2):
                    w = 2 * i + half
                    if w >= 2:
                        pe.wait_ge(g("x2"), w - 1)
                    for k, src in enumerate((gg, attT)):
                        if k == 1:
                            pe.wait_ge(g("atT"), i + 1)
                        for c in range(LC):
                            last = pe.matmul(psum[2 + 2 * half + k][:, :], src[:, c, i * P:(i + 1) * P],
                                             wout[:, (1 - k) * LC + c, half * 512:(half + 1) * 512],
                                             start=(c == 0), stop=(c == LC - 1))
                    last.then_inc(g("op"), 1)
                if i >= 1:
                    router(i - 1)
            router(NT - 1)
            pe.wait_ge(g("rt_m"), 1)
            for i in range(NT):
                for j in range(i):
                    pe.matmul(psum[1][:, i * NE:(i + 1) * NE], ones, mask[:, j, :], start=(i == 0 and j == 0),
                              stop=False, skip_group_check=True)
                pe.matmul(psum[1][:, i * NE:(i + 1) * NE], before, mask[:, i, :], start=(i == 0),
                          stop=(i == NT - 1), skip_group_check=True)
            for j in range(NT):
                last = pe.matmul(psum[2][:, 0:NE], ones, mask[:, j, :], start=(j == 0), stop=(j == NT - 1))
            last.then_inc(g("rt_p"), 1)
            pe.wait_ge(g("rt_a"), 1)
            for k in range(2 * NT):
                last = pe.matmul(psum[3][0:WB, 0:NBC], oh_w[:, k, :], oh_b[:, k, :], start=(k == 0), stop=(k == 2 * NT - 1))
            last.then_inc(g("rt_ap"), 1)

            pe.wait_ge(g("ctl"), 1)
            iters = pe.value_load(ctl[0:1, NBC:NBC + 1], min_val=NE // RING, max_val=ITERS_MAX)

            def turn_rows(par, b, first=False):
                pe.wait_ge(g(f"xg{par}"), 16 if first else (b - par) * 8 + 16)
                if not first:
                    pe.wait_ge(g("xT"), b * 2)
                for j in range(2):
                    for c in range(4):
                        last = pe.transpose(psum[2 + j][:, c * WB:(c + 1) * WB],
                                            xg[0:WB, par, (4 * j + c) * P:(4 * j + c + 1) * P], ident[0:WB, 0:WB])
                last.then_inc(g("xgp"), 1)
            pe.sem_inc(g("xgp"), 1)
            pe.sem_inc(g("dn"), 1)
            pe.wait_ge(g("idx"), 1)
            turn_rows(0, 0, True)
            with pe.Fori(0, iters) as i:
                for s in range(RING):
                    b = i * RING + s
                    w = ring[:, s * SLOT:(s + 1) * SLOT]
                    wgu = w[:, 0:2 * DC * F].rearrange("p (t c n) -> p t c n", t=2, c=DC)
                    wdn = w[:, 2 * DC * F:].rearrange("p (k n) -> p k n", k=FC)
                    pe.wait_ge(s_wg[s], i * 32 + 32)
                    pe.wait_ge(g("xT"), b * 2 + 2)
                    for f in range(FC):
                        pe.wait_ge(g("hh"), b * FC + f + 1)
                        for t in range(2):
                            for c in range(DC):
                                last = pe.matmul(psum[f][:, t * WB:(t + 1) * WB], wgu[:, t, c, f * P:(f + 1) * P],
                                                 xT[:, s % 2, c, :], start=(t == 0 and c == 0), stop=(t == 1 and c == DC - 1),
                                                 skip_group_check=True)
                        if f == 0:
                            last.then_inc(g("gp2"), 1)
                    last.then_inc(g("gu"), 1)
                    turn_rows((s + 1) % 2, b + 1)
                    pe.wait_ge(s_wd[s], i * 16 + 16)
                    pe.wait_ge(g("ye"), b + 1)
                    for k in range(FC):
                        pe.wait_ge(g("hh"), (b + 1) * FC + k + 1)
                        for half in range(2):
                            last = pe.matmul(psum[4 + 2 * (s % 2) + half][0:WB, :], hT[:, k, :],
                                             wdn[:, k, half * 512:(half + 1) * 512], start=(k == 0), stop=(k == FC - 1),
                                             skip_group_check=True)
                    last.then_inc(g("dn"), 1)

        @block.scalar
        def _(ac):
            chain = [0]

            def link(ins):
                chain[0] += 1
                ins.then_inc(g("ach"), 1)
                ac.wait_ge(g("ach"), chain[0])
            eps = C("eps")
            ac.wait_ge(g("consts"), 16)
            ac.wait_ge(g("cols"), 16)
            for i in range(NT):
                ac.wait_ge(g(f"x{i % 2}"), 16 * (i // 2 + 1))
                link(ac.activation(junk, xin[:, i % 2, :], ACT.Square, accum_out=ssq[:, i:i + 1]))
                ac.activation(rstd1[:, i:i + 1], ssq[:, i:i + 1], ACT.Sqrt, bias=eps, scale=1.0 / D).then_inc(g("sd"), 1)
            ac.wait_ge(g("lam"), 1)
            ac.activation(lam_t[:, 1, :], lam_t[:, 0, :], ACT.Exp, scale=-1.0).then_inc(g("lamA"), 1)
            ac.wait_ge(g("lam"), 2)
            ac.activation(lam_t[:, 3, :], lam_t[:, 2, :], ACT.Ln).then_inc(g("lamA"), 1)

            def unit_gates(u):
                c, d = u // 2, u % 2
                j = d * LC + c
                th_r, th_i, dec, dec2 = temps[d]
                ac.wait_ge(g("gp"), u + 1)
                if u >= 2:
                    ac.wait_ge(g("gh"), u - 1)
                else:
                    ac.wait_ge(g("uTp"), 2 * NT)
                for t, (dst, hb) in enumerate(((th_r, hb_r), (th_i, hb_i))):
                    ac.activation(dst[:, PROMPT:TOK], psum[5 + t][:, :], ACT.Tanh, bias=hb[:, j:j + 1], scale=0.5).then_inc(g("ga"), 1)
                    ac.activation(dst[:, 0:PROMPT], psum[7][:, t * PROMPT:(t + 1) * PROMPT], ACT.Tanh,
                                  bias=hb[:, j:j + 1], scale=0.5).then_inc(g("ga"), 1)
                ac.wait_ge(g("ga"), 4 * u + 4)
                ac.activation(dec, th_r, ACT.Exp, bias=lamc[:, j:j + 1], scale=lamc[:, j:j + 1]).then_inc(g("gx"), 1)
                ac.activation(dec2, th_r, ACT.Exp, bias=lam2[:, j:j + 1], scale=lam2[:, j:j + 1]).then_inc(g("gx"), 1)
                ac.wait_ge(g("gx"), 3 * u + 2)
                ac.activation(th_r, th_r, ACT.Tanh, bias=nlamc[:, j:j + 1], scale=nlamc[:, j:j + 1]).then_inc(g("gx"), 1)

            def pair_roots(c):
                for d in range(2):
                    u = 2 * c + d
                    ac.wait_ge(g("gm"), 2 * u + 1)
                    dec2 = temps[d][3]
                    ac.activation(dec2, dec2, ACT.Sqrt, scale=0.25).then_inc(g("gs"), 1)
            ac.wait_ge(g("pads"), 1)
            for u, (kind, c, n) in enumerate(units):
                if u in GATES_AT:
                    if GATES_AT[u] == 0:
                        ac.wait_ge(g("lam"), 4)
                    unit_gates(GATES_AT[u])
                if u in ROOTS_AT:
                    pair_roots(ROOTS_AT[u])
                if u == U_G:
                    ac.wait_ge(g("ze"), U_G)
                    ac.activation(sqz, zl, ACT.Square).then_inc(g("sqz"), 1)
                ac.wait_ge(g("zp"), u + 1)
                t0, tn = CHUNKS[n]
                src = psum[u % ZB]
                if kind == "x":
                    dst = xb[:, c, XOFF[n] + 1:XOFF[n] + 1 + tn]
                elif kind == "z":
                    dst = zl[:, c, t0:t0 + tn]
                elif kind == "k":
                    dst = kr[0:RP, t0:t0 + tn]
                else:
                    dst = gg[:, c, t0:t0 + tn]
                m = RP if kind == "k" else P
                ac.activation(dst, src[0:m, 0:tn], ACT.Copy).then_inc(g("ze"), 1)
                if u == STATS_END:
                    ac.wait_ge(g("stc"), 4)
                    ac.activation(rn, rn, ACT.Sqrt).then_inc(g("rqs"), 1)
                    pair_roots(3)
            for u, (kind, j, n) in enumerate(ups):
                ac.wait_ge(g("up"), u + 1)
                t0, tn = CHUNKS[n]
                src = psum[u % ZB]
                if kind == "qr":
                    if u == 0:
                        ac.wait_ge(g("zn"), QC + KVC)
                        ac.wait_ge(g("ropek"), 1)
                    ins = ac.activation(qr[:, j, t0:t0 + tn], src[:, 0:tn], ACT.Copy)
                elif kind == "v":
                    if j == 0:
                        ac.wait_ge(g("statp"), 4)
                    ins = ac.activation(V[:, j, :], src[:, :], ACT.Copy)
                else:
                    dst = qT if kind == "qn" else kT
                    if n == 0 and j == 0:
                        ac.wait_ge(g("zp"), len(units))
                    ac.activation(dst[0:64, 2 * j, t0:t0 + tn], src[0:64, 0:tn], ACT.Copy)
                    ins = ac.activation(dst[0:64, 2 * j + 1, t0:t0 + tn], src[64:128, 0:tn], ACT.Copy)
                ins.then_inc(g("upe"), 1)
                if u in GELU_AT:
                    c = GELU_AT[u]
                    if c == 0:
                        ac.wait_ge(g("ze"), len(units))
                    ac.activation(gg[:, c, :], gg[:, c, :], ACT.Gelu_apprx_tanh).then_inc(g("gel"), 1)
            for n, (t0, tn) in enumerate(CHUNKS):
                ac.wait_ge(g("lst"), n + 1)
                ac.activation(rnorm2[:, t0:t0 + tn], psum[6 + n][:, 0:tn], ACT.Sqrt, bias=eps, scale=1.0 / LRU).then_inc(g("lrs"), 1)

            def exps(n):
                kn = keys(steps[n][1])[1]
                k = n % 4
                ac.wait_ge(g("mxd"), n + 1)
                if n >= 2:
                    ac.wait_ge(g("pT"), n - 1)
                if n >= 4:
                    ac.wait_ge(g("pve"), n - 3)
                ac.activation(prob[:, n % 2, 0:kn], psum[n % 3][:, 0:kn], ACT.Exp, bias=nm[:, k:k + 1], scale=SCALE,
                              accum_out=rs[:, k:k + 1]).then_inc(g("pr"), 1)

            def pt_out(n):
                kn = keys(steps[n][1])[1]
                ac.wait_ge(g("pT"), n + 1)
                if n >= 2:
                    ac.wait_ge(g("pv"), n - 1)
                ac.activation(probT[:, n % 2, 0:kn], psum[3 + n % 2][:, 0:kn], ACT.Copy).then_inc(g("pTe"), 1)

            def att_squares(i):
                ac.wait_ge(g("pve"), len(steps) - NT + i + 1)
                if i >= 1:
                    ac.wait_ge(g("asq"), i)
                ac.activation(att_junk, att[:, i, :], ACT.Square, accum_out=ssq[:, i:i + 1]).then_inc(g("asq"), 1)
            ac.wait_ge(g("gh"), 8)
            exps(0)
            for n in range(len(steps)):
                if n + 1 < len(steps):
                    exps(n + 1)
                pt_out(n)
                if n - 3 >= len(steps) - NT:
                    att_squares(n - 3 - (len(steps) - NT))
            for i in range(NT - 3, NT):
                att_squares(i)
            ac.wait_ge(g("asq"), NT)
            ac.activation(rstd1, ssq, ACT.Sqrt, bias=eps, scale=1.0 / 512).then_inc(g("asd"), 1)
            for i in range(NT):
                ac.wait_ge(g("x2"), 2 * i + 2)
                link(ac.activation(sqj, x2t[:, i % 2, :], ACT.Square, accum_out=ssq2[:, i:i + 1]))
                ac.activation(rstd2[:, i:i + 1], ssq2[:, i:i + 1], ACT.Sqrt, bias=eps, scale=1.0 / D).then_inc(g("x2s"), 1)
                ac.dma_start(x2_d[i * P:(i + 1) * P, :], x2t[:, i % 2, :]).then_inc(g(f"x2st{i % 2}"), 16)
                ac.wait_ge(g("x2n"), i + 1)
                ac.dma_start(xn_d[i * P:(i + 1) * P, :], xn[:, i % 2, :]).then_inc(g(f"xnst{i % 2}"), 16)
            ac.wait_ge(g("rt_d"), 1)
            ac.activation(g4b, g4b, ACT.Exp).then_inc(g("rt_e"), 1)
            ac.wait_ge(g("rt_d"), 2)
            ac.activation(v6[5], v6[4], ACT.Exp).then_inc(g("rt_e"), 1)
            ac.wait_ge(g("ctl"), 1)
            iters = ac.value_load(ctl[0:1, NBC:NBC + 1], min_val=NE // RING, max_val=ITERS_MAX)
            ac.sem_inc(g("ys0"), 16)
            ac.sem_inc(g("ys1"), 16)
            ac.sem_inc(g("ye"), 2)
            with ac.Fori(0, iters) as i:
                for s in range(RING):
                    b = i * RING + s
                    for f in range(FC):
                        ac.wait_ge(g("gp2") if f == 0 else g("gu"), b + 1)
                        ac.activation(act_t[:, f, :], psum[f][:, 0:WB], ACT.Tanh, scale=0.5).then_inc(g("tnh"), 1)
                    ac.wait_ge(g(f"ys{s % 2}"), (b - s % 2) * 8 + 16)
                    ac.wait_ge(g("dn"), b + 2)
                    for half in range(2):
                        ins = ac.activation(ysb[0:WB, s % 2, half * 512:(half + 1) * 512],
                                            psum[4 + 2 * (s % 2) + half][0:WB, :], ACT.Copy)
                    ins.then_inc(g("ye"), 1)
                    ac.wait_ge(g("ye"), b + 3)
                    ac.dma_start(ys_d[bass.ds(b * WB, WB), :], ysb[0:WB, s % 2, :]).then_inc(g(f"ys{s % 2}"), 16)
            for i in range(NT):
                ac.wait_ge(g("fs"), 2 * i + 2)
                link(ac.activation(fin_junk, fin_x[:, i, :], ACT.Square, accum_out=ssq3[:, i:i + 1]))
                ac.activation(rstd3[:, i:i + 1], ssq3[:, i:i + 1], ACT.Sqrt, bias=eps, scale=1.0 / D).then_inc(g("fq"), 1)

        def bc(a, n):
            return a.unsqueeze(2).to_broadcast([P, a.shape[1], n])

        def bm(a, n):
            return a.unsqueeze(1).to_broadcast([P, n, a.shape[1]])

        def routing(v, link):
            v.wait_ge(g("lg"), NT)
            gl, el = logits[:, :, 0:NG], logits[:, :, NG:NG + NE]
            iota_e = C("iota_e", NE)

            def first_max(src, n, work, top, at, hot):
                io = bm(iota_e[:, 0:n], NT)
                link(v.tensor_reduce(top, src, AX.X, ALU.max))
                link(v.tensor_tensor(work, src, bc(top, n), ALU.is_equal))
                link(v.scalar_tensor_tensor(out=work, in0=work, scalar=-64.0, in1=io, op0=ALU.mult, op1=ALU.add))
                link(v.tensor_reduce(at, work, AX.X, ALU.min))
                link(v.tensor_scalar(at, at, 64.0, None, ALU.add))
                link(v.tensor_tensor(hot, io, bc(at, n), ALU.is_equal))
            first_max(gl, NG, g4, v6[0], v6[1], g4)
            v.tensor_tensor(g4b, gl, bc(v6[0], NG), ALU.subtract).then_inc(g("rt_d"), 1)
            link(v.tensor_tensor(em.rearrange("p i (g e) -> p i g e", g=NG), el.rearrange("p i (g e) -> p i g e", g=NG),
                                 g4.unsqueeze(3).to_broadcast([P, NT, NG, EG]), ALU.mult))
            link(v.tensor_scalar(g4, g4, -1.0, BIG, ALU.add, ALU.mult))
            link(v.tensor_tensor(em.rearrange("p i (g e) -> p i g e", g=NG), em.rearrange("p i (g e) -> p i g e", g=NG),
                                 g4.unsqueeze(3).to_broadcast([P, NT, NG, EG]), ALU.add))
            first_max(em, NE, t1, v6[2], v6[3], E0)
            link(v.scalar_tensor_tensor(out=em, in0=E0, scalar=-2 * BIG, in1=em, op0=ALU.mult, op1=ALU.add))
            first_max(em, NE, t1, v6[6], v6[7], E1)
            v.tensor_tensor(mask, E0, E1, ALU.add).then_inc(g("rt_m"), 1)
            v.tensor_tensor(v6[4], v6[6], v6[2], ALU.subtract).then_inc(g("rt_d"), 1)
            v.wait_ge(g("rt_e"), 2)
            link(v.tensor_reduce(v6[8], g4b, AX.X, ALU.add))
            link(v.tensor_scalar(v6[9], v6[5], 1.0, None, ALU.add))
            link(v.tensor_tensor(v6[9], v6[9], v6[8], ALU.mult))
            link(v.reciprocal(v6[9], v6[9]))
            link(v.tensor_scalar(gate0, v6[9], 0.5, None, ALU.mult))
            link(v.tensor_tensor(gate1, gate0, v6[5], ALU.mult))
            r, q, ovs, at, blk, sel, place, pos = v12
            v.wait_ge(g("rt_p"), 1)
            link(v.tensor_copy(rank.rearrange("p i e -> p (i e)"), psum[1][:, 0:NT * NE]))
            link(v.tensor_copy(cnt, psum[2][:, 0:NE]))
            for k, E in enumerate((E0, E1)):
                link(v.tensor_tensor(t1, E, rank, ALU.mult))
                link(v.tensor_reduce(r[:, k * NT:(k + 1) * NT], t1, AX.X, ALU.add))
            thr_m = C("thr", MAXQ)
            link(v.tensor_tensor(q9, bc(r, MAXQ), bm(thr_m, 2 * NT), ALU.is_ge))
            link(v.tensor_reduce(q, q9, AX.X, ALU.add))
            link(v.tensor_tensor(q9e, bc(cnt, MAXQ), bm(thr_m, NE), ALU.is_gt))
            link(v.tensor_reduce(ovf, q9e, AX.X, ALU.add))
            link(v.tensor_tensor_scan(off_end, ones[:, 0:NE], ovf, 0.0, ALU.mult, ALU.add))
            link(v.tensor_tensor(off, off_end, ovf, ALU.subtract))
            for k, (E, a) in enumerate(((E0, v6[3]), (E1, v6[7]))):
                link(v.tensor_tensor(t1, E, bm(off, NT), ALU.mult))
                link(v.tensor_reduce(ovs[:, k * NT:(k + 1) * NT], t1, AX.X, ALU.add))
                link(v.tensor_copy(at[:, k * NT:(k + 1) * NT], a))
            link(v.tensor_tensor(ovs, ovs, q, ALU.add))
            link(v.scalar_tensor_tensor(out=blk, in0=ovs, scalar=float(NE - 1), in1=at, op0=ALU.add, op1=ALU.subtract))
            link(v.tensor_scalar(sel, q, 0.5, None, ALU.is_gt))
            link(v.tensor_tensor(blk, blk, sel, ALU.mult))
            link(v.tensor_tensor(blk, blk, at, ALU.add))
            link(v.scalar_tensor_tensor(out=place, in0=q, scalar=-float(WB), in1=r, op0=ALU.mult, op1=ALU.add))
            link(v.tensor_tensor(oh_w, bc(place, WB), bm(C("iota_w", WB), 2 * NT), ALU.is_equal))
            link(v.tensor_tensor(oh_b, bc(blk, NBC), bm(C("iota_b", NBC), 2 * NT), ALU.is_equal))
            for k in range(2):
                part = oh_b[:, k * NT:(k + 1) * NT, :]
                ins = v.tensor_tensor(part, part, bc(C("tokid", NT), NBC), ALU.mult)
            ins.then_inc(g("rt_a"), 1)
            link(v.tensor_tensor(xe, bc(C("iota_x", EXTRA), NE), bm(off, EXTRA), ALU.is_ge))
            link(v.tensor_tensor(xe2, bc(C("iota_x", EXTRA), NE), bm(off_end, EXTRA), ALU.is_lt))
            link(v.tensor_tensor(xe, xe, xe2, ALU.mult))
            link(v.tensor_tensor(xe, xe, bm(iota_e, EXTRA), ALU.mult))
            link(v.tensor_reduce(ctlf[:, NE:NBC], xe, AX.X, ALU.add))
            link(v.tensor_copy(ctlf[:, 0:NE], iota_e))
            link(v.tensor_scalar(itt, C("iter_thr", ITERS_MAX), off_end[:, NE - 1:NE], None, ALU.is_lt))
            link(v.tensor_reduce(ctlf[:, NBC:NBC + 1], itt, AX.X, ALU.add))
            link(v.tensor_scalar(ctlf[:, NBC:NBC + 1], ctlf[:, NBC:NBC + 1], float(NE // RING), None, ALU.add))
            v.tensor_copy(ctl[0:1, 0:NBC + 1], ctlf[0:1, :]).then_inc(g("ctl"), 1)
            link(v.scalar_tensor_tensor(out=pos, in0=blk, scalar=float(WB), in1=place, op0=ALU.mult, op1=ALU.add))
            link(v.tensor_copy(pos_i[:], pos))
            v.wait_ge(g("rt_ap"), 1)
            v.tensor_copy(idx[:], psum[3][0:WB, 0:NBC]).then_inc(g("idx"), 1)

        @block.vector
        def _(v):
            chain = [0]

            def link(ins):
                chain[0] += 1
                ins.then_inc(g("dch"), 1)
                v.wait_ge(g("dch"), chain[0])
            v.wait_ge(g("cols"), 16)
            lam = cols[:, COLS["lam"]:COLS["lam"] + 8]
            link(v.tensor_scalar(lam_t[:, 4, :], lam, -1.0, None, ALU.mult))
            link(v.tensor_tensor(lam_t[:, 0, :], lam_t[:, 4, :], lam, ALU.max))
            link(v.tensor_scalar(hb_r, cols[:, COLS["b_rg"]:COLS["b_rg"] + 8], 0.5, None, ALU.mult))
            v.tensor_scalar(hb_i, cols[:, COLS["b_ig"]:COLS["b_ig"] + 8], 0.5, None, ALU.mult).then_inc(g("lam"), 1)
            for i in range(NT):
                v.wait_ge(g("sd"), i + 1)
                link(v.reciprocal(rstd1[:, i:i + 1], rstd1[:, i:i + 1]))
                if i >= 2:
                    v.wait_ge(g("uTp"), 2 * (i - 1))
                v.tensor_scalar(un[:, i % 2, :].rearrange("t (c p) -> t p c", c=DC),
                                xin[:, i % 2, :].rearrange("t (p c) -> t p c", c=DC),
                                rstd1[:, i:i + 1], None, ALU.mult).then_inc(g("un"), 1)
                for j in range(2):
                    v.wait_ge(g("uTp"), 2 * i + j + 1)
                    n1 = cols[:, COLS["norm1"] + 4 * j:COLS["norm1"] + 4 * j + 4].unsqueeze(2).to_broadcast([P, 4, P])
                    v.tensor_tensor(uT[:, 4 * j:4 * j + 4, i * P:(i + 1) * P],
                                    psum[4 + j][:, :].rearrange("p (c t) -> p c t", c=4), n1, ALU.mult).then_inc(g("uT"), 1)
            v.wait_ge(g("lamA"), 1)
            v.tensor_scalar(lam_t[:, 2, :], lam_t[:, 1, :], 1.0, None, ALU.add).then_inc(g("lam"), 1)
            v.wait_ge(g("lam"), 2)
            v.wait_ge(g("lamA"), 2)
            link(v.tensor_scalar(lam_t[:, 5, :], lam_t[:, 2, :], 1.0, None, ALU.is_equal))
            link(v.tensor_tensor(lam_t[:, 3, :], lam_t[:, 3, :], lam_t[:, 5, :], ALU.add))
            link(v.tensor_tensor(lam_t[:, 3, :], lam_t[:, 3, :], lam_t[:, 1, :], ALU.mult))
            link(v.scalar_tensor_tensor(out=lam_t[:, 5, :], in0=lam_t[:, 2, :], scalar=-1.0, in1=lam_t[:, 5, :],
                                        op0=ALU.add, op1=ALU.add))
            link(v.reciprocal(lam_t[:, 5, :], lam_t[:, 5, :]))
            link(v.tensor_tensor(lam_t[:, 3, :], lam_t[:, 3, :], lam_t[:, 5, :], ALU.mult))
            link(v.scalar_tensor_tensor(out=lam_t[:, 3, :], in0=lam_t[:, 4, :], scalar=0.0, in1=lam_t[:, 3, :],
                                        op0=ALU.max, op1=ALU.add))
            link(v.tensor_scalar(lamc, lam_t[:, 3, :], -4.0, None, ALU.mult))
            link(v.tensor_scalar(nlamc, lam_t[:, 3, :], 4.0, None, ALU.mult))
            v.tensor_scalar(lam2[:], lam_t[:, 3, :], -8.0, None, ALU.mult).then_inc(g("lam"), 2)

            def conv(c):
                n = XPAD - 3
                v.wait_ge(g("ze"), LC + c + 1)
                v.wait_ge(g("pads"), 1)
                if c >= 2:
                    v.wait_ge(g("gp"), 2 * c - 2)
                wcol = lambda t: col("conv_w", t * LC + c)
                link(v.tensor_scalar(xc[:, c % 2, 0:n], xb[:, c, 0:n], wcol(0), col("conv_b", c), ALU.mult, ALU.add))
                for t in range(1, 4):
                    ins = v.scalar_tensor_tensor(out=xc[:, c % 2, 0:n], in0=xb[:, c, t:t + n], scalar=wcol(t),
                                                 in1=xc[:, c % 2, 0:n], op0=ALU.mult, op1=ALU.add)
                    if t < 3:
                        link(ins)
                ins.then_inc(g("conv"), 1)

            def unit_m(u):
                c = u // 2
                th_r, th_i, dec, dec2 = temps[u % 2]
                v.wait_ge(g("gx"), 3 * u + 3)
                v.scalar_tensor_tensor(out=dec2, in0=dec2, scalar=1.0, in1=th_r, op0=ALU.add, op1=ALU.mult).then_inc(g("gm"), 1)
                for n, (t0, tn) in enumerate(CHUNKS):
                    ins = v.scalar_tensor_tensor(out=th_i[:, t0:t0 + tn], in0=th_i[:, t0:t0 + tn], scalar=1.0,
                                                 in1=xc[:, c % 2, XOFF[n]:XOFF[n] + tn], op0=ALU.add, op1=ALU.mult)
                ins.then_inc(g("gm"), 1)

            def unit_s(u):
                c, d = u // 2, u % 2
                th_r, th_i, dec, dec2 = temps[d]
                v.wait_ge(g("gs"), u + 1)
                v.wait_ge(g("gm"), 2 * u + 2)
                link(v.tensor_tensor(th_i, th_i, dec2, ALU.mult))
                h_fwd = xb[:, c, 0:TOK]
                for n, (t0, tn) in enumerate(CHUNKS):
                    if d == 0:
                        ins = v.tensor_tensor_scan(h_fwd[:, t0:t0 + tn], dec[:, t0:t0 + tn], th_i[:, t0:t0 + tn], 0.0,
                                                   ALU.mult, ALU.add)
                    else:
                        ins = v.tensor_tensor_scan(th_r[:, t0:t0 + tn][:, ::-1], dec[:, t0:t0 + tn][:, ::-1],
                                                   th_i[:, t0:t0 + tn][:, ::-1], 0.0, ALU.mult, ALU.add)
                    if d == 1 or n == 0:
                        link(ins)
                if d == 0:
                    ins.then_inc(g("gh"), 1)
                else:
                    v.wait_ge(g("gh"), u)
                    v.tensor_tensor(h_fwd, h_fwd, th_r, ALU.add).then_inc(g("gh"), 1)

            def pair(c):
                unit_m(2 * c)
                unit_m(2 * c + 1)
                unit_s(2 * c)
                unit_s(2 * c + 1)
            conv(0)
            conv(1)
            pair(0)
            conv(2)
            pair(1)
            conv(3)
            pair(2)
            v.wait_ge(g("zp"), U_G)
            for k in range(4):
                a, n = k // 2, k % 2
                t0, tn = CHUNKS[n]
                v.wait_ge(g("statp"), k + 1)
                v.tensor_scalar(rn[:, a, t0:t0 + tn], psum[4][:, 0:tn], 1.0 / (QL, KVL)[a], EPS, ALU.mult,
                                ALU.add).then_inc(g("stc"), 1)
                if k == 1:
                    unit_m(6)
            unit_m(7)
            v.wait_ge(g("rqs"), 1)
            for a in range(2):
                link(v.reciprocal(rn[:, a, :], rn[:, a, :]))
                for c in range(QC) if a == 0 else range(QC, QC + KVC):
                    gain = col("q_norm", c) if a == 0 else col("kv_norm", c - QC)
                    v.scalar_tensor_tensor(out=zl[:, c, :], in0=zl[:, c, :], scalar=gain, in1=rn[:, a, :],
                                           op0=ALU.mult, op1=ALU.mult).then_inc(g("zn"), 1)
            swap = list(range(16, 32)) + list(range(0, 16))
            v.wait_ge(g("rope"), 16)
            link(v.stream_shuffle(krs, kr[0:RP, :], swap))
            link(v.tensor_tensor(krs, krs, rope[0:RP, 1, :], ALU.mult))
            link(v.tensor_tensor(kr[0:RP, :], kr[0:RP, :], rope[0:RP, 0, :], ALU.mult))
            v.tensor_tensor(kT[64:96, 0, :], kr[0:RP, :], krs, ALU.add).then_inc(g("ropek"), 1)
            unit_s(6)
            unit_s(7)
            v.wait_ge(g("upe"), 4)
            for r in range(2):
                link(v.stream_shuffle(qs[:, r, :], qr[:, r, :], swap))
                link(v.tensor_tensor(qs[:, r, :], qs[:, r, :], rope[:, 1, :], ALU.mult))
                link(v.tensor_tensor(qr[:, r, :], qr[:, r, :], rope[:, 0, :], ALU.mult))
                for j in range(4):
                    v.tensor_tensor(qT[64:96, 4 * r + j, :], qr[32 * j:32 * j + 32, r, :], qs[32 * j:32 * j + 32, r, :],
                                    ALU.add).then_inc(g("ropeq"), 1)

            def maxes(n):
                kn = keys(steps[n][1])[1]
                k = n % 4
                v.wait_ge(g("sc"), n + 1)
                if n >= 4:
                    v.wait_ge(g("pr"), n - 3)
                link(v.tensor_reduce(mx[:, k:k + 1], psum[n % 3][:, 0:kn], AX.X, ALU.max))
                v.tensor_scalar(nm[:, k:k + 1], mx[:, k:k + 1], -SCALE, None, ALU.mult).then_inc(g("mxd"), 1)

            def att_out(n):
                h, i = steps[n]
                k = n % 4
                v.wait_ge(g("pr"), n + 1)
                link(v.reciprocal(rr[:, k:k + 1], rs[:, k:k + 1]))
                v.wait_ge(g("pv"), n + 1)
                v.tensor_scalar(att[:, i, h * VH:(h + 1) * VH], psum[5][:, 0:VH], rr[:, k:k + 1], None,
                                ALU.mult).then_inc(g("pve"), 1)

            def attT_out(i):
                v.wait_ge(g("atp"), i + 1)
                v.tensor_tensor(attT[:, :, i * P:(i + 1) * P], psum[6 + i % 2][:, :].rearrange("p (c t) -> p c t", c=LC),
                                att_gain, ALU.mult).then_inc(g("atT"), 1)
            att_gain = cols[:, COLS["att_norm"]:COLS["att_norm"] + LC].unsqueeze(2).to_broadcast([P, LC, P])
            maxes(0)
            maxes(1)
            for n in range(len(steps)):
                if n + 2 < len(steps):
                    maxes(n + 2)
                if n >= 1:
                    att_out(n - 1)
                if n == 2:
                    v.wait_ge(g("lrs"), 2)
                    link(v.reciprocal(rnorm2, rnorm2))
                if 3 <= n < 3 + LC:
                    c = n - 3
                    v.wait_ge(g("lsq"), LC)
                    v.scalar_tensor_tensor(out=gg[:, c, :], in0=gg[:, c, :], scalar=col("lru_norm", c), in1=rnorm2,
                                           op0=ALU.mult, op1=ALU.mult).then_inc(g("ln"), 1)
                if n - 4 >= len(steps) - NT:
                    attT_out(n - 4 - (len(steps) - NT))
            att_out(len(steps) - 1)
            for i in range(NT - 4, NT):
                attT_out(i)
            v.wait_ge(g("asd"), 1)
            link(v.reciprocal(rstd1, rstd1))
            v.wait_ge(g("rows"), 32)

            def logits_out(i):
                v.wait_ge(g("lgp"), i + 1)
                v.tensor_tensor(logits[:, i, :], psum[0][:, 0:NG + NE], brt[:], ALU.add).then_inc(g("lg"), 1)

            def tt_out(i):
                for j in range(2):
                    v.wait_ge(g("ttp"), 2 * i + j + 1)
                    if i >= 1:
                        v.wait_ge(g("lgp"), i)
                    v.tensor_copy(tT[:, 4 * j:4 * j + 4, :], psum[6 + j][:, :].rearrange("p (c t) -> p c t", c=4)).then_inc(g("tt"), 1)
            for i in range(NT):
                v.wait_ge(g(f"xr{i % 2}"), 16 * (i // 2 + 1))
                for half in range(2):
                    part = x2t[:, i % 2, half * 512:(half + 1) * 512]
                    v.wait_ge(g("op"), 2 * i + half + 1)
                    link(v.tensor_tensor(part, psum[2 + 2 * half][:, :], part, ALU.add))
                    v.scalar_tensor_tensor(out=part, in0=psum[3 + 2 * half][:, :], scalar=rstd1[:, i:i + 1], in1=part,
                                           op0=ALU.mult, op1=ALU.add).then_inc(g("x2"), 1)
                v.wait_ge(g("x2s"), i + 1)
                link(v.reciprocal(rstd2[:, i:i + 1], rstd2[:, i:i + 1]))
                if i >= 2:
                    v.wait_ge(g(f"xnst{i % 2}"), 16 * (i // 2))
                    v.wait_ge(g("ttp"), 2 * (i - 1))
                v.scalar_tensor_tensor(out=xn[:, i % 2, :].rearrange("t (c p) -> t p c", c=DC),
                                       in0=x2t[:, i % 2, :].rearrange("t (p c) -> t p c", c=DC), scalar=rstd2[:, i:i + 1],
                                       in1=n2row[:].rearrange("t (p c) -> t p c", c=DC),
                                       op0=ALU.mult, op1=ALU.mult).then_inc(g("x2n"), 1)
                tt_out(i)
                logits_out(i)
            routing(v, link)
            v.wait_ge(g("idx"), 1)
            v.wait_ge(g("ctl"), 1)
            iters = v.value_load(ctl[0:1, NBC:NBC + 1], min_val=NE // RING, max_val=ITERS_MAX)

            def rows_out(par, b, first=False):
                v.wait_ge(g("xgp"), 2 if first else b + 2)
                for j in range(2):
                    v.tensor_copy(xT[:, par, 4 * j:4 * j + 4, :],
                                  psum[2 + j][:, 0:4 * WB].rearrange("p (c n) -> p c n", c=4)).then_inc(g("xT"), 1)
            v.sem_inc(g("hh"), FC)
            rows_out(0, 0, True)
            with v.Fori(0, iters) as i:
                for s in range(RING):
                    b = i * RING + s
                    for f in range(FC):
                        v.wait_ge(g("tnh"), b * FC + f + 1)
                        v.scalar_tensor_tensor(out=act_s[:, f, :], in0=act_t[:, f, :], scalar=1.0, in1=psum[f][:, 0:WB],
                                               op0=ALU.add, op1=ALU.mult).then_inc(g("acs"), 1)
                        v.wait_ge(g("acs"), b * FC + f + 1)
                        v.wait_ge(g("dn"), b + 1)
                        v.tensor_tensor(hT[:, f, :], act_s[:, f, :], psum[f][:, WB:2 * WB], ALU.mult).then_inc(g("hh"), 1)
                    rows_out((s + 1) % 2, b + 1)
            v.wait_ge(g("frow"), 16)
            v.wait_ge(g("fx0"), 16 * NT)
            for i in range(NT):
                for k, gt in enumerate((gate0, gate1)):
                    v.wait_ge(s_fy[2 * i + k], 16)
                    v.scalar_tensor_tensor(out=fin_x[:, i, :], in0=fin_y[:, k, i, :], scalar=gt[:, i:i + 1],
                                           in1=fin_x[:, i, :], op0=ALU.mult, op1=ALU.add).then_inc(g("fs"), 1)
                    v.wait_ge(g("fs"), 2 * i + k + 1)
                v.wait_ge(g("fq"), i + 1)
                link(v.reciprocal(rstd3[:, i:i + 1], rstd3[:, i:i + 1]))
                v.scalar_tensor_tensor(out=fin_x[:, i, :], in0=fin_x[:, i, :], scalar=rstd3[:, i:i + 1], in1=fin_row,
                                       op0=ALU.mult, op1=ALU.mult).then_inc(g("fo"), 1)


def kernel(**inputs):
    import numpy as np
    import concourse.bacc as bacc
    from concourse.bass_utils import run_bass_kernel_spmd as run

    a = {k: np.asarray(v) for k, v in inputs.items()}

    def feat(v, inner):
        return v.reshape(P, -1) if inner else v.reshape(-1, P).T
    cols = np.concatenate([feat(a["norm1"][0], True), feat(a["q_norm"][0], False), feat(a["kv_norm"][0], False)] +
                          [feat(a["conv_w"][0].reshape(-1), False), feat(a["conv_b"][0], False),
                           feat(a["b_rg"][0].reshape(-1), False), feat(a["b_ig"][0].reshape(-1), False),
                           feat(a["lru_lambda"][0].reshape(-1), False), feat(a["att_out_norm"][0], False),
                           feat(a["lru_out_norm"][0], False)], axis=1)
    c = np.zeros((P, NCONSTS), np.float32)

    def put(name, v):
        v = np.asarray(v, np.float32)
        c[:, CONSTS[name]:CONSTS[name] + v.shape[-1]] = v
    put("ident", np.eye(P))
    put("before", np.triu(np.ones((P, P)), 1))
    put("ones", np.ones((P, P)))
    put("iota_w", np.arange(WB)[None])
    put("iota_b", np.arange(NBC)[None])
    put("iota_e", np.arange(NE)[None])
    put("thr", WB * (1 + np.arange(MAXQ))[None])
    put("tokid", np.arange(TOK).reshape(NT, P).T)
    put("eps", np.full((1, 1), EPS))
    put("iota_x", np.arange(EXTRA)[None])
    put("iter_thr", RING * np.arange(ITERS_MAX)[None])
    inv = 1.0 / (np.float32(10000.0) ** (np.arange(0, RP, 2, dtype=np.float32) / np.float32(RP)))
    at = np.concatenate([np.arange(n, dtype=np.float32) for _, n in CHUNKS])
    ang = (at[None, :] * inv[:, None].astype(np.float32)).astype(np.float32)
    cos, sin = np.cos(ang), np.sin(ang)
    rope = np.concatenate([np.tile(np.concatenate([cos, cos]), (4, 1)), np.tile(np.concatenate([-sin, sin]), (4, 1))], axis=1)
    rows = np.zeros((3, D), np.float32)
    rows[0] = a["norm2"][0]
    rows[1] = a["final_norm"]
    rows[2, :NG] = a["b_group"][0]
    rows[2, NG:NG + NE] = a["b_router"][0]
    wq = a["w_q_up"][0].reshape(QL, NH, NOPE + RP)
    wkv = a["w_kv_up"][0].reshape(KVL, NH, NOPE + VH)
    ins = {
        "x": np.concatenate([a["x_prompt"].reshape(-1, D), a["x_sample"].reshape(-1, D)]),
        "cols": cols, "consts": c, "rope_t": rope, "rows": rows, "w_in": a["w_in"][0],
        "w_q": np.concatenate([wq[..., :NOPE].reshape(QL, -1), wq[..., NOPE:].reshape(QL, -1)], axis=1),
        "w_kv": np.concatenate([wkv[..., :NOPE].reshape(KVL, -1), wkv[..., NOPE:].reshape(KVL, -1)], axis=1),
        "w_rg": a["w_rg"][0], "w_ig": a["w_ig"][0], "w_out": a["w_out"][0],
        "w_router": np.concatenate([a["w_group"][0], a["w_router"][0]], axis=1),
        "w_gate": a["w_gate"][0], "w_up": a["w_up"][0], "w_down": a["w_down"][0],
    }
    nc = bacc.Bacc("TRN2", target_bir_lowering=False, num_devices=1)
    arrays, args = {}, []
    for name, v in ins.items():
        v = np.ascontiguousarray(v)
        arrays[f"in_{name}"] = v
        args.append(nc.dram_tensor(f"in_{name}", v.shape, mybir.dt.from_np(v.dtype), kind="ExternalInput").ap())
    for i, n in enumerate((PROMPT, TOK - PROMPT)):
        args.append(nc.dram_tensor(f"out_{i}", (1, n, D), mybir.dt.float32, kind="ExternalOutput").ap())
    encoder_layer(nc, *args)
    r = run(nc, [arrays], core_ids=[0])
    return tuple(r.results[0][f"out_{i}"] for i in range(2))
```

```python
import concourse.bass as bass
from concourse import mybir
from contextlib import ExitStack

P = 128
TOK, PROMPT = 768, 256
NT = TOK // P
D = 1024
DC = D // P
QL, KVL, RP, LRU = 384, 256, 32, 512
NH, NOPE, VH = 8, 64, 64
LC = LRU // P
QC, KVC = QL // P, KVL // P
CHUNKS = ((0, PROMPT), (PROMPT, TOK - PROMPT))
XPAD = (PROMPT + 3) + (TOK - PROMPT + 3)
XOFF = (0, PROMPT + 3)
NE, NG, EG, F = 32, 4, 8, 256
FC = F // P
WB = 100
RING = 6
MAXQ = (TOK - 1) // WB
MAXB = NE + (2 * TOK) // WB
ROUNDS = -(-MAXB // RING)
NBC = RING * ROUNDS + 1
EXTRA = NBC - NE
EPS = 1e-6
SCALE = float(NOPE + RP) ** -0.5
BIG = 1e30
LOW = 64

COLS = {}
_at = 0
for _n, _w in (("norm1", DC), ("q_norm", QC), ("kv_norm", KVC), ("conv_w", 4 * LC), ("conv_b", LC),
               ("b_rg", 2 * LC), ("b_ig", 2 * LC), ("lam", 2 * LC), ("att_norm", LC), ("lru_norm", LC)):
    COLS[_n] = _at
    _at += _w
NCOLS = _at
CONSTS = {}
_at = 0
for _n, _w in (("ident", P), ("before", P), ("ones", P), ("iota_w", WB), ("iota_b", NBC), ("iota_m", NE),
               ("thr", MAXQ), ("tokid", NT), ("eps", 1), ("iota_x", EXTRA), ("round_thr", ROUNDS - 1), ("evens", EXTRA // 2)):
    CONSTS[_n] = _at
    _at += _w
NCONSTS = _at


def encoder_layer(nc, A_x, A_cols, A_consts, A_rope, A_rows, A_win, A_wq, A_wkv, A_wrg, A_wig, A_wout,
                  A_wrt, A_wgate, A_wup, A_wdown, y_prompt, y_sample):
    f32, f32r, i32 = mybir.dt.float32, mybir.dt.float32r, mybir.dt.int32
    ALU = mybir.AluOpType
    ACT = mybir.ActivationFunctionType
    AX = mybir.AxisListType
    ctx = ExitStack()
    with ctx:
        def sb(name, shape, dt=f32):
            return ctx.enter_context(nc.sbuf_tensor(name, shape, dt))

        def sem(name):
            return ctx.enter_context(nc.semaphore(name))

        SLOT = 3 * DC * F
        MIX_SLOTS = 2
        W_RING = 4
        with ExitStack() as early:
            u_high, u_low, w_high, w_low = (early.enter_context(nc.sbuf_tensor(name, [P, n], f32r)) for name, n in (
                ("u_high", DC * TOK), ("u_low", DC * TOK), ("w_high", W_RING * DC * P), ("w_low", W_RING * DC * P)))
        with ExitStack() as late:
            ring_parts = late.enter_context(nc.sbuf_tensor("ring_parts", [P, (RING - MIX_SLOTS) * SLOT], f32r))
        ring = sb("ring", [P, (RING - MIX_SLOTS) * SLOT])
        SPLIT = 2 * DC * TOK + 2 * W_RING * DC * P
        LOWRANK, UPW, GG = (QC + KVC) * TOK, QC * TOK + KVC * D, LC * TOK
        with ExitStack() as late:
            mix_parts = late.enter_context(nc.sbuf_tensor("mix_parts", [P, LOWRANK + UPW + GG + 4 * LC * P], f32r))
        mix = sb("mix", [P, LOWRANK + UPW + GG + 4 * LC * P])
        lowrank = mix[:, 0:LOWRANK]
        upw = mix[:, LOWRANK:LOWRANK + UPW]
        gg = mix[:, LOWRANK + UPW:LOWRANK + UPW + GG].rearrange("p (c t) -> p c t", c=LC)
        gatew = mix[:, LOWRANK + UPW + GG:].rearrange("p (t d c o) -> p t d c o", t=2, d=2, c=LC)
        xb = sb("xb", [P, LC, XPAD])
        softm = sb("softm", [P, 2048])
        rope = sb("rope", [P, 2, TOK])
        consts = sb("consts", [P, NCONSTS])
        cols = sb("cols", [P, NCOLS])
        norm_row = sb("norm_row", [P, D])
        tmp = sb("tmp", [P, 6144])
        wrt = sb("wrt", [P, DC, NG + NE])
        brt = sb("brt", [P, NG + NE])
        small = sb("small", [P, 160])
        idx = sb("idx", [WB, NBC], i32)
        idx_now = sb("idx_now", [WB, RING], i32)
        pos_i = sb("pos_i", [P, 2 * NT], i32)
        C_FULL, C_REST, C_BLOCKS, C_YS0, C_YS1 = (NBC + k for k in range(5))
        ctl = sb("ctl", [1, NBC + 5], i32)
        psum = [ctx.enter_context(nc.psum_tensor(f"bank{b}", [P, 512], f32)) for b in range(8)]
        x2_d = nc.dram_tensor("x2_rows", [TOK, D], f32, kind="Internal").ap()
        xn_d = nc.dram_tensor("xn_rows", [TOK, D], f32, kind="Internal").ap()
        ys_d = nc.dram_tensor("expert_rows", [NBC * WB, D], f32, kind="Internal").ap()

        def C(name, n=None, p0=0, p1=P):
            a = CONSTS[name]
            return consts[p0:p1, a:a + (n or 1)]

        def slot_at(k):
            return ring[:, k * SLOT:(k + 1) * SLOT] if k < RING - MIX_SLOTS else \
                mix[:, (k - RING + MIX_SLOTS) * SLOT:(k - RING + MIX_SLOTS + 1) * SLOT]

        ident, before, ones = C("ident", P), C("before", P), C("ones", P)

        def col(name, j, p0=0, p1=P):
            a = COLS[name] + j
            return cols[p0:p1, a:a + 1]

        logits = rope[:, 0, 0:NT * (NG + NE)].rearrange("p (i n) -> p i n", i=NT)
        uh, ul = (u[:, :].rearrange("p (c t) -> p c t", c=DC) for u in (u_high, u_low))
        wh, wl = (w[:, :].rearrange("p (s c m) -> p s c m", s=W_RING, c=DC) for w in (w_high, w_low))
        w_raw = ring[:, SPLIT:SPLIT + 2 * DC * P].rearrange("p (b c m) -> p b c m", b=2, c=DC)
        qT = ring[:, 0:NH * TOK].rearrange("p (h t) -> p h t", h=NH)
        kT = ring[:, SLOT:SLOT + NH * TOK].rearrange("p (h t) -> p h t", h=NH)
        wout = ring[:, 2 * SLOT:2 * SLOT + DC * D].rearrange("p (c n) -> p c n", c=DC)
        V = ring[:, 3 * SLOT + 3072:4 * SLOT].rearrange("p (i n) -> p i n", i=NT)
        zl = lowrank[:, :].rearrange("p (c t) -> p c t", c=QC + KVC)
        att = lowrank[:, 0:NT * 512].rearrange("p (i n) -> p i n", i=NT)
        wq = upw[:, 0:QC * TOK].rearrange("p (c n) -> p c n", c=QC)
        wkv = upw[:, QC * TOK:].rearrange("p (c n) -> p c n", c=KVC)
        W_HIGH = [(part + j * D, ((j + 1) * D - 1) // TOK) for part, j in
                  ((0, 0), (0, 1), (0, 3), (0, 4), (SLOT, 0), (SLOT, 1), (SLOT, 2), (0, 2))]
        wo_high = [ring_parts[:, at:at + D] for at, _ in W_HIGH]
        wo_low = [ring_parts[:, 2 * SLOT + j * D:2 * SLOT + (j + 1) * D] for j in range(DC)]
        gg_high = [ring_parts[:, SLOT + (LC + c) * TOK:SLOT + (LC + c + 1) * TOK] for c in range(LC)]
        gg_low = [mix_parts[:, LOWRANK + UPW + c * TOK:LOWRANK + UPW + (c + 1) * TOK] for c in range(LC)]
        at_high = mix_parts[:, LOWRANK:LOWRANK + LC * TOK].rearrange("p (c t) -> p c t", c=LC)
        at_low = [part[:, at:at + TOK] for part, at in (
            (mix_parts, LOWRANK + LC * TOK), (mix_parts, LC * TOK), (mix_parts, LOWRANK + UPW + GG), (ring_parts, 5 * D))]
        prob = softm[:, 0:1024].rearrange("p (b n) -> p b n", b=2)
        probT = softm[:, 1024:2048].rearrange("p (b n) -> p b n", b=2)
        xin = tmp[:, 0:2 * D].rearrange("p (b n) -> p b n", b=2)
        un = tmp[:, 2 * D:4 * D].rearrange("p (b n) -> p b n", b=2)
        junk = tmp[:, 4 * D:5 * D]
        sqz = upw[:, 0:(QC + KVC) * TOK].rearrange("p (c t) -> p c t", c=QC + KVC)
        rn = ring[:, SPLIT + 2 * DC * P:SPLIT + 2 * DC * P + 2 * TOK].rearrange("p (a t) -> p a t", a=2)
        kr = norm_row[:, 0:TOK]
        krs = ring[0:RP, SPLIT:SPLIT + TOK]
        qr = ring[:, 2 * SLOT:2 * SLOT + 2 * TOK].rearrange("p (r t) -> p r t", r=2)
        qs = ring[:, 2 * SLOT + 2 * TOK:2 * SLOT + 4 * TOK].rearrange("p (r t) -> p r t", r=2)
        xc = softm[:, 0:2 * (XPAD - 3)].rearrange("p (b n) -> p b n", b=2)
        temps = [[tmp[:, (4 * k + m) * TOK:(4 * k + m + 1) * TOK] for m in range(4)] for k in range(2)]
        rnorm2 = tmp[:, 5 * D:5 * D + TOK]
        att_junk = tmp[:, 4 * D:4 * D + 512]
        rstd1 = small[:, 0:NT]
        ssq = small[:, 8:8 + NT]
        lamc = small[:, 16:24]
        nlamc = small[:, 24:32]
        lam_t = small[:, 32:80].rearrange("p (k n) -> p k n", k=6)
        hb_r = small[:, 80:88]
        hb_i = small[:, 88:96]
        mx, nm, rs, rr = (small[:, 32 + 4 * k:36 + 4 * k] for k in range(4))
        ssq2 = small[:, 104:104 + NT]
        rstd2 = small[:, 112:112 + NT]
        gate0 = small[:, 120:120 + NT]
        gate1 = small[:, 128:128 + NT]
        ssq3 = small[:, 136:136 + NT]
        rstd3 = small[:, 144:144 + NT]

        xn = tmp[:, 2 * D:4 * D].rearrange("p (b n) -> p b n", b=2)
        x2t = tmp[:, 0:2 * D].rearrange("p (b n) -> p b n", b=2)
        tT = tmp[:, 4 * D:5 * D].rearrange("p (c t) -> p c t", c=DC)
        flat = xb[:].rearrange("p c n -> p (c n)")
        E = flat[:, 0:2 * NT * NE].rearrange("p (i k e) -> p i k e", i=NT, k=2)
        Ek = flat[:, 0:2 * NT * NE].rearrange("p (k e) -> p k e", e=NE)
        mask = flat[:, 384:576].rearrange("p (i e) -> p i e", i=NT)
        seen = flat[:, 576:768].rearrange("p (i e) -> p i e", i=NT)
        em = flat[:, 768:800]
        t1 = flat[:, 800:832]
        t2 = flat[:, 832:896].rearrange("p (k e) -> p k e", k=2)
        t12 = flat[:, 896:1280].rearrange("p (k e) -> p k e", e=NE)
        g4 = flat[:, 1280:1284]
        g4b = flat[:, 1284:1308].rearrange("p (i n) -> p i n", i=NT)
        gat = flat[:, 1308:1309]
        gtop, e0top, e1top, ediff, egap, gsum, den = (flat[:, 1312 + 8 * k:1312 + 8 * k + NT] for k in range(7))
        at, r, q, place, ovs, sel, blk, pos = (flat[:, 1376 + 12 * k:1376 + 12 * (k + 1)] for k in range(8))
        ovf, off, off_end = (flat[:, 1472 + NE * k:1472 + NE * (k + 1)] for k in range(3))
        xe = flat[:, 1600:1600 + EXTRA * NE].rearrange("p (x e) -> p x e", e=NE)
        q9 = softm[:, 1520:1520 + 2 * MAXQ].rearrange("p (k m) -> p k m", m=MAXQ)
        q9e = softm[:, 1680:1680 + NE * MAXQ].rearrange("p (e m) -> p e m", m=MAXQ)
        marks = rope[:, 1, 700:700 + EXTRA]
        ctlf = rope[:, 1, 600:600 + NBC + 5]
        oh_w = [(tmp[:, 5 * D + k * WB:5 * D + (k + 1) * WB] if k < NT else
                 mix[:, MIX_SLOTS * SLOT + (k - NT) * WB:MIX_SLOTS * SLOT + (k - NT + 1) * WB]) for k in range(2 * NT)]
        oh_b = flat[:, 2348:2348 + 2 * NT * NBC].rearrange("p (k w) -> p k w", k=2 * NT)
        zeros = norm_row[:, 0:D]
        sqj = softm[:, 0:D]
        lam2 = small[:, 152:160]
        ahead = small[:, 126:127]
        fin_x = [xb[:].rearrange("p c n -> p (c n)")[:, i * D:(i + 1) * D] for i in range(3)] + \
                [softm[:, i * D:(i + 1) * D] for i in range(2)] + [norm_row[:, 0:D]]
        fin_row = mix[:, MIX_SLOTS * SLOT:MIX_SLOTS * SLOT + D]
        FIN_BANKS = 4
        diag = rope[:, 0, :].rearrange("p (i n) -> p i n", i=NT)
        fin_y = ring[:, 0:2 * NT * D].rearrange("p (k i n) -> p k i n", k=2, i=NT)
        fin_junk = ring[:, 2 * SLOT:2 * SLOT + D]
        xg = tmp[:, 0:2 * D].rearrange("p (b n) -> p b n", b=2)
        ysb = tmp[:, 2 * D:4 * D].rearrange("p (b n) -> p b n", b=2)
        xT = tmp[:, 4 * D:4 * D + 2 * DC * WB].rearrange("p (b c n) -> p b c n", b=2, c=DC)
        act_t = rope[:, 1, 0:FC * WB].rearrange("p (f n) -> p f n", f=FC)
        act_s = rope[:, 1, FC * WB:2 * FC * WB].rearrange("p (f n) -> p f n", f=FC)
        hT = rope[:, 1, 2 * FC * WB:3 * FC * WB].rearrange("p (f n) -> p f n", f=FC)

        S = {}
        for n in ("consts", "cols", "rope", "rows", "x0", "x1", "woh", "wop", "ggh", "ggl", "wah", "wod",
                  "ath", "ahead", "n1", "wr0", "wr1", "whi", "wlo", "uTh", "gel", "stc", "wq", "wkv", "gw",
                  "wout", "wrt", "gatew0", "pads", "gather_go", "zero", "ys_init", "sd", "un", "uTp", "uT",
                  "zp", "ze", "conv", "lamA", "lam", "sqz", "statp", "rqs", "zn", "up", "upe", "ropeq",
                  "ropek", "kpe", "sc", "mxd", "pr", "pT", "pTe", "pv", "pve", "gp", "ga", "gm", "gs", "gh",
                  "lsq", "lst", "lrs", "ln", "asq", "asd", "atp", "atT", "xr0", "xr1", "op", "x2", "x2s",
                  "x2n", "x2r", "x2st0", "x2st1", "xnst0", "xnst1", "ttp", "tt", "lgp", "lg", "rt_e", "rt_d",
                  "mask", "rk", "ranked", "onehot", "rt_ap", "iters", "cx", "sqa", "ctl", "idx", "pos",
                  "gates", "diag", "fp", "ic", "xg0", "xg1", "xgp", "xT", "gu", "tnh", "hh", "dn", "ye", "ys0",
                  "ys1", "fx0", "fs", "fq", "fo", "fst0", "fst1", "frow", "dch", "ach", "pch", "gp2", "gx",
                  "acs"):
            S[n] = sem("s_" + n)
        s_wg = [sem(f"s_wgu{s}") for s in range(RING)]
        s_fy = [sem(f"s_fy{k}") for k in range(2 * NT)]
        s_wd = [sem(f"s_wd{s}") for s in range(RING)]

        def g(name):
            return S[name]

        units = [("x", c, n) for n in range(2) for c in range(LC)] + \
                [("z", c, n) for c in range(QC + KVC) for n in range(2)] + [("k", 0, n) for n in range(2)] + \
                [("g", c, n) for c in range(LC) for n in range(2)]
        w_tiles = [("x", c) for c in range(LC)] + [("z", c) for c in range(QC + KVC)] + [("k", 0)] + \
                  [("g", c) for c in range(LC)]
        first_col = {"z": 0, "k": QL + KVL, "x": QL + KVL + RP, "g": QL + KVL + RP + LRU}

        def width(kind):
            return RP if kind == "k" else P

        def last_unit(t):
            return max(u for u, (kind, c, n) in enumerate(units) if (kind, c) == w_tiles[t])
        U_Z, U_G = 2 * LC, 2 * (LC + QC + KVC + 1)
        GATES_AT = {U_Z + 1: 0, U_Z + 2: 1, U_Z + 5: 2, U_Z + 6: 3, U_Z + 9: 4, U_Z + 10: 5, U_G + 1: 6, U_G + 2: 7}
        ROOTS_AT = {U_Z + 4: 0, U_Z + 8: 1, U_G: 2}
        STATS_AT = {U_G + 1 + k: k for k in range(4)}
        STATS_END = U_G + 4
        ZB = 4
        ROWS_AT = {NT * (W_HIGH[j][1] + 1) + 1: j for j in range(LC)}
        steps = [(h, i) for h in range(NH) for i in range(NT)]

        def keys(i):
            return CHUNKS[0] if i * P < PROMPT else CHUNKS[1]

        ups = [("qr", r, n) for r in range(2) for n in range(2)] + \
              [("qn", m, n) for m in range(4) for n in range(2)] + \
              [("kn", m, n) for m in range(4) for n in range(2)] + \
              [("v", i, 0) for i in range(NT)]
        LSUM_AT = len(ups) - 7
        GELU_AT = {2: 0, 4: 1, 6: 2, 8: 3}

        def rank_bank(i):
            return psum[4] if i == NT - 1 else psum[1]

        def rounds(eng):
            return (eng.value_load(ctl[0:1, C_FULL:C_FULL + 1], min_val=(NE - 1) // RING, max_val=ROUNDS - 1),
                    eng.value_load(ctl[0:1, C_REST:C_REST + 1], min_val=1, max_val=RING))

        def each_block(eng, full_and_rest, step, first=0):
            full, rest = full_and_rest
            with eng.Fori(first, full) as i:
                for s in range(RING):
                    step(i, s)
            step(full, 0)
            for s in range(1, RING):
                with eng.If(rest > s):
                    step(full, s)

        block = ctx.enter_context(nc.Block())

        @block.sync
        def _(sp):
            xv = A_x.rearrange("(i p) d -> i p d", p=P)

            def load_x(i):
                if i >= 2:
                    sp.wait_ge(g("un"), i - 1)
                sp.dma_start(xin[:, i % 2, :], xv[i]).then_inc(g(f"x{i % 2}"), 16)
            wv = A_win.rearrange("(p c) n -> p c n", c=DC)

            def load_w(t):
                kind, c = w_tiles[t]
                if t >= 2:
                    sp.wait_ge(g("wlo"), t - 1)
                col0, m = first_col[kind] + c * P, width(kind)
                sp.dma_start(w_raw[:, t % 2, :, 0:m], wv[:, :, col0:col0 + m]).then_inc(g(f"wr{t % 2}"), 16)
            load_x(0)
            sp.dma_start(cols[:], A_cols).then_inc(g("cols"), 16)
            sp.dma_start(norm_row[:], A_rows[3:4, 0:D].to_broadcast([P, D])).then_inc(g("n1"), 16)
            sp.dma_start(consts[:], A_consts).then_inc(g("consts"), 16)
            load_x(1)
            load_w(0)
            load_w(1)
            load_x(2)
            load_w(2)
            load_x(3)
            load_w(3)
            load_x(4)
            load_x(5)
            sp.wait_ge(g("gatew0"), 1)
            for t, src in enumerate((A_wrg, A_wig)):
                for half in range(2):
                    for d in range(2):
                        sp.dma_start(gatew[64 * half:64 * half + 64, t, d, :, 64 * half:64 * half + 64],
                                     src[d].rearrange("(c two) i o -> two i c o", two=2)[half]).then_inc(g("gw"), 16)
            sp.dma_start(rope[:], A_rope.rearrange("p (a t) -> p a t", a=2)).then_inc(g("rope"), 16)
            sp.dma_start(brt[:], A_rows[2:3, 0:NG + NE].to_broadcast([P, NG + NE])).then_inc(g("rows"), 16)
            sp.dma_start(wrt[:], A_wrt.rearrange("(p c) n -> p c n", c=DC)).then_inc(g("wrt"), 16)
            load_w(4)
            load_w(5)
            sp.wait_ge(g("zero"), 1)
            sp.dma_start(ys_d[NE * WB:, :].rearrange("(p r) d -> p r d", r=EXTRA),
                         zeros[0:WB, :].unsqueeze(1).to_broadcast([WB, EXTRA, D])).then_inc(g("ys_init"), 16)
            for t in range(6, len(w_tiles)):
                load_w(t)
            sp.wait_ge(g("statp"), 4)
            sp.dma_start(wq, A_wq.rearrange("(c p) n -> p c n", p=P)).then_inc(g("wq"), 16)
            sp.dma_start(wkv, A_wkv.rearrange("(c p) n -> p c n", p=P)).then_inc(g("wkv"), 16)
            sp.wait_ge(g("ropek"), 1)
            sp.dma_start(norm_row[:], A_rows[0:1, 0:D].to_broadcast([P, D])).then_inc(g("rows"), 16)
            sp.wait_ge(g("zp"), len(units))
            sp.wait_ge(g("statp"), 4)
            sp.wait_ge(g("ropeq"), 8)
            sp.dma_start(wout, A_wout.rearrange("(c p) n -> p c n", p=P)).then_inc(g("wout"), 16)

            def load_res(i):
                if i >= 2:
                    sp.wait_ge(g(f"x2st{i % 2}"), 16 * (i // 2))
                    sp.wait_ge(g("x2n"), 2 * i - 2)
                sp.dma_start(tmp[:, (i % 2) * D:(i % 2 + 1) * D], xv[i]).then_inc(g(f"xr{i % 2}"), 16)
            sp.wait_ge(g("gh"), 8)
            load_res(0)
            load_res(1)

            wg_v = A_wgate.rearrange("e (p c) n -> e p (c n)", c=DC)
            wu_v = A_wup.rearrange("e (p c) n -> e p (c n)", c=DC)
            wd_v = A_wdown.rearrange("e (k p) n -> e p k n", p=P)

            def load_part(s, e, part):
                w = slot_at(s)[:, part * DC * F:(part + 1) * DC * F]
                if part < 2:
                    sp.dma_start(w, (wg_v, wu_v)[part][e]).then_inc(s_wg[s], 16)
                else:
                    sp.dma_start(w.rearrange("p (k n) -> p k n", k=FC), wd_v[e]).then_inc(s_wd[s], 16)

            def load_expert(s, e):
                for part in range(3):
                    load_part(s, e, part)
            sp.wait_ge(g("pv"), len(steps))
            load_part(3, 3, 1)
            load_part(3, 3, 2)
            for i in range(2, NT):
                load_res(i)
            sp.wait_ge(g("op"), 2 * NT)
            for s in range(2):
                load_expert(s, s)
            sp.wait_ge(g("xnst0"), 8 * NT)
            sp.wait_ge(g("xnst1"), 8 * NT)
            load_part(2, 2, 0)
            sp.wait_ge(g("xg0"), 16)
            load_part(2, 2, 1)
            load_part(2, 2, 2)
            sp.wait_ge(g("xg1"), 16)
            load_part(3, 3, 0)
            for s in range(4, RING):
                sp.wait_ge(g("gu"), RING + s - 4)
                load_expert(s, s)
            sp.wait_ge(g("ctl"), 1)

            def load_next(i, s):
                b = i * RING + s
                e = sp.value_load(ctl[0:1, bass.ds(b, 1)], min_val=0, max_val=NE - 1)
                w = slot_at(s)
                sp.wait_ge(g("gu"), b + 1)
                sp.dma_start(w[:, 0:DC * F], wg_v[bass.ds(e, 1)].rearrange("e p n -> (e p) n")).then_inc(s_wg[s], 16)
                sp.dma_start(w[:, DC * F:2 * DC * F], wu_v[bass.ds(e, 1)].rearrange("e p n -> (e p) n")).then_inc(s_wg[s], 16)
                sp.wait_ge(g("dn"), b + 2)
                sp.dma_start(w[:, 2 * DC * F:].rearrange("p (k n) -> p k n", k=FC),
                             wd_v[bass.ds(e, 1)].rearrange("e p k n -> (e p) k n")).then_inc(s_wd[s], 16)
            each_block(sp, rounds(sp), load_next, 1)
            sp.wait_ge(g("x2st0"), 8 * NT)
            sp.wait_ge(g("x2st1"), 8 * NT)
            sp.wait_ge(g("x2n"), 2 * NT)
            sp.wait_ge(g("gates"), 1)
            sp.dma_start(fin_row, A_rows[1:2, 0:D].to_broadcast([P, D])).then_inc(g("frow"), 16)
            x2v = x2_d.rearrange("(i p) d -> i p d", p=P)
            blocks = sp.value_load(ctl[0:1, C_BLOCKS:C_BLOCKS + 1], min_val=NE, max_val=NBC)
            for i in range(NT):
                if i % 2 == 1:
                    sp.wait_ge(g("gu"), blocks + (i + 1) // 2)
                sp.dma_start(fin_x[i], x2v[i]).then_inc(g("fx0"), 16)
            outs = [y_prompt.rearrange("b (i p) d -> (b i) p d", p=P)[i] for i in range(PROMPT // P)] + \
                   [y_sample.rearrange("b (i p) d -> (b i) p d", p=P)[i] for i in range((TOK - PROMPT) // P)]
            for i in range(NT):
                sp.wait_ge(g("fo"), i + 1)
                sp.dma_start(outs[i], fin_x[i]).then_inc(g("fst0"), 16)
            sp.wait_ge(g("fst0"), 16 * NT)

        @block.gpsimd
        def _(po):
            chain = [0]

            def link(ins):
                chain[0] += 1
                ins.then_inc(g("pch"), 1)
                po.wait_ge(g("pch"), chain[0])
            po.memset(gatew, 0.0).then_inc(g("gatew0"), 1)
            po.memset(xb[:], 0.0).then_inc(g("pads"), 1)

            def split(t):
                k, m = t % W_RING, width(w_tiles[t][0])
                raw = w_raw[:, t % 2, :, 0:m]
                if t >= W_RING:
                    po.wait_ge(g(f"wr{t % 2}"), 16 * (t // 2 + 1))
                    po.wait_ge(g("zp"), last_unit(t - W_RING) + 1)
                    po.tensor_copy(wh[:, k, :, 0:m], raw).then_inc(g("whi"), 1)
                po.wait_ge(g("whi"), t + 1)
                po.tensor_tensor(wl[:, k, :, 0:m], raw, wh[:, k, :, 0:m].bitcast(f32), ALU.subtract).then_inc(g("wlo"), 1)
                po.wait_ge(g("wlo"), t + 1)

            def add_squares(c, into, n):
                po.wait_ge(g("sqz"), c + 1)
                po.tensor_tensor(sqz[:, into, :], sqz[:, into, :], sqz[:, c, :], ALU.add).then_inc(g("sqa"), 1)
                po.wait_ge(g("sqa"), n)
            for t in range(W_RING):
                split(t)
            po.wait_ge(g("un"), NT)
            po.memset(zeros, 0.0).then_inc(g("zero"), 1)
            for t in range(W_RING, len(w_tiles)):
                if t == len(w_tiles) - 4:
                    add_squares(1, 0, 1)
                if t == len(w_tiles) - 3:
                    add_squares(2, 0, 2)
                if t == len(w_tiles) - 1:
                    add_squares(4, QC, 3)
                split(t)
            for c in range(LC):
                po.wait_ge(g("gel"), c + 1)
                po.wait_ge(g("gh"), 2 * c + 2)
                link(po.tensor_tensor(gg[:, c, :], gg[:, c, :], xb[:, c, 0:TOK], ALU.mult))
                po.tensor_tensor(xb[:, c, 0:TOK], gg[:, c, :], gg[:, c, :], ALU.mult).then_inc(g("lsq"), 1)
                if c >= 1:
                    po.wait_ge(g("lsq"), 2 * c)
                    po.tensor_tensor(xb[:, 0, 0:TOK], xb[:, 0, 0:TOK], xb[:, c, 0:TOK], ALU.add).then_inc(g("lsq"), 1)
                po.wait_ge(g("lsq"), 2 * c + 1)
            def split_rows(j):
                po.wait_ge(g("sc"), NT * (W_HIGH[j][1] + 1))
                raw = wout[:, j, :]
                po.tensor_copy(wo_high[j], raw).then_inc(g("woh"), 1)
                po.wait_ge(g("woh"), j - LC + 1)
                po.tensor_tensor(wo_low[j], raw, wo_high[j].bitcast(f32), ALU.subtract).then_inc(g("wop"), 1)

            def split_branch(c):
                po.wait_ge(g("sc"), NT * (LC + c + 1))
                po.wait_ge(g("ln"), c + 1)
                po.tensor_copy(gg_high[c], gg[:, c, :]).then_inc(g("ggh"), 1)
                po.wait_ge(g("ggh"), c + 1)
                po.tensor_tensor(gg_low[c], gg[:, c, :], gg_high[c].bitcast(f32), ALU.subtract).then_inc(g("ggl"), 1)
            po.wait_ge(g("wout"), 16)
            for j in (LC, LC + 1, LC + 2, LC + 3):
                split_rows(j)
            for c in range(LC):
                split_branch(c)
            po.wait_ge(g("idx"), 1)
            po.wait_ge(g("xnst0"), 8 * NT)
            po.wait_ge(g("xnst1"), 8 * NT)
            po.wait_ge(g("iters"), 1)
            link(po.tensor_copy(idx_now[:, 0:1], idx[:, 0:1]))
            po.wait_ge(g("lgp"), NT)
            po.wait_ge(g("x2st0"), 8 * NT)
            po.wait_ge(g("x2st1"), 8 * NT)
            po.indirect_dma_start(xg[0:WB, 0, :], None, xn_d, bass.IndirectOffsetOnAxis(idx_now[:, 0:1], 0)).then_inc(g("xg0"), 16)

            def next_rows(i, s):
                b = i * RING + s
                po.tensor_copy(idx_now[:, (s + 1) % RING:(s + 1) % RING + 1],
                               idx[:, bass.ds(b + 1, 1)]).then_inc(g("ic"), 1)
                po.wait_ge(g("xgp"), b + 1)
                po.wait_ge(g("ic"), b + 1)
                po.sem_inc(g("gather_go"), 1)
                po.indirect_dma_start(xg[0:WB, (s + 1) % 2, :], None, xn_d,
                                      bass.IndirectOffsetOnAxis(idx_now[:, (s + 1) % RING:(s + 1) % RING + 1], 0)
                                      ).then_inc(g(f"xg{(s + 1) % 2}"), 16)
            each_block(po, rounds(po), next_rows)
            po.wait_ge(g("pos"), 1)
            po.wait_ge(g("ctl"), 1)
            blocks, end0, end1 = (po.value_load(ctl[0:1, k:k + 1], min_val=1, max_val=16 * NBC)
                                  for k in (C_BLOCKS, C_YS0, C_YS1))
            po.wait_ge(g("ys0"), end0)
            po.wait_ge(g("ys1"), end1)
            po.wait_ge(g("dn"), blocks + RING + 1)
            po.sem_inc(g("gather_go"), 1)
            for i in range(NT):
                for k in range(2):
                    po.indirect_dma_start(fin_y[:, k, i, :], None, ys_d,
                                          bass.IndirectOffsetOnAxis(pos_i[:, 2 * i + k:2 * i + k + 1], 0)
                                          ).then_inc(s_fy[2 * i + k], 16)

        @block.tensor
        def _(pe):
            pe.wait_ge(g("consts"), 16)
            def turn_input(i):
                pe.wait_ge(g("un"), i + 1)
                for j in range(2):
                    if i >= 2:
                        pe.wait_ge(g("uT"), 2 * (i - 2) + j + 1)
                    for c in range(4):
                        last = pe.transpose(psum[4 + 2 * (i % 2) + j][:, c * P:(c + 1) * P],
                                            un[:, i % 2, (4 * j + c) * P:(4 * j + c + 1) * P], ident)
                    last.then_inc(g("uTp"), 1)

            def gates(u):
                c, d = u // 2, u % 2
                pe.wait_ge(g("conv"), c + 1)
                if u >= 1:
                    pe.wait_ge(g("ga"), 4 * u)
                for t in range(2):
                    pe.matmul(psum[5 + t][:, :], gatew[:, t, d, c, :], xc[:, c % 2, XOFF[1]:XOFF[1] + 512],
                              start=True, stop=True)
                for t in range(2):
                    last = pe.matmul(psum[7][:, t * PROMPT:(t + 1) * PROMPT], gatew[:, t, d, c, :],
                                     xc[:, c % 2, 0:PROMPT], start=(t == 0), stop=(t == 1), skip_group_check=True)
                last.then_inc(g("gp"), 1)

            def latent_sums(k):
                a, n = k // 2, k % 2
                t0, tn = CHUNKS[n]
                pe.wait_ge(g("sqa"), (2, 3)[a])
                if k >= 1:
                    pe.wait_ge(g("stc"), k)
                last = pe.matmul(psum[4][:, 0:tn], ones, sqz[:, (0, QC)[a], t0:t0 + tn], start=True, stop=True)
                last.then_inc(g("statp"), 1)

            turn_input(0)
            turn_input(1)
            pe.wait_ge(g("uT"), 4)
            for u, (kind, c, n) in enumerate(units):
                if u == LC:
                    pe.wait_ge(g("uT"), 2 * NT)
                if u == U_Z:
                    pe.wait_ge(g("gw"), 16 * 8)
                if u in GATES_AT:
                    gates(GATES_AT[u])
                if u in STATS_AT:
                    latent_sums(STATS_AT[u])
                if u >= ZB:
                    pe.wait_ge(g("ze"), u - ZB + 1)
                t0, tn = CHUNKS[n]
                t, m = w_tiles.index((kind, c)), width(kind)
                pe.wait_ge(g("wlo"), t + 1)
                for k in range(DC):
                    for p, (w, x) in enumerate(((wh, uh), (wl, uh), (wh, ul))):
                        last = pe.matmul(psum[u % ZB][0:m, 0:tn], w[:, t % W_RING, k, 0:m], x[:, k, t0:t0 + tn],
                                         start=(k == 0 and p == 0), stop=(k == DC - 1 and p == 2))
                last.then_inc(g("zp"), 1)
                if u < LC:
                    turn_input(2 + u)
            pe.wait_ge(g("wq"), 16)
            pe.wait_ge(g("zn"), QC)
            pe.wait_ge(g("ze"), len(units))
            for u, (kind, j, n) in enumerate(ups):
                if u == LSUM_AT:
                    pe.wait_ge(g("ga"), 32)
                    for m, (t0, tn) in enumerate(CHUNKS):
                        pe.wait_ge(g("lsq"), 2 * LC - 1)
                        pe.matmul(psum[6 + m][:, 0:tn], ones, xb[:, 0, t0:t0 + tn], start=True, stop=True).then_inc(g("lst"), 1)
                if kind == "kn" and j == 0 and n == 0:
                    pe.wait_ge(g("zn"), QC + KVC)
                    pe.wait_ge(g("wkv"), 16)
                if u >= ZB:
                    pe.wait_ge(g("upe"), u - ZB + 1)
                t0, tn = CHUNKS[n]
                bank = psum[u % ZB]
                if kind in ("qr", "qn"):
                    o = 512 + j * P if kind == "qr" else j * P
                    for c in range(QC):
                        last = pe.matmul(bank[:, 0:tn], wq[:, c, o:o + P], zl[:, c, t0:t0 + tn],
                                         start=(c == 0), stop=(c == QC - 1))
                elif kind == "kn":
                    for c in range(KVC):
                        last = pe.matmul(bank[:, 0:tn], wkv[:, c, j * P:(j + 1) * P], zl[:, QC + c, t0:t0 + tn],
                                         start=(c == 0), stop=(c == KVC - 1))
                else:
                    for c in range(KVC):
                        last = pe.matmul(bank[:, :], zl[:, QC + c, j * P:(j + 1) * P], wkv[:, c, 512:1024],
                                         start=(c == 0), stop=(c == KVC - 1))
                last.then_inc(g("up"), 1)
            def scores(n):
                h, i = steps[n]
                k0, kn = keys(i)
                if n >= 3:
                    pe.wait_ge(g("pr"), n - 2)
                pe.matmul(psum[n % 3][:, 0:kn], qT[0:96, h, i * P:(i + 1) * P], kT[0:96, h, k0:k0 + kn],
                          start=True, stop=True).then_inc(g("sc"), 1)

            def turn(n):
                kn = keys(steps[n][1])[1]
                pe.wait_ge(g("pr"), n + 1)
                if n >= 2:
                    pe.wait_ge(g("pTe"), n - 1)
                for b in range(kn // P):
                    last = pe.transpose(psum[3 + n % 2][:, b * P:(b + 1) * P], prob[:, n % 2, b * P:(b + 1) * P], ident)
                last.then_inc(g("pT"), 1)

            def values(n):
                h, i = steps[n]
                k0, kn = keys(i)
                pe.wait_ge(g("pTe"), n + 1)
                if n >= 1:
                    pe.wait_ge(g("pve"), n)
                for b in range(kn // P):
                    last = pe.matmul(psum[5][:, 0:VH], probT[:, n % 2, b * P:(b + 1) * P],
                                     V[:, k0 // P + b, h * VH:(h + 1) * VH], start=(b == 0), stop=(b == kn // P - 1))
                last.then_inc(g("pv"), 1)

            def turn_att(i):
                pe.wait_ge(g("pve"), len(steps) - NT + i + 1)
                if i < 2:
                    pe.wait_ge(g("lrs"), 2)
                else:
                    pe.wait_ge(g("atT"), i - 1)
                for c in range(LC):
                    last = pe.transpose(psum[6 + i % 2][:, c * P:(c + 1) * P], att[:, i, c * P:(c + 1) * P], ident)
                last.then_inc(g("atp"), 1)
            pe.wait_ge(g("ropeq"), 8)
            pe.wait_ge(g("kpe"), 1)
            pe.wait_ge(g("upe"), len(ups) - 1)
            scores(0)
            pe.wait_ge(g("upe"), len(ups))
            scores(1)
            for n in range(len(steps)):
                if n + 2 < len(steps):
                    scores(n + 2)
                turn(n)
                if n >= 1:
                    values(n - 1)
                if n - 3 >= len(steps) - NT:
                    turn_att(n - 3 - (len(steps) - NT))
            values(len(steps) - 1)
            for i in range(NT - 3, NT):
                turn_att(i)
            pe.wait_ge(g("wout"), 16)
            pe.wait_ge(g("wop"), LC)
            pe.wait_ge(g("wod"), LC)
            pe.wait_ge(g("wrt"), 16)

            def turn_rows2(i):
                pe.wait_ge(g("x2n"), 2 * i + 2)
                pe.wait_ge(g("atT"), NT)
                for j in range(2):
                    if i >= 1:
                        pe.wait_ge(g("tt"), 2 * (i - 1) + j + 1)
                    for c in range(4):
                        last = pe.transpose(psum[6 + j][:, c * P:(c + 1) * P],
                                            xn[:, i % 2, (4 * j + c) * P:(4 * j + c + 1) * P], ident)
                    last.then_inc(g("ttp"), 1)

            def router(i):
                pe.wait_ge(g("tt"), 2 * i + 2)
                if i >= 1:
                    pe.wait_ge(g("lg"), i)
                for c in range(DC):
                    last = pe.matmul(psum[0][:, 0:NG + NE], tT[:, c, :], wrt[:, c, :], start=(c == 0), stop=(c == DC - 1))
                last.then_inc(g("lgp"), 1)

            def ranks(i):
                end = i == NT - 1
                pe.wait_ge(g("mask"), i + 1)
                if i >= 1 and not end:
                    pe.wait_ge(g("ranked"), i)
                bank = rank_bank(i)
                last = pe.matmul(bank[:, 0:NE], before, mask[:, i, :], start=True, stop=(i == 0), skip_group_check=True)
                if i >= 1:
                    last = pe.matmul(bank[:, 0:NE], ones, seen[:, i, :], start=False, stop=not end,
                                     skip_group_check=True)
                if end:
                    pe.matmul(bank[:, NE:2 * NE], ones, seen[:, i, :], start=False, stop=False, skip_group_check=True)
                    last = pe.matmul(bank[:, NE:2 * NE], ones, mask[:, i, :], start=False, stop=True,
                                     skip_group_check=True)
                last.then_inc(g("rk"), 1)
            for i in range(NT):
                for half in range(2):
                    w = 2 * i + half
                    if w >= 2:
                        pe.wait_ge(g("x2"), w - 1)
                    t, out = slice(i * P, (i + 1) * P), slice(half * 512, (half + 1) * 512)
                    for k in range(2):
                        if k == 1:
                            pe.wait_ge(g("atT"), i + 1)
                            if half == 0 and i >= 1:
                                turn_rows2(i - 1)
                        for c in range(LC):
                            if k == 0:
                                pe.wait_ge(g("ggl"), c + 1)
                            j = (1 - k) * LC + c
                            high, low = (gg_high[c][:, t], gg_low[c][:, t]) if k == 0 else (at_high[:, c, t], at_low[c][:, t])
                            for p, (x, w) in enumerate(((high, wo_high[j]), (high, wo_low[j]), (low, wo_high[j]))):
                                last = pe.matmul(psum[2 + 2 * half + k][:, :], x, w[:, out],
                                                 start=(c == 0 and p == 0), stop=(c == LC - 1 and p == 2))
                    last.then_inc(g("op"), 1)
                    if i >= 1:
                        if half == 0:
                            router(i - 1)
                        else:
                            ranks(i - 1)
            turn_rows2(NT - 1)
            router(NT - 1)
            ranks(NT - 1)
            for k in range(2 * NT):
                pe.wait_ge(g("onehot"), k + 1)
                last = pe.matmul(psum[3][0:WB, 0:NBC], oh_w[k], oh_b[:, k, :], start=(k == 0), stop=(k == 2 * NT - 1))
            last.then_inc(g("rt_ap"), 1)

            pe.wait_ge(g("iters"), 1)
            pe_rounds = rounds(pe)

            def turn_rows(par, b, first=False):
                pe.wait_ge(g(f"xg{par}"), 16 if first else (b - par) * 8 + 16)
                if not first:
                    pe.wait_ge(g("xT"), b * 2)
                for j in range(2):
                    for c in range(4):
                        last = pe.transpose(psum[2 + j][:, c * WB:(c + 1) * WB],
                                            xg[0:WB, par, (4 * j + c) * P:(4 * j + c + 1) * P], ident[0:WB, 0:WB])
                last.then_inc(g("xgp"), 1)
            pe.sem_inc(g("xgp"), 1)
            pe.sem_inc(g("gu"), RING)
            pe.sem_inc(g("dn"), RING + 1)
            pe.wait_ge(g("idx"), 1)
            turn_rows(0, 0, True)

            def block_products(i, s):
                b = i * RING + s
                w = slot_at(s)
                wgu = w[:, 0:2 * DC * F].rearrange("p (t c n) -> p t c n", t=2, c=DC)
                wdn = w[:, 2 * DC * F:].rearrange("p (k n) -> p k n", k=FC)
                pe.wait_ge(s_wg[s], i * 32 + 32)
                pe.wait_ge(g("xT"), b * 2 + 2)
                for f in range(FC):
                    pe.wait_ge(g("hh"), b * FC + f + 1)
                    for t in range(2):
                        for c in range(DC):
                            last = pe.matmul(psum[f][:, t * WB:(t + 1) * WB], wgu[:, t, c, f * P:(f + 1) * P],
                                             xT[:, s % 2, c, :], start=(t == 0 and c == 0), stop=(t == 1 and c == DC - 1),
                                             skip_group_check=True)
                    if f == 0:
                        last.then_inc(g("gp2"), 1)
                last.then_inc(g("gu"), 1)
                turn_rows((s + 1) % 2, b + 1)
                pe.wait_ge(s_wd[s], i * 16 + 16)
                pe.wait_ge(g("ye"), b + 1)
                for k in range(FC):
                    pe.wait_ge(g("hh"), (b + 1) * FC + k + 1)
                    for half in range(2):
                        last = pe.matmul(psum[4 + 2 * (s % 2) + half][0:WB, :], hT[:, k, :],
                                         wdn[:, k, half * 512:(half + 1) * 512], start=(k == 0), stop=(k == FC - 1),
                                         skip_group_check=True)
                last.then_inc(g("dn"), 1)
            each_block(pe, pe_rounds, block_products)
            pe.wait_ge(g("ctl"), 1)
            blocks = pe.value_load(ctl[0:1, C_BLOCKS:C_BLOCKS + 1], min_val=NE, max_val=NBC)
            pe.wait_ge(g("hh"), blocks * FC + FC)
            pe.wait_ge(g("ye"), blocks + 2)
            pe.wait_ge(g("xT"), blocks * 2 + 2)

            def residual(i):
                if i >= FIN_BANKS:
                    pe.wait_ge(g("fs"), 2 * (i - FIN_BANKS) + 2)
                for half in range(2):
                    pe.matmul(psum[2 * (i % FIN_BANKS) + half][:, :], ident, fin_x[i][:, half * 512:(half + 1) * 512],
                              start=True, stop=False)
            pe.wait_ge(g("fx0"), 16 * NT)
            pe.wait_ge(g("gates"), 1)
            pe.wait_ge(g("diag"), NT)
            for i in range(FIN_BANKS):
                residual(i)
            for i in range(NT):
                pe.wait_ge(s_fy[2 * i], 16)
                for half in range(2):
                    last = pe.matmul(psum[2 * (i % FIN_BANKS) + half][:, :], diag[:, i, :],
                                     fin_y[:, 0, i, half * 512:(half + 1) * 512], start=False, stop=True)
                last.then_inc(g("fp"), 1)
                if 1 <= i and i - 1 + FIN_BANKS < NT:
                    residual(i - 1 + FIN_BANKS)

        @block.scalar
        def _(ac):
            chain = [0]

            def link(ins):
                chain[0] += 1
                ins.then_inc(g("ach"), 1)
                ac.wait_ge(g("ach"), chain[0])
            eps = C("eps")
            ac.wait_ge(g("ahead"), 1)
            ac.activation(ahead, ahead, ACT.Sqrt).then_inc(g("ahead"), 1)
            ac.wait_ge(g("consts"), 16)
            ac.wait_ge(g("cols"), 16)
            def row_norm(i):
                ac.wait_ge(g(f"x{i % 2}"), 16 * (i // 2 + 1))
                link(ac.activation(junk, xin[:, i % 2, :], ACT.Square, accum_out=ssq[:, i:i + 1]))
                ac.activation(rstd1[:, i:i + 1], ssq[:, i:i + 1], ACT.Sqrt, bias=eps, scale=1.0 / D).then_inc(g("sd"), 1)

            def input_high(i):
                for j in range(2):
                    ac.wait_ge(g("uTp"), 2 * i + j + 1)
                    ac.activation(uh[:, 4 * j:4 * j + 4, i * P:(i + 1) * P],
                                  psum[4 + 2 * (i % 2) + j][:, :].rearrange("p (c t) -> p c t", c=4),
                                  ACT.Copy).then_inc(g("uTh"), 1)

            def weight_high(t):
                ac.wait_ge(g(f"wr{t % 2}"), 16 * (t // 2 + 1))
                ac.activation(wh[:, t, :, :], w_raw[:, t % 2, :, :], ACT.Copy).then_inc(g("whi"), 1)

            def move_out(u):
                kind, c, n = units[u]
                ac.wait_ge(g("zp"), u + 1)
                t0, tn = CHUNKS[n]
                if kind == "x":
                    dst = xb[:, c, XOFF[n] + 1:XOFF[n] + 1 + tn]
                elif kind == "z":
                    dst = zl[:, c, t0:t0 + tn]
                elif kind == "k":
                    dst = kr[0:RP, t0:t0 + tn]
                else:
                    dst = gg[:, c, t0:t0 + tn]
                ac.activation(dst, psum[u % ZB][0:width(kind), 0:tn], ACT.Copy).then_inc(g("ze"), 1)
            ac.wait_ge(g("pads"), 1)
            row_norm(0)
            row_norm(1)
            weight_high(0)
            input_high(0)
            input_high(1)
            weight_high(1)
            row_norm(2)
            for i in range(2, NT):
                if i + 1 < NT:
                    row_norm(i + 1)
                input_high(i)
                if i < W_RING:
                    weight_high(i)
                move_out(i - 2)
            ac.wait_ge(g("lam"), 1)
            ac.activation(lam_t[:, 1, :], lam_t[:, 0, :], ACT.Exp, scale=-1.0).then_inc(g("lamA"), 1)
            ac.wait_ge(g("lam"), 2)
            ac.activation(lam_t[:, 3, :], lam_t[:, 2, :], ACT.Ln).then_inc(g("lamA"), 1)

            def unit_gates(u):
                c, d = u // 2, u % 2
                j = d * LC + c
                th_r, th_i, dec, dec2 = temps[d]
                ac.wait_ge(g("gp"), u + 1)
                if u >= 2:
                    ac.wait_ge(g("gh"), u - 1)
                else:
                    ac.wait_ge(g("uTp"), 2 * NT)
                for t, (dst, hb) in enumerate(((th_r, hb_r), (th_i, hb_i))):
                    ac.activation(dst[:, PROMPT:TOK], psum[5 + t][:, :], ACT.Tanh, bias=hb[:, j:j + 1], scale=0.5).then_inc(g("ga"), 1)
                    ac.activation(dst[:, 0:PROMPT], psum[7][:, t * PROMPT:(t + 1) * PROMPT], ACT.Tanh,
                                  bias=hb[:, j:j + 1], scale=0.5).then_inc(g("ga"), 1)
                ac.wait_ge(g("ga"), 4 * u + 4)
                ac.activation(dec, th_r, ACT.Exp, bias=lamc[:, j:j + 1], scale=lamc[:, j:j + 1]).then_inc(g("gx"), 1)
                ac.activation(dec2, th_r, ACT.Exp, bias=lam2[:, j:j + 1], scale=lam2[:, j:j + 1]).then_inc(g("gx"), 1)
                ac.wait_ge(g("gx"), 3 * u + 2)
                ac.activation(th_r, th_r, ACT.Tanh, bias=nlamc[:, j:j + 1], scale=nlamc[:, j:j + 1]).then_inc(g("gx"), 1)

            def pair_roots(c):
                for d in range(2):
                    u = 2 * c + d
                    ac.wait_ge(g("gm"), 2 * u + 1)
                    dec2 = temps[d][3]
                    ac.activation(dec2, dec2, ACT.Sqrt, scale=0.25).then_inc(g("gs"), 1)
            for u, (kind, c, n) in enumerate(units):
                if u in GATES_AT:
                    if GATES_AT[u] == 0:
                        ac.wait_ge(g("lam"), 4)
                    unit_gates(GATES_AT[u])
                if u in ROOTS_AT:
                    pair_roots(ROOTS_AT[u])
                if u == U_Z + 2 * (QC + KVC):
                    ac.wait_ge(g("ys_init"), 16)
                if u >= NT - 2:
                    move_out(u)
                if kind == "z" and n == 1:
                    ac.wait_ge(g("ze"), u + 1)
                    ac.activation(sqz[:, c, :], zl[:, c, :], ACT.Square).then_inc(g("sqz"), 1)
                if u == STATS_END:
                    ac.wait_ge(g("stc"), 4)
                    ac.activation(rn, rn, ACT.Sqrt).then_inc(g("rqs"), 1)
                    pair_roots(3)
            for u, (kind, j, n) in enumerate(ups):
                ac.wait_ge(g("up"), u + 1)
                t0, tn = CHUNKS[n]
                src = psum[u % ZB]
                if kind == "qr":
                    if u == 0:
                        ac.wait_ge(g("zp"), len(units))
                    ins = ac.activation(qr[:, j, t0:t0 + tn], src[:, 0:tn], ACT.Copy)
                elif kind == "v":
                    if j == 0:
                        ac.wait_ge(g("zn"), QC + KVC)
                    ins = ac.activation(V[:, j, :], src[:, :], ACT.Copy)
                else:
                    dst = qT if kind == "qn" else kT
                    if n == 0 and j == 0:
                        ac.wait_ge(g("zp"), len(units))
                    ac.activation(dst[0:64, 2 * j, t0:t0 + tn], src[0:64, 0:tn], ACT.Copy)
                    ins = ac.activation(dst[0:64, 2 * j + 1, t0:t0 + tn], src[64:128, 0:tn], ACT.Copy)
                ins.then_inc(g("upe"), 1)
                if u in GELU_AT:
                    c = GELU_AT[u]
                    if c == 0:
                        ac.wait_ge(g("ze"), len(units))
                    ac.activation(gg[:, c, :], gg[:, c, :], ACT.Gelu_apprx_tanh).then_inc(g("gel"), 1)
                if u == LSUM_AT - 1:
                    for n, (t0, tn) in enumerate(CHUNKS):
                        ac.wait_ge(g("lst"), n + 1)
                        ac.activation(rnorm2[:, t0:t0 + tn], psum[6 + n][:, 0:tn], ACT.Sqrt, bias=eps, scale=1.0 / LRU).then_inc(g("lrs"), 1)
                    ac.wait_ge(g("ahead"), 2)
                    ac.activation(ahead, eps, ACT.Exp).then_inc(g("ahead"), 1)

            def exps(n):
                kn = keys(steps[n][1])[1]
                k = n % 4
                ac.wait_ge(g("mxd"), n + 1)
                if n >= 2:
                    ac.wait_ge(g("pT"), n - 1)
                if n >= 4:
                    ac.wait_ge(g("pve"), n - 3)
                ac.activation(prob[:, n % 2, 0:kn], psum[n % 3][:, 0:kn], ACT.Exp, bias=nm[:, k:k + 1], scale=SCALE,
                              accum_out=rs[:, k:k + 1]).then_inc(g("pr"), 1)

            def pt_out(n):
                kn = keys(steps[n][1])[1]
                ac.wait_ge(g("pT"), n + 1)
                if n >= 2:
                    ac.wait_ge(g("pv"), n - 1)
                ac.activation(probT[:, n % 2, 0:kn], psum[3 + n % 2][:, 0:kn], ACT.Copy).then_inc(g("pTe"), 1)

            def rows_high(j):
                ac.wait_ge(g("sc"), NT * (W_HIGH[j][1] + 1))
                ac.wait_ge(g("wout"), 16)
                ac.activation(wo_high[j], wout[:, j, :], ACT.Copy, scale=col("att_norm", j)).then_inc(g("wah"), 1)

            def att_high(i):
                ac.wait_ge(g("atp"), i + 1)
                ac.activation(at_high[:, :, i * P:(i + 1) * P], psum[6 + i % 2][:, :].rearrange("p (c t) -> p c t", c=LC),
                              ACT.Copy).then_inc(g("ath"), 1)

            def att_squares(i):
                ac.wait_ge(g("pve"), len(steps) - NT + i + 1)
                if i >= 1:
                    ac.wait_ge(g("asq"), i)
                ac.activation(att_junk, att[:, i, :], ACT.Square, accum_out=ssq[:, i:i + 1]).then_inc(g("asq"), 1)
            ac.wait_ge(g("gh"), 8)
            exps(0)
            for n in range(len(steps)):
                if n + 1 < len(steps):
                    exps(n + 1)
                pt_out(n)
                if n - 3 >= len(steps) - NT:
                    att_squares(n - 3 - (len(steps) - NT))
                if n - 4 >= len(steps) - NT:
                    att_high(n - 4 - (len(steps) - NT))
                if n in ROWS_AT:
                    rows_high(ROWS_AT[n])
            for i in range(NT - 4, NT):
                att_high(i)
                if i >= NT - 3:
                    att_squares(i)
            ac.wait_ge(g("asq"), NT)
            ac.activation(rstd1, ssq, ACT.Sqrt, bias=eps, scale=1.0 / 512).then_inc(g("asd"), 1)
            for i in range(NT):
                ac.wait_ge(g("x2"), 2 * i + 2)
                link(ac.activation(sqj, x2t[:, i % 2, :], ACT.Square, accum_out=ssq2[:, i:i + 1]))
                ac.activation(rstd2[:, i:i + 1], ssq2[:, i:i + 1], ACT.Sqrt, bias=eps, scale=1.0 / D).then_inc(g("x2s"), 1)
                ac.dma_start(x2_d[i * P:(i + 1) * P, :], x2t[:, i % 2, :]).then_inc(g(f"x2st{i % 2}"), 16)
                ac.wait_ge(g("x2r"), i + 1)
                ac.wait_ge(g("x2n"), 2 * i + 2)
                ac.wait_ge(g("ttp"), 2 * i + 2)
                link(ac.activation(xn[:, i % 2, :], xn[:, i % 2, :], ACT.Copy, scale=rstd2[:, i:i + 1]))
                ac.dma_start(xn_d[i * P:(i + 1) * P, :], xn[:, i % 2, :]).then_inc(g(f"xnst{i % 2}"), 16)
            ac.wait_ge(g("rt_d"), 1)
            ac.activation(g4b, g4b, ACT.Exp).then_inc(g("rt_e"), 1)
            ac.wait_ge(g("rt_d"), 2)
            ac.activation(egap, ediff, ACT.Exp).then_inc(g("rt_e"), 1)
            ac.wait_ge(g("iters"), 1)
            ac.sem_inc(g("ys0"), 16)
            ac.sem_inc(g("ys1"), 16)
            ac.sem_inc(g("ye"), 2)

            def block_moves(i, s):
                b = i * RING + s
                for f in range(FC):
                    if f == 0:
                        ac.wait_ge(g("gp2"), b + 1)
                    else:
                        ac.wait_ge(g("gu"), b + RING + 1)
                    ac.activation(act_t[:, f, :], psum[f][:, 0:WB], ACT.Tanh, scale=0.5).then_inc(g("tnh"), 1)
                ac.wait_ge(g(f"ys{s % 2}"), (b - s % 2) * 8 + 16)
                ac.wait_ge(g("dn"), b + RING + 2)
                for half in range(2):
                    ins = ac.activation(ysb[0:WB, s % 2, half * 512:(half + 1) * 512],
                                        psum[4 + 2 * (s % 2) + half][0:WB, :], ACT.Copy)
                ins.then_inc(g("ye"), 1)
                ac.wait_ge(g("ye"), b + 3)
                ac.dma_start(ys_d[bass.ds(b * WB, WB), :], ysb[0:WB, s % 2, :]).then_inc(g(f"ys{s % 2}"), 16)
            each_block(ac, rounds(ac), block_moves)
            ac.wait_ge(g("ahead"), 3)
            ac.activation(ahead, eps, ACT.Sqrt)
            for i in range(NT):
                ac.wait_ge(g("fs"), 2 * i + 2)
                link(ac.activation(fin_junk, fin_x[i], ACT.Square, accum_out=ssq3[:, i:i + 1]))
                ac.activation(rstd3[:, i:i + 1], ssq3[:, i:i + 1], ACT.Sqrt, bias=eps, scale=1.0 / D).then_inc(g("fq"), 1)

        def bc(a, n):
            return a.unsqueeze(2).to_broadcast([P, a.shape[1], n])

        def bm(a, n):
            return a.unsqueeze(1).to_broadcast([P, n, a.shape[1]])

        def route_tile(v, link, i):
            gl, el = logits[:, i, 0:NG], logits[:, i, NG:NG + NE]
            iota = C("iota_m", NE)
            link(v.tensor_reduce(gtop[:, i:i + 1], gl, AX.X, ALU.max))
            link(v.scalar_tensor_tensor(out=g4, in0=gl, scalar=gtop[:, i:i + 1], in1=iota[:, 0:NG],
                                        op0=ALU.is_equal, op1=ALU.mult))
            link(v.tensor_reduce(gat, g4, AX.X, ALU.min))
            link(v.tensor_scalar(g4, iota[:, 0:NG], gat, -BIG, ALU.not_equal, ALU.mult))
            link(v.tensor_tensor(em.rearrange("p (g e) -> p g e", g=NG), el.rearrange("p (g e) -> p g e", g=NG),
                                 g4.unsqueeze(2).to_broadcast([P, NG, EG]), ALU.add))
            for k, top in enumerate((e0top, e1top)):
                m = 2 * i + k
                link(v.tensor_reduce(top[:, i:i + 1], em, AX.X, ALU.max))
                link(v.scalar_tensor_tensor(out=t1, in0=em, scalar=top[:, i:i + 1], in1=iota, op0=ALU.is_equal,
                                            op1=ALU.mult))
                link(v.tensor_reduce(at[:, m:m + 1], t1, AX.X, ALU.min))
                link(v.tensor_scalar(E[:, i, k, :], iota, at[:, m:m + 1], None, ALU.is_equal))
                if k == 0:
                    link(v.scalar_tensor_tensor(out=em, in0=E[:, i, 0, :], scalar=-2 * BIG, in1=em, op0=ALU.mult,
                                                op1=ALU.add))
            v.tensor_tensor(mask[:, i, :], E[:, i, 0, :], E[:, i, 1, :], ALU.add).then_inc(g("mask"), 1)
            v.wait_ge(g("mask"), i + 1)
            if i == 0:
                link(v.tensor_copy(seen[:, 1, :], mask[:, 0, :]))
            elif i < NT - 1:
                link(v.tensor_tensor(seen[:, i + 1, :], seen[:, i, :], mask[:, i, :], ALU.add))

        def rank_tile(v, link, i):
            m = slice(2 * i, 2 * i + 2)
            v.wait_ge(g("rk"), i + 1)
            ins = v.tensor_tensor(t2, E[:, i], bm(rank_bank(i)[:, 0:NE], 2), ALU.mult)
            ins.then_inc(g("ranked"), 1)
            v.wait_ge(g("ranked"), i + 1)
            link(v.tensor_reduce(r[:, m], t2, AX.X, ALU.add))
            link(v.tensor_tensor(q9, bc(r[:, m], MAXQ), bm(C("thr", MAXQ), 2), ALU.is_ge))
            link(v.tensor_reduce(q[:, m], q9, AX.X, ALU.add))
            link(v.scalar_tensor_tensor(out=place[:, m], in0=q[:, m], scalar=-float(WB), in1=r[:, m], op0=ALU.mult,
                                        op1=ALU.add))

        def place_tile(v, link, i):
            for k in range(2):
                link(v.tensor_scalar(oh_w[2 * i + k], C("iota_w", WB), place[:, 2 * i + k:2 * i + k + 1],
                                     consts[:, CONSTS["tokid"] + i:CONSTS["tokid"] + i + 1], ALU.is_equal, ALU.mult))

        def routing(v, link):
            v.wait_ge(g("rk"), NT)
            link(v.tensor_tensor(q9e, bc(rank_bank(NT - 1)[:, NE:2 * NE], MAXQ), bm(C("thr", MAXQ), NE), ALU.is_gt))
            link(v.tensor_reduce(ovf, q9e, AX.X, ALU.add))
            link(v.tensor_tensor_scan(off_end, ones[:, 0:NE], ovf, 0.0, ALU.mult, ALU.add))
            link(v.tensor_tensor(off, off_end, ovf, ALU.subtract))
            rank_tile(v, link, NT - 1)
            link(v.tensor_tensor(t12, Ek, bm(off, 2 * NT), ALU.mult))
            link(v.tensor_reduce(ovs, t12, AX.X, ALU.add))
            link(v.tensor_scalar(sel, q, 0.5, None, ALU.is_gt))
            link(v.tensor_tensor(ovs, ovs, q, ALU.add))
            link(v.scalar_tensor_tensor(out=blk, in0=ovs, scalar=float(NE - 1 - LOW), in1=at, op0=ALU.add,
                                        op1=ALU.subtract))
            link(v.tensor_tensor(blk, blk, sel, ALU.mult))
            link(v.tensor_tensor(blk, blk, at, ALU.add))
            for k in range(2 * NT):
                if k == 2:
                    place_tile(v, link, NT - 1)
                v.tensor_scalar(oh_b[:, k, :], C("iota_b", NBC), blk[:, k:k + 1], None, ALU.is_equal).then_inc(g("onehot"), 1)
            extra = off_end[:, NE - 1:NE]
            f = lambda k: ctlf[:, k:k + 1]
            link(v.tensor_scalar(marks[:, 0:ROUNDS - 1], C("round_thr", ROUNDS - 1), extra, None, ALU.is_lt))
            link(v.tensor_reduce(f(C_FULL), marks[:, 0:ROUNDS - 1], AX.X, ALU.add))
            link(v.scalar_tensor_tensor(out=f(C_REST), in0=f(C_FULL), scalar=-float(RING), in1=extra, op0=ALU.mult,
                                        op1=ALU.add))
            link(v.tensor_scalar(f(C_REST), f(C_REST), float(NE), None, ALU.add))
            v.tensor_copy(ctl[0:1, C_FULL:C_REST + 1], ctlf[0:1, C_FULL:C_REST + 1]).then_inc(g("iters"), 1)
            v.wait_ge(g("rt_ap"), 1)
            v.tensor_copy(idx[:], psum[3][0:WB, 0:NBC]).then_inc(g("idx"), 1)
            link(v.tensor_tensor(xe, bc(C("iota_x", EXTRA), NE), bm(off_end, EXTRA), ALU.is_ge))
            link(v.tensor_reduce(ctlf[:, NE:NBC], xe, AX.X, ALU.add))
            link(v.tensor_scalar(ctlf[:, NE:NBC], ctlf[:, NE:NBC], float(NE - 1), None, ALU.min))
            link(v.tensor_scalar(ctlf[:, 0:NE], C("iota_m", NE), float(LOW), None, ALU.add))
            link(v.tensor_scalar(marks[:, 0:EXTRA // 2], C("evens", EXTRA // 2), extra, None, ALU.is_le))
            link(v.tensor_reduce(f(C_YS1), marks[:, 0:EXTRA // 2], AX.X, ALU.add))
            link(v.tensor_tensor(f(C_YS0), extra, f(C_YS1), ALU.subtract))
            link(v.tensor_scalar(ctlf[:, C_YS0:C_YS1 + 1], ctlf[:, C_YS0:C_YS1 + 1], 16.0, float(16 * (NE // 2) + 16),
                                 ALU.mult, ALU.add))
            link(v.tensor_scalar(f(C_BLOCKS), extra, float(NE), None, ALU.add))
            v.wait_ge(g("iters"), 1)
            v.tensor_copy(ctl[0:1, 0:NBC], ctlf[0:1, 0:NBC]).then_inc(g("cx"), 1)
            v.tensor_copy(ctl[0:1, C_BLOCKS:C_YS1 + 1], ctlf[0:1, C_BLOCKS:C_YS1 + 1]).then_inc(g("cx"), 1)
            v.wait_ge(g("cx"), 2)
            v.sem_inc(g("ctl"), 1)
            link(v.scalar_tensor_tensor(out=pos, in0=blk, scalar=float(WB), in1=place, op0=ALU.mult, op1=ALU.add))
            v.tensor_scalar(pos_i[:], pos, float(WB * LOW), None, ALU.add).then_inc(g("pos"), 1)
            v.tensor_tensor(g4b, logits[:, :, 0:NG], bc(gtop, NG), ALU.subtract).then_inc(g("rt_d"), 1)
            v.tensor_tensor(ediff, e1top, e0top, ALU.subtract).then_inc(g("rt_d"), 1)
            v.wait_ge(g("rt_e"), 2)
            link(v.tensor_reduce(gsum, g4b, AX.X, ALU.add))
            link(v.tensor_scalar(den, egap, 1.0, None, ALU.add))
            link(v.tensor_tensor(den, den, gsum, ALU.mult))
            link(v.reciprocal(den, den))
            link(v.tensor_scalar(gate0, den, 0.5, None, ALU.mult))
            v.tensor_tensor(gate1, gate0, egap, ALU.mult).then_inc(g("gates"), 1)
            for i in range(NT):
                v.tensor_scalar(diag[:, i, :], ident, gate0[:, i:i + 1], None, ALU.mult).then_inc(g("diag"), 1)

        @block.vector
        def _(v):
            chain = [0]

            def link(ins):
                chain[0] += 1
                ins.then_inc(g("dch"), 1)
                v.wait_ge(g("dch"), chain[0])
            v.memset(ahead, 1.0).then_inc(g("ahead"), 1)
            v.wait_ge(g("cols"), 16)
            lam = cols[:, COLS["lam"]:COLS["lam"] + 8]
            link(v.tensor_scalar(lam_t[:, 4, :], lam, -1.0, None, ALU.mult))
            link(v.tensor_tensor(lam_t[:, 0, :], lam_t[:, 4, :], lam, ALU.max))
            link(v.tensor_scalar(hb_r, cols[:, COLS["b_rg"]:COLS["b_rg"] + 8], 0.5, None, ALU.mult))
            v.tensor_scalar(hb_i, cols[:, COLS["b_ig"]:COLS["b_ig"] + 8], 0.5, None, ALU.mult).then_inc(g("lam"), 1)
            def norm_rows(i):
                v.wait_ge(g("sd"), i + 1)
                link(v.reciprocal(rstd1[:, i:i + 1], rstd1[:, i:i + 1]))
                if i >= 2:
                    v.wait_ge(g("uTp"), 2 * (i - 1))
                v.scalar_tensor_tensor(out=un[:, i % 2, :].rearrange("t (c p) -> t p c", c=DC),
                                       in0=xin[:, i % 2, :].rearrange("t (p c) -> t p c", c=DC), scalar=rstd1[:, i:i + 1],
                                       in1=norm_row[:].rearrange("t (p c) -> t p c", c=DC),
                                       op0=ALU.mult, op1=ALU.mult).then_inc(g("un"), 1)

            def input_low(i):
                for j in range(2):
                    cut = (slice(None), slice(4 * j, 4 * j + 4), slice(i * P, (i + 1) * P))
                    v.wait_ge(g("uTh"), 2 * i + j + 1)
                    v.tensor_tensor(ul[cut], psum[4 + 2 * (i % 2) + j][:, :].rearrange("p (c t) -> p c t", c=4),
                                    uh[cut].bitcast(f32), ALU.subtract).then_inc(g("uT"), 1)
            v.wait_ge(g("n1"), 16)
            norm_rows(0)
            norm_rows(1)
            input_low(0)
            input_low(1)
            norm_rows(2)
            for i in range(2, NT):
                if i + 1 < NT:
                    norm_rows(i + 1)
                input_low(i)
            v.wait_ge(g("lamA"), 1)
            v.tensor_scalar(lam_t[:, 2, :], lam_t[:, 1, :], 1.0, None, ALU.add).then_inc(g("lam"), 1)
            v.wait_ge(g("lam"), 2)
            v.wait_ge(g("lamA"), 2)
            link(v.tensor_scalar(lam_t[:, 5, :], lam_t[:, 2, :], 1.0, None, ALU.is_equal))
            link(v.tensor_tensor(lam_t[:, 3, :], lam_t[:, 3, :], lam_t[:, 5, :], ALU.add))
            link(v.tensor_tensor(lam_t[:, 3, :], lam_t[:, 3, :], lam_t[:, 1, :], ALU.mult))
            link(v.scalar_tensor_tensor(out=lam_t[:, 5, :], in0=lam_t[:, 2, :], scalar=-1.0, in1=lam_t[:, 5, :],
                                        op0=ALU.add, op1=ALU.add))
            link(v.reciprocal(lam_t[:, 5, :], lam_t[:, 5, :]))
            link(v.tensor_tensor(lam_t[:, 3, :], lam_t[:, 3, :], lam_t[:, 5, :], ALU.mult))
            link(v.scalar_tensor_tensor(out=lam_t[:, 3, :], in0=lam_t[:, 4, :], scalar=0.0, in1=lam_t[:, 3, :],
                                        op0=ALU.max, op1=ALU.add))
            link(v.tensor_scalar(lamc, lam_t[:, 3, :], -4.0, None, ALU.mult))
            link(v.tensor_scalar(nlamc, lam_t[:, 3, :], 4.0, None, ALU.mult))
            v.tensor_scalar(lam2[:], lam_t[:, 3, :], -8.0, None, ALU.mult).then_inc(g("lam"), 2)

            def conv(c):
                n = XPAD - 3
                v.wait_ge(g("ze"), LC + c + 1)
                v.wait_ge(g("pads"), 1)
                if c >= 2:
                    v.wait_ge(g("gp"), 2 * c - 2)
                wcol = lambda t: col("conv_w", t * LC + c)
                link(v.tensor_scalar(xc[:, c % 2, 0:n], xb[:, c, 0:n], wcol(0), col("conv_b", c), ALU.mult, ALU.add))
                for t in range(1, 4):
                    ins = v.scalar_tensor_tensor(out=xc[:, c % 2, 0:n], in0=xb[:, c, t:t + n], scalar=wcol(t),
                                                 in1=xc[:, c % 2, 0:n], op0=ALU.mult, op1=ALU.add)
                    if t < 3:
                        link(ins)
                ins.then_inc(g("conv"), 1)

            def unit_m(u):
                c = u // 2
                th_r, th_i, dec, dec2 = temps[u % 2]
                v.wait_ge(g("gx"), 3 * u + 3)
                v.scalar_tensor_tensor(out=dec2, in0=dec2, scalar=1.0, in1=th_r, op0=ALU.add, op1=ALU.mult).then_inc(g("gm"), 1)
                for n, (t0, tn) in enumerate(CHUNKS):
                    ins = v.scalar_tensor_tensor(out=th_i[:, t0:t0 + tn], in0=th_i[:, t0:t0 + tn], scalar=1.0,
                                                 in1=xc[:, c % 2, XOFF[n]:XOFF[n] + tn], op0=ALU.add, op1=ALU.mult)
                ins.then_inc(g("gm"), 1)

            def unit_s(u):
                c, d = u // 2, u % 2
                th_r, th_i, dec, dec2 = temps[d]
                v.wait_ge(g("gs"), u + 1)
                v.wait_ge(g("gm"), 2 * u + 2)
                link(v.tensor_tensor(th_i, th_i, dec2, ALU.mult))
                h_fwd = xb[:, c, 0:TOK]
                for n, (t0, tn) in enumerate(CHUNKS):
                    if d == 0:
                        ins = v.tensor_tensor_scan(h_fwd[:, t0:t0 + tn], dec[:, t0:t0 + tn], th_i[:, t0:t0 + tn], 0.0,
                                                   ALU.mult, ALU.add)
                    else:
                        ins = v.tensor_tensor_scan(th_r[:, t0:t0 + tn][:, ::-1], dec[:, t0:t0 + tn][:, ::-1],
                                                   th_i[:, t0:t0 + tn][:, ::-1], 0.0, ALU.mult, ALU.add)
                    if d == 1 or n == 0:
                        link(ins)
                if d == 0:
                    ins.then_inc(g("gh"), 1)
                else:
                    v.wait_ge(g("gh"), u)
                    v.tensor_tensor(h_fwd, h_fwd, th_r, ALU.add).then_inc(g("gh"), 1)

            def pair(c):
                unit_m(2 * c)
                unit_m(2 * c + 1)
                unit_s(2 * c)
                unit_s(2 * c + 1)
            conv(0)
            conv(1)
            pair(0)
            conv(2)
            pair(1)
            conv(3)
            pair(2)
            for k in range(4):
                a, n = k // 2, k % 2
                t0, tn = CHUNKS[n]
                v.wait_ge(g("statp"), k + 1)
                v.tensor_scalar(rn[:, a, t0:t0 + tn], psum[4][:, 0:tn], 1.0 / (QL, KVL)[a], EPS, ALU.mult,
                                ALU.add).then_inc(g("stc"), 1)
                if k == 1:
                    unit_m(6)
            unit_m(7)
            v.wait_ge(g("rqs"), 1)
            for a in range(2):
                link(v.reciprocal(rn[:, a, :], rn[:, a, :]))
                for c in range(QC) if a == 0 else range(QC, QC + KVC):
                    gain = col("q_norm", c) if a == 0 else col("kv_norm", c - QC)
                    v.scalar_tensor_tensor(out=zl[:, c, :], in0=zl[:, c, :], scalar=gain, in1=rn[:, a, :],
                                           op0=ALU.mult, op1=ALU.mult).then_inc(g("zn"), 1)
            unit_s(6)
            unit_s(7)
            swap = list(range(16, 32)) + list(range(0, 16))
            v.wait_ge(g("rope"), 16)
            v.wait_ge(g("wlo"), len(w_tiles))
            v.wait_ge(g("zp"), len(units))
            v.wait_ge(g("ze"), U_G)
            link(v.stream_shuffle(krs, kr[0:RP, :], swap))
            link(v.tensor_tensor(krs, krs, rope[0:RP, 1, :], ALU.mult))
            link(v.tensor_tensor(kr[0:RP, :], kr[0:RP, :], rope[0:RP, 0, :], ALU.mult))
            v.tensor_tensor(kT[64:96, 0, :], kr[0:RP, :], krs, ALU.add).then_inc(g("ropek"), 1)
            v.wait_ge(g("upe"), 4)
            for r in range(2):
                link(v.stream_shuffle(qs[:, r, :], qr[:, r, :], swap))
                link(v.tensor_tensor(qs[:, r, :], qs[:, r, :], rope[:, 1, :], ALU.mult))
                link(v.tensor_tensor(qr[:, r, :], qr[:, r, :], rope[:, 0, :], ALU.mult))
                for j in range(4):
                    v.tensor_tensor(qT[64:96, 4 * r + j, :], qr[32 * j:32 * j + 32, r, :], qs[32 * j:32 * j + 32, r, :],
                                    ALU.add).then_inc(g("ropeq"), 1)

            v.wait_ge(g("ropek"), 1)
            v.tensor_copy(kT[64:96, 1:NH, :], kT[64:96, 0:1, :].to_broadcast([RP, NH - 1, TOK])).then_inc(g("kpe"), 1)
            v.wait_ge(g("lrs"), 2)
            link(v.reciprocal(rnorm2, rnorm2))

            def maxes(n):
                kn = keys(steps[n][1])[1]
                k = n % 4
                v.wait_ge(g("sc"), n + 1)
                if n >= 4:
                    v.wait_ge(g("pr"), n - 3)
                link(v.tensor_reduce(mx[:, k:k + 1], psum[n % 3][:, 0:kn], AX.X, ALU.max))
                v.tensor_scalar(nm[:, k:k + 1], mx[:, k:k + 1], -SCALE, None, ALU.mult).then_inc(g("mxd"), 1)

            def att_out(n):
                h, i = steps[n]
                k = n % 4
                v.wait_ge(g("pr"), n + 1)
                link(v.reciprocal(rr[:, k:k + 1], rs[:, k:k + 1]))
                v.wait_ge(g("pv"), n + 1)
                v.tensor_scalar(att[:, i, h * VH:(h + 1) * VH], psum[5][:, 0:VH], rr[:, k:k + 1], None,
                                ALU.mult).then_inc(g("pve"), 1)

            def att_low(i):
                v.wait_ge(g("ath"), i + 1)
                for c in range(LC):
                    t = slice(i * P, (i + 1) * P)
                    ins = v.tensor_tensor(at_low[c][:, t], psum[6 + i % 2][:, c * P:(c + 1) * P],
                                          at_high[:, c, t].bitcast(f32), ALU.subtract)
                ins.then_inc(g("atT"), 1)

            def rows_low(j):
                v.wait_ge(g("wah"), j + 1)
                v.scalar_tensor_tensor(out=wo_low[j], in0=wout[:, j, :], scalar=col("att_norm", j),
                                       in1=wo_high[j].bitcast(f32), op0=ALU.mult, op1=ALU.subtract).then_inc(g("wod"), 1)
            maxes(0)
            maxes(1)
            for n in range(len(steps)):
                if n + 2 < len(steps):
                    maxes(n + 2)
                if n >= 1:
                    att_out(n - 1)
                if n % 8 == 5 and n // 8 < LC:
                    c = n // 8
                    v.wait_ge(g("lsq"), 2 * LC - 1)
                    v.scalar_tensor_tensor(out=gg[:, c, :], in0=gg[:, c, :], scalar=col("lru_norm", c), in1=rnorm2,
                                           op0=ALU.mult, op1=ALU.mult).then_inc(g("ln"), 1)
                if n - 4 >= len(steps) - NT:
                    att_low(n - 4 - (len(steps) - NT))
                if n - 1 in ROWS_AT:
                    rows_low(ROWS_AT[n - 1])
            att_out(len(steps) - 1)
            for i in range(NT - 4, NT):
                att_low(i)
            v.wait_ge(g("asd"), 1)
            link(v.reciprocal(rstd1, rstd1))
            v.wait_ge(g("rows"), 32)

            def logits_out(i):
                v.wait_ge(g("lgp"), i + 1)
                v.scalar_tensor_tensor(out=logits[:, i, :], in0=psum[0][:, 0:NG + NE], scalar=rstd2[:, i:i + 1], in1=brt[:],
                                       op0=ALU.mult, op1=ALU.add).then_inc(g("lg"), 1)
                v.wait_ge(g("lg"), i + 1)

            def tt_out(i):
                for j in range(2):
                    v.wait_ge(g("ttp"), 2 * i + j + 1)
                    if i >= 1:
                        v.wait_ge(g("lgp"), i)
                    v.tensor_copy(tT[:, 4 * j:4 * j + 4, :], psum[6 + j][:, :].rearrange("p (c t) -> p c t", c=4)).then_inc(g("tt"), 1)
            v.wait_ge(g("lst"), 2)
            for i in range(NT):
                v.wait_ge(g(f"xr{i % 2}"), 16 * (i // 2 + 1))
                if i >= 1:
                    tt_out(i - 1)
                for half in range(2):
                    part = x2t[:, i % 2, half * 512:(half + 1) * 512]
                    v.wait_ge(g("op"), 2 * i + half + 1)
                    link(v.tensor_tensor(part, psum[2 + 2 * half][:, :], part, ALU.add))
                    v.scalar_tensor_tensor(out=part, in0=psum[3 + 2 * half][:, :], scalar=rstd1[:, i:i + 1], in1=part,
                                           op0=ALU.mult, op1=ALU.add).then_inc(g("x2"), 1)
                    if half == 0 and i >= 2:
                        v.wait_ge(g(f"xnst{i % 2}"), 16 * (i // 2))
                        v.wait_ge(g("ttp"), 2 * (i - 1))
                    v.wait_ge(g("x2"), 2 * i + half + 1)
                    p0 = half * (P // 2)
                    v.tensor_tensor(xn[:, i % 2, :].rearrange("t (c p) -> t p c", c=DC)[:, p0:p0 + P // 2, :],
                                    part.rearrange("t (p c) -> t p c", c=DC),
                                    norm_row[:, half * 512:(half + 1) * 512].rearrange("t (p c) -> t p c", c=DC),
                                    ALU.mult).then_inc(g("x2n"), 1)
                    if half == 0 and i >= 1:
                        logits_out(i - 1)
                        route_tile(v, link, i - 1)
                v.wait_ge(g("x2s"), i + 1)
                v.reciprocal(rstd2[:, i:i + 1], rstd2[:, i:i + 1]).then_inc(g("x2r"), 1)
                v.wait_ge(g("x2r"), i + 1)
                if 1 <= i < NT - 1:
                    rank_tile(v, link, i - 1)
                    place_tile(v, link, i - 1)
            tt_out(NT - 1)
            rank_tile(v, link, NT - 2)
            place_tile(v, link, NT - 2)
            logits_out(NT - 1)
            route_tile(v, link, NT - 1)
            routing(v, link)
            v.wait_ge(g("idx"), 1)
            v.wait_ge(g("iters"), 1)

            def rows_out(par, b, first=False):
                v.wait_ge(g("xgp"), 2 if first else b + 2)
                for j in range(2):
                    v.tensor_copy(xT[:, par, 4 * j:4 * j + 4, :],
                                  psum[2 + j][:, 0:4 * WB].rearrange("p (c n) -> p c n", c=4)).then_inc(g("xT"), 1)
            v.sem_inc(g("hh"), FC)
            rows_out(0, 0, True)

            def block_silu(i, s):
                b = i * RING + s
                for f in range(FC):
                    v.wait_ge(g("tnh"), b * FC + f + 1)
                    v.scalar_tensor_tensor(out=act_s[:, f, :], in0=act_t[:, f, :], scalar=1.0, in1=psum[f][:, 0:WB],
                                           op0=ALU.add, op1=ALU.mult).then_inc(g("acs"), 1)
                    v.wait_ge(g("acs"), b * FC + f + 1)
                    v.wait_ge(g("dn"), b + RING + 1)
                    v.tensor_tensor(hT[:, f, :], act_s[:, f, :], psum[f][:, WB:2 * WB], ALU.mult).then_inc(g("hh"), 1)
                rows_out((s + 1) % 2, b + 1)
            each_block(v, rounds(v), block_silu)
            v.wait_ge(g("frow"), 16)
            v.wait_ge(g("gates"), 1)
            v.wait_ge(g("fx0"), 16 * NT)
            v.wait_ge(g("gates"), 1)

            def add_rows(i):
                v.wait_ge(s_fy[2 * i + 1], 16)
                v.wait_ge(g("fp"), i + 1)
                for half in range(2):
                    cut = slice(half * 512, (half + 1) * 512)
                    v.scalar_tensor_tensor(out=fin_x[i][:, cut], in0=fin_y[:, 1, i, cut], scalar=gate1[:, i:i + 1],
                                           in1=psum[2 * (i % FIN_BANKS) + half][:, :], op0=ALU.mult,
                                           op1=ALU.add).then_inc(g("fs"), 1)
            add_rows(0)
            for i in range(NT):
                if i + 1 < NT:
                    add_rows(i + 1)
                v.wait_ge(g("fq"), i + 1)
                link(v.reciprocal(rstd3[:, i:i + 1], rstd3[:, i:i + 1]))
                v.scalar_tensor_tensor(out=fin_x[i], in0=fin_x[i], scalar=rstd3[:, i:i + 1], in1=fin_row,
                                       op0=ALU.mult, op1=ALU.mult).then_inc(g("fo"), 1)


def kernel(**inputs):
    import numpy as np
    import concourse.bacc as bacc
    from concourse.bass_utils import run_bass_kernel_spmd as run

    a = {k: np.asarray(v) for k, v in inputs.items()}

    def feat(v, inner):
        return v.reshape(P, -1) if inner else v.reshape(-1, P).T
    cols = np.concatenate([feat(a["norm1"][0], True), feat(a["q_norm"][0], False), feat(a["kv_norm"][0], False)] +
                          [feat(a["conv_w"][0].reshape(-1), False), feat(a["conv_b"][0], False),
                           feat(a["b_rg"][0].reshape(-1), False), feat(a["b_ig"][0].reshape(-1), False),
                           feat(a["lru_lambda"][0].reshape(-1), False), feat(a["att_out_norm"][0], False),
                           feat(a["lru_out_norm"][0], False)], axis=1)
    c = np.zeros((P, NCONSTS), np.float32)

    def put(name, v):
        v = np.asarray(v, np.float32)
        c[:, CONSTS[name]:CONSTS[name] + v.shape[-1]] = v
    put("ident", np.eye(P))
    put("before", np.triu(np.ones((P, P)), 1))
    put("ones", np.ones((P, P)))
    put("iota_w", np.arange(WB)[None])
    put("iota_b", np.arange(NBC)[None] - LOW)
    put("iota_m", np.arange(NE)[None] - LOW)
    put("thr", WB * (1 + np.arange(MAXQ))[None])
    put("tokid", np.arange(TOK).reshape(NT, P).T)
    put("eps", np.full((1, 1), EPS))
    put("iota_x", np.arange(EXTRA)[None])
    put("round_thr", RING * np.arange(1, ROUNDS)[None] - NE)
    put("evens", 2 * np.arange(1, EXTRA // 2 + 1)[None])
    inv = 1.0 / (np.float32(10000.0) ** (np.arange(0, RP, 2, dtype=np.float32) / np.float32(RP)))
    at = np.concatenate([np.arange(n, dtype=np.float32) for _, n in CHUNKS])
    ang = (at[None, :] * inv[:, None].astype(np.float32)).astype(np.float32)
    cos, sin = np.cos(ang), np.sin(ang)
    rope = np.concatenate([np.tile(np.concatenate([cos, cos]), (4, 1)), np.tile(np.concatenate([-sin, sin]), (4, 1))], axis=1)
    rows = np.zeros((4, D), np.float32)
    rows[3] = a["norm1"][0]
    rows[0] = a["norm2"][0]
    rows[1] = a["final_norm"]
    rows[2, :NG] = a["b_group"][0]
    rows[2, NG:NG + NE] = a["b_router"][0]
    wq = a["w_q_up"][0].reshape(QL, NH, NOPE + RP)
    wkv = a["w_kv_up"][0].reshape(KVL, NH, NOPE + VH)
    ins = {
        "x": np.concatenate([a["x_prompt"].reshape(-1, D), a["x_sample"].reshape(-1, D)]),
        "cols": cols, "consts": c, "rope_t": rope, "rows": rows, "w_in": a["w_in"][0],
        "w_q": np.concatenate([wq[..., :NOPE].reshape(QL, -1), wq[..., NOPE:].reshape(QL, -1)], axis=1),
        "w_kv": np.concatenate([wkv[..., :NOPE].reshape(KVL, -1), wkv[..., NOPE:].reshape(KVL, -1)], axis=1),
        "w_rg": a["w_rg"][0], "w_ig": a["w_ig"][0], "w_out": a["w_out"][0],
        "w_router": np.concatenate([a["w_group"][0], a["w_router"][0]], axis=1),
        "w_gate": a["w_gate"][0], "w_up": a["w_up"][0], "w_down": a["w_down"][0],
    }
    nc = bacc.Bacc("TRN2", target_bir_lowering=False, num_devices=1)
    arrays, args = {}, []
    for name, v in ins.items():
        v = np.ascontiguousarray(v)
        arrays[f"in_{name}"] = v
        args.append(nc.dram_tensor(f"in_{name}", v.shape, mybir.dt.from_np(v.dtype), kind="ExternalInput").ap())
    for i, n in enumerate((PROMPT, TOK - PROMPT)):
        args.append(nc.dram_tensor(f"out_{i}", (1, n, D), mybir.dt.float32, kind="ExternalOutput").ap())
    encoder_layer(nc, *args)
    r = run(nc, [arrays], core_ids=[0])
    return tuple(r.results[0][f"out_{i}"] for i in range(2))
```
